# Optimizing a Trainium2 kernel written in Bass

```python
import jax, jax.numpy as jnp
from jax import lax
import numpy as np

D_MODEL = 1024
BATCH = 1
SEQ = 2048
DEPTH = 1

CHUNK = 64
SB_BLOCK = 128
PLE_DIM = 256
MIX_WIDTH = D_MODEL
SB_WIDTH = MIX_WIDTH // 2
ML_WIDTH = MIX_WIDTH - SB_WIDTH
SB_HEADS = 8
SB_HEAD_DIM = SB_WIDTH // SB_HEADS
ML_HEADS = 4
ML_HEAD_DIM = ML_WIDTH // ML_HEADS
CONV_K = 4
EPS = 1e-6
SPLIT_SIZES = (SB_WIDTH, SB_WIDTH, SB_WIDTH, SB_WIDTH, ML_WIDTH, ML_WIDTH, ML_WIDTH, ML_WIDTH, ML_WIDTH, ML_HEADS, ML_HEADS)
N_IN = 4 * SB_WIDTH + 5 * ML_WIDTH + 2 * ML_HEADS

kernel_name = 'hybrid_stickbreaking_mlstm_block'

def _rmsnorm(x, w):
    xf = x.astype(jnp.float32)
    y = xf * lax.rsqrt(jnp.mean(xf * xf, axis=-1, keepdims=True) + EPS)
    return (y * w.astype(jnp.float32)).astype(x.dtype)

def _head_rmsnorm(y, w, n_heads):
    b, s, width = y.shape
    yf = y.astype(jnp.float32).reshape(b, s, n_heads, width // n_heads)
    yf = yf * lax.rsqrt(jnp.mean(yf * yf, axis=-1, keepdims=True) + EPS)
    return (yf.reshape(b, s, width) * w.astype(jnp.float32)).astype(y.dtype)

def _split_cols(u):
    bounds = []
    acc = 0
    for size in SPLIT_SIZES[:-1]:
        acc += size
        bounds.append(acc)
    return jnp.split(u, bounds, axis=-1)

def _split_heads(u, n_heads):
    b, s, width = u.shape
    return u.reshape(b, s, n_heads, width // n_heads).transpose(0, 2, 1, 3)

def _merge_heads(u):
    b, h, s, d = u.shape
    return u.transpose(0, 2, 1, 3).reshape(b, s, h * d)

def _causal_conv(u, w, bias):
    s = u.shape[1]
    k = w.shape[0]
    up = jnp.pad(u, ((0, 0), (k - 1, 0), (0, 0)))
    out = bias
    for j in range(k):
        out = out + w[j] * up[:, j:j + s]
    return out

def _stick_breaking_attention(q, k, v):
    s = q.shape[2]
    d = q.shape[3]
    scale = d ** -0.5
    outs = []
    for blk in range(s // SB_BLOCK):
        q0 = blk * SB_BLOCK
        k_end = q0 + SB_BLOCK
        qb = q[:, :, q0:k_end]
        kb = k[:, :, :k_end]
        vb = v[:, :, :k_end]
        z = jnp.einsum('bhqd,bhkd->bhqk', qb, kb).astype(jnp.float32) * scale
        t_pos = q0 + jnp.arange(SB_BLOCK)[:, None]
        s_pos = jnp.arange(k_end)[None, :]
        strict = s_pos < t_pos
        log_beta = jax.nn.log_sigmoid(z)
        log_keep = jnp.where(strict, log_beta - z, 0.0)
        after = lax.cumsum(log_keep, axis=3, reverse=True) - log_keep
        a = jnp.where(strict, jnp.exp(log_beta + after), 0.0)
        outs.append(jnp.einsum('bhqk,bhkd->bhqd', a, vb.astype(jnp.float32)))
    return jnp.concatenate(outs, axis=2).astype(q.dtype)

def _mlstm_chunkwise(q, k, v, i_pre, f_pre):
    out_dtype = q.dtype
    f32 = jnp.float32
    bsz, nh, s, d = q.shape
    nc = s // CHUNK

    def chunks(t):
        return t.astype(f32).reshape(bsz, nh, nc, CHUNK, d)

    q = chunks(q)
    k = chunks(k) * (d ** -0.5)
    v = chunks(v)
    ig = i_pre.astype(f32).transpose(0, 2, 1).reshape(bsz, nh, nc, CHUNK)
    lf = jax.nn.log_sigmoid(f_pre.astype(f32)).transpose(0, 2, 1).reshape(bsz, nh, nc, CHUNK)
    b = jnp.cumsum(lf, axis=-1)
    b_last = b[..., -1]

    g = b_last[..., None] - b + ig
    m_loc = jnp.max(g, axis=-1)
    w_loc = jnp.exp(g - m_loc[..., None])
    c_loc = jnp.einsum('bhcs,bhcsv,bhcsd->bhcvd', w_loc, v, k)
    n_loc = jnp.einsum('bhcs,bhcsd->bhcd', w_loc, k)

    def step(carry, xs):
        c_st, n_st, m_st = carry
        bl, ml, cl, nl = xs
        m_new = jnp.maximum(bl + m_st, ml)
        a = jnp.exp(bl + m_st - m_new)
        gg = jnp.exp(ml - m_new)
        c_new = a[..., None, None] * c_st + gg[..., None, None] * cl
        n_new = a[..., None] * n_st + gg[..., None] * nl
        return (c_new, n_new, m_new), (c_st, n_st, m_st)

    init = (jnp.zeros((bsz, nh, d, d), f32), jnp.zeros((bsz, nh, d), f32), jnp.zeros((bsz, nh), f32))
    xs = (jnp.moveaxis(b_last, 2, 0), jnp.moveaxis(m_loc, 2, 0), jnp.moveaxis(c_loc, 2, 0), jnp.moveaxis(n_loc, 2, 0))
    _, (c_prev, n_prev, m_prev) = lax.scan(step, init, xs)
    c_prev = jnp.moveaxis(c_prev, 0, 2)
    n_prev = jnp.moveaxis(n_prev, 0, 2)
    m_prev = jnp.moveaxis(m_prev, 0, 2)

    causal = jnp.tril(jnp.ones((CHUNK, CHUNK), dtype=bool))
    d_log = jnp.where(causal, b[..., :, None] - b[..., None, :] + ig[..., None, :], -jnp.inf)
    m_t = jnp.maximum(b + m_prev[..., None], jnp.max(d_log, axis=-1))
    w_intra = jnp.exp(d_log - m_t[..., None])
    scores = jnp.einsum('bhcld,bhcsd->bhcls', q, k) * w_intra
    carry_scale = jnp.exp(b + m_prev[..., None] - m_t)
    num = jnp.einsum('bhcls,bhcsv->bhclv', scores, v) + carry_scale[..., None] * jnp.einsum('bhcld,bhcvd->bhclv', q, c_prev)
    den = jnp.sum(scores, axis=-1) + carry_scale * jnp.einsum('bhcld,bhcd->bhcl', q, n_prev)
    h = num / jnp.maximum(jnp.abs(den), jnp.exp(-m_t))[..., None]
    return h.reshape(bsz, nh, s, d).astype(out_dtype)

def setup_inputs(seed: int = 0) -> dict:
    key = jax.random.key(seed)
    ks = jax.random.split(key, 15)
    nrm = jax.random.normal
    f32 = jnp.float32
    return {
        'x': nrm(ks[0], (BATCH, SEQ, D_MODEL), f32),
        'p': nrm(ks[1], (DEPTH, BATCH, SEQ, PLE_DIM), f32),
        'pre_norm_w': 1.0 + 0.05 * nrm(ks[2], (DEPTH, D_MODEL), f32),
        'w_in': nrm(ks[3], (DEPTH, D_MODEL, N_IN), f32) * D_MODEL ** -0.5,
        'ml_conv_w': nrm(ks[4], (DEPTH, CONV_K, 2 * ML_WIDTH), f32) * CONV_K ** -0.5,
        'ml_conv_b': 0.02 * nrm(ks[5], (DEPTH, 2 * ML_WIDTH), f32),
        'ml_i_bias': 0.1 * nrm(ks[6], (DEPTH, ML_HEADS), f32),
        'ml_f_bias': jnp.linspace(3.0, 6.0, ML_HEADS, dtype=f32)[None, :] + 0.01 * nrm(ks[7], (DEPTH, ML_HEADS), f32),
        'sb_norm_w': 1.0 + 0.05 * nrm(ks[8], (DEPTH, SB_WIDTH), f32),
        'ml_norm_w': 1.0 + 0.05 * nrm(ks[9], (DEPTH, ML_WIDTH), f32),
        'w_out': nrm(ks[10], (DEPTH, MIX_WIDTH, D_MODEL), f32) * MIX_WIDTH ** -0.5,
        'post_norm_w': 1.0 + 0.05 * nrm(ks[11], (DEPTH, D_MODEL), f32),
        'ple_w_up': nrm(ks[12], (DEPTH, PLE_DIM, D_MODEL), f32) * PLE_DIM ** -0.5,
        'ple_w_gate': nrm(ks[13], (DEPTH, D_MODEL, D_MODEL), f32) * D_MODEL ** -0.5,
        'ple_b_gate': 0.02 * nrm(ks[14], (DEPTH, D_MODEL), f32),
    }

def reference(x, p, pre_norm_w, w_in, ml_conv_w, ml_conv_b, ml_i_bias, ml_f_bias, sb_norm_w, ml_norm_w, w_out, post_norm_w, ple_w_up, ple_w_gate, ple_b_gate):
    h = x
    for i in range(DEPTH):
        u = _rmsnorm(h, pre_norm_w[i])
        proj = u @ w_in[i]
        sb_q, sb_k, sb_v, sb_z, ml_q, ml_k, ml_v, ml_o, ml_z, ml_i, ml_f = _split_cols(proj)

        y_sb = _stick_breaking_attention(_split_heads(sb_q, SB_HEADS), _split_heads(sb_k, SB_HEADS), _split_heads(sb_v, SB_HEADS))
        y_sb = _head_rmsnorm(_merge_heads(y_sb), sb_norm_w[i], SB_HEADS) * jax.nn.silu(sb_z)

        qk = jax.nn.silu(_causal_conv(jnp.concatenate([ml_q, ml_k], axis=-1), ml_conv_w[i], ml_conv_b[i]))
        ml_q, ml_k = jnp.split(qk, 2, axis=-1)
        y_ml = _mlstm_chunkwise(_split_heads(ml_q, ML_HEADS), _split_heads(ml_k, ML_HEADS), _split_heads(ml_v, ML_HEADS), ml_i + ml_i_bias[i], ml_f + ml_f_bias[i])
        y_ml = jax.nn.sigmoid(ml_o) * _merge_heads(y_ml)
        y_ml = _head_rmsnorm(y_ml, ml_norm_w[i], ML_HEADS) * jax.nn.silu(ml_z)

        y = jnp.concatenate([y_sb, y_ml], axis=-1) @ w_out[i]
        h = h + _rmsnorm(y, post_norm_w[i])

        gate = jax.nn.sigmoid(h @ ple_w_gate[i] + ple_b_gate[i])
        h = h + gate * (p[i] @ ple_w_up[i])
    return h


_drawn_inputs = setup_inputs


def setup_inputs(seed=0):
    import zlib

    import numpy as np

    out = dict(_drawn_inputs(seed))
    spreads = {}
    factors = {'ml_conv_b': 5.754, 'ml_i_bias': 64.0, 'ple_b_gate': 22.889}
    for name, (base, spread) in spreads.items():
        noise = np.random.default_rng([zlib.crc32(name.encode()), seed]).standard_normal(out[name].shape)
        drawn = base * np.exp(spread * noise) if base else spread * noise
        out[name] = __import__('jax').numpy.asarray(drawn.astype(out[name].dtype))
    for name, factor in factors.items():
        out[name] = (out[name] * factor).astype(out[name].dtype)
    return out
```

```python
from contextlib import ExitStack

import concourse.bass as bass
import concourse.mybir as mybir

P = 128
F32 = mybir.dt.float32
F32R = mybir.dt.float32r
BF16 = mybir.dt.bfloat16
ALU = mybir.AluOpType
ACT = mybir.ActivationFunctionType
AX = mybir.AxisListType

SEQ, D_MODEL, PLE = 2048, 1024, 256
SB_WIDTH, ML_WIDTH = 512, 512
SB_HEADS, SB_DIM = 8, 64
ML_HEADS, ML_DIM = 4, 128
CONV_K = 4
EPS = 1e-6
SB_SCALE = SB_DIM ** -0.5
ML_SCALE = ML_DIM ** -0.5

TOK = SEQ // P
KT = D_MODEL // P
GROUP = 512
TG = SEQ // GROUP
BANKS = 4
GATES = 2 * ML_HEADS
GATE_COL = 4 * SB_WIDTH + 5 * ML_WIDTH
GROUPS = GATE_COL // GROUP
MASKED = -1e30
LN_MAX = 40.0


def input_projection(nc, x, pre_norm_w, w_in, conv_w, conv_b, sb_norm_w, ml_norm_w, qk_hi, qk_lo, ml_t, proj_n,
                     gates_t):
    with ExitStack() as ctx:
        def sb(name, shape, dt=F32):
            return ctx.enter_context(nc.sbuf_tensor(name, shape, dt))

        def sem(name):
            return ctx.enter_context(nc.semaphore(name))

        ident = sb("a_ident", [P, P])
        cw = sb("conv_w", [P, 2 * TG, CONV_K])
        cb = sb("conv_b", [P, 2 * TG])
        pre_w = sb("pre_w", [P, D_MODEL])
        minus_half = sb("a_minus_half", [P, 1])
        eps = sb("a_eps", [P, 1])
        x_in = [sb(f"x_in{i}", [P, D_MODEL]) for i in range(2)]
        xn = [sb(f"xn{i}", [P, D_MODEL]) for i in range(2)]
        mean_sq = sb("a_mean_sq", [P, 2])
        mean_eps = sb("a_mean_eps", [P, 2])
        rstd = sb("a_rstd", [P, 2])
        uT_hi = sb("uT_hi", [P, KT, SEQ], F32R)
        uT_lo = sb("uT_lo", [P, KT, SEQ], F32R)
        w_raw = sb("w_raw", [P, KT, GROUP])
        w_hi = sb("w_hi", [P, KT, GROUP], F32R)
        w_lo = sb("w_lo", [P, KT, GROUP], F32R)
        wg_raw = sb("wg_raw", [P, KT, GATES])
        wg_hi = sb("wg_hi", [P, KT, GATES], F32R)
        wg_lo = sb("wg_lo", [P, KT, GATES], F32R)
        stage = [x_in[i // 2][:, i % 2 * GROUP:(i % 2 + 1) * GROUP] for i in range(BANKS)]
        HALO = CONV_K - 1
        stage_hi = [sb(f"stage_hi{i}", [P, GROUP + HALO + 1], F32R) for i in range(2)]
        stage_lo = [sb(f"stage_lo{i}", [P, GROUP], F32R) for i in range(2)]
        conv_in = [t[:, 0:GROUP + HALO].bitcast(F32) for t in stage_hi]
        conv_out = [t[:].bitcast(F32) for t in stage_lo]
        gate_w = [xn[0][:, 0:SB_WIDTH], xn[0][:, SB_WIDTH:]]
        pt = [ctx.enter_context(nc.psum_tensor(f"a_pt{i}", [P, GROUP], F32)) for i in range(2)]
        po = [ctx.enter_context(nc.psum_tensor(f"a_po{i}", [P, GROUP], F32)) for i in range(BANKS)]

        consts_loaded = sem("a_consts_loaded")
        half_ready = sem("a_half_ready")
        ident_ready = sem("a_ident_ready")
        x_loaded = [sem(f"x_loaded{i}") for i in range(2)]
        x_read = sem("x_read")
        mean_sq_done = sem("a_mean_sq_done")
        mean_eps_done = sem("a_mean_eps_done")
        rstd_done = sem("a_rstd_done")
        xpose_done = sem("a_xpose_done")
        u_hi_done = sem("u_hi_done")
        u_lo_done = sem("u_lo_done")
        w_loaded = sem("w_loaded")
        wg_loaded = sem("wg_loaded")
        w_hi_done = sem("w_hi_done")
        w_lo_done = sem("w_lo_done")
        wg_hi_done = sem("wg_hi_done")
        wg_lo_done = sem("wg_lo_done")
        w_used = sem("w_used")
        out_ready = sem("out_ready")
        evacuated = [sem(f"evacuated{i}") for i in range(BANKS)]
        stored = [sem(f"stored{i}") for i in range(BANKS)]
        staged_hi = [sem(f"staged_hi{i}") for i in range(2)]
        stored_hi = [sem(f"stored_hi{i}") for i in range(2)]
        stored_lo = [sem(f"stored_lo{i}") for i in range(2)]

        conv_w_loaded = sem("conv_w_loaded")
        gate_w_loaded = sem("gate_w_loaded")
        halo_done = sem("halo_done")
        conv_in_done = sem("conv_in_done")
        tap_done = sem("tap_done")
        staged = [sem(f"staged{i}") for i in range(BANKS)]

        w_view = w_in.rearrange("(k p) n -> p k n", p=P)
        block = ctx.enter_context(nc.Block())

        @block.gpsimd
        def _(pool):
            nc.gpsimd.memset(minus_half[:], -0.5).then_inc(half_ready, 1)
            nc.gpsimd.memset(eps[:], EPS).then_inc(half_ready, 1)
            nc.gpsimd.memset(ident[:], 0.0).then_inc(half_ready, 1)
            pool.wait_ge(half_ready, 3)
            nc.gpsimd.affine_select(out=ident[:], in_=ident[:], compare_op=ALU.not_equal, fill=1.0, base=0,
                                    pattern=[[-1, P]], channel_multiplier=1).then_inc(ident_ready, 1)
            pool.dma_start(w_raw[:], w_view[:, :, 0:GROUP]).then_inc(w_loaded, 16)
            with nc.allow_non_contiguous_dma("eight gate columns"):
                pool.dma_start(wg_raw[:], w_view[:, :, GATE_COL:GATE_COL + GATES]).then_inc(wg_loaded, 16)
            with pool.Fori(0, TOK // 2) as n:
                for i in range(2):
                    m = mean_eps[:, i:i + 1]
                    pool.wait_ge(mean_sq_done, 2 * n + (i + 1))
                    pool.wait_ge(x_read, 2 * n + (i + 1))
                    nc.gpsimd.tensor_tensor(m, mean_sq[:, i:i + 1], eps[:], ALU.add).then_inc(mean_eps_done, 1)
                    pool.wait_ge(mean_eps_done, 2 * n + (i + 1))
                    nc.gpsimd.tensor_tensor(rstd[:, i:i + 1], m, minus_half[:], ALU.pow).then_inc(rstd_done, 1)
            with pool.Fori(1, GROUPS) as g:
                pool.wait_ge(w_lo_done, g * KT)
                pool.dma_start(w_raw[:], w_view[:, :, bass.ds(g * GROUP, GROUP)]).then_inc(w_loaded, 16)

        @block.sync
        def _(sp):
            sp.dma_start(pre_w[:], pre_norm_w.broadcast_to([P, D_MODEL])).then_inc(consts_loaded, 16)
            with sp.Fori(0, TOK // 2) as n:
                for i in range(2):
                    sp.wait_ge(x_read, 2 * n + (i + 1))
                    sp.dma_start(x_in[i][:], x[bass.ds((2 * n + i) * P, P), :]).then_inc(x_loaded[i], 16)

            sp.wait_ge(u_lo_done, 2 * TOK + 4)
            sp.dma_start(gate_w[0], sb_norm_w.broadcast_to([P, SB_WIDTH])).then_inc(gate_w_loaded, 16)
            sp.dma_start(gate_w[1], ml_norm_w.broadcast_to([P, ML_WIDTH])).then_inc(gate_w_loaded, 16)
            with nc.allow_non_contiguous_dma("the convolution's few weights"):
                for j in range(CONV_K):
                    sp.dma_start(cw[:, :, j], conv_w[j, :].rearrange("(c p) -> p c", p=P)).then_inc(conv_w_loaded, 16)
                sp.dma_start(cb[:], conv_b.rearrange("a (c p) -> p (a c)", p=P)).then_inc(conv_w_loaded, 16)

            for g in range(2):
                with sp.Fori(0, TG) as m:
                    for t in range(TG):
                        i = t % 2
                        rows, cols = bass.ds((g * TG + m) * P, P), bass.ds(t * GROUP, GROUP)
                        n = 2 * TG * g + 2 * m + (t // 2 + 1)
                        sp.wait_ge(staged_hi[i], n)
                        sp.dma_start(qk_hi[rows, cols], stage_hi[i][:, 0:GROUP].bitcast(F32))\
                            .then_inc(stored_hi[i], 16)
                        sp.wait_ge(evacuated[t], TG * g + m + 2)
                        sp.dma_start(qk_lo[rows, cols], stage_lo[i][:].bitcast(F32)).then_inc(stored_lo[i], 16)

            def store(ready, g, dram, row, row_step, col):
                with sp.Fori(0, TG) as m:
                    for t in range(BANKS):
                        sp.wait_ge(ready[t], g * TG + m + 2)
                        rows = bass.ds((row + m * row_step + (0 if dram is ml_t else t)) * P, P)
                        cols = slice(t * GROUP, (t + 1) * GROUP) if dram is ml_t else slice(col, col + GROUP)
                        sp.dma_start(dram[rows, cols], stage[t]).then_inc(stored[t], 16)

            store(evacuated, 2, proj_n, 0, BANKS, 0)
            store(staged, 0, proj_n, 0, BANKS, GROUP)
            for c in range(2):
                store(staged, 1 + c, ml_t, c * TG, 1, 0)
            store(evacuated, 6, proj_n, 0, BANKS, 2 * GROUP)
            store(evacuated, 7, proj_n, 0, BANKS, 3 * GROUP)
            store(staged, 3, proj_n, 0, BANKS, 4 * GROUP)
            for t in range(TG):
                sp.wait_ge(evacuated[t], GROUPS * TG + 2)
                sp.dma_start(gates_t[:, t * GROUP:(t + 1) * GROUP], stage[t][0:GATES, :]).then_inc(stored[t], 16)
            for t in range(BANKS):
                sp.wait_ge(stored[t], 16 * ((GROUPS - 2) * TG + 2))
            for i in range(2):
                sp.wait_ge(stored_hi[i], 16 * (4 * TG + 1))
                sp.wait_ge(stored_lo[i], 16 * (4 * TG + 1))

        @block.scalar
        def _(act):
            with act.Fori(0, TOK // 2) as n:
                for i in range(2):
                    act.wait_ge(x_loaded[i], 16 * (n + 1))
                    act.wait_ge(u_lo_done, 4 * n + 2 * (i + 1))
                    nc.scalar.activation(xn[i][:], x_in[i][:], ACT.Square, scale=D_MODEL ** -0.5,
                                         accum_out=mean_sq[:, i:i + 1])\
                        .then_inc(mean_sq_done, 1)
                for i in range(2):
                    for h in range(2):
                        act.wait_ge(xpose_done, 4 * n + (2 * i + h + 1))
                        nc.scalar.copy(uT_hi[:, 4 * h:4 * h + 4, bass.ds((2 * n + i) * P, P)],
                                       pt[h][:].rearrange("p (k t) -> p k t", k=4)).then_inc(u_hi_done, 1)

            def split(g):
                act.wait_ge(w_loaded, 16 * g + 16)
                for k in range(KT):
                    if k < KT - 1:
                        act.wait_ge(w_used, (KT - 1) * g + (k + 1))
                    else:
                        act.wait_ge(out_ready, 16 * g + 1)
                    nc.scalar.copy(w_hi[:, k, :], w_raw[:, k, :]).then_inc(w_hi_done, 1)

            def evacuate_hi(g, scale):
                with act.Fori(0, TG) as m:
                    for t in range(TG):
                        act.wait_ge(out_ready, 16 * g + 4 * m + (t + 2))
                        act.wait_ge(stored_hi[t % 2], 16 * (2 * TG * g + 2 * m + (t // 2 + 1)))
                        act.wait_ge(evacuated[(t + 2) % BANKS], TG * g + m + (1 if t < 2 else 2))
                        nc.scalar.mul(stage_hi[t % 2][:, 0:GROUP], po[t][:], scale).then_inc(staged_hi[t % 2], 1)

            def evacuate_copy(g):
                with act.Fori(0, TG) as m:
                    for t in (1, 3):
                        act.wait_ge(out_ready, 16 * g + 4 * m + (t + 2))
                        act.wait_ge(stored[t], 16 * ((g - 2) * TG + m + 1))
                        nc.scalar.copy(stage[t], po[t][:]).then_inc(evacuated[t], 1)

            def evacuate_gate(g, func):
                with act.Fori(0, TG) as m:
                    for t in range(BANKS):
                        act.wait_ge(out_ready, 16 * g + 4 * m + (t + 2))
                        act.wait_ge(stored[t], 16 * ((g - 2) * TG + m + 1))
                        nc.scalar.activation(stage[t], po[t][:], func).then_inc(evacuated[t], 1)

            def evacuate_conv(g):
                with act.Fori(0, TG) as m:
                    n = TG * TG * (g - 4) + TG * m
                    for t in range(BANKS + 1):
                        if t < BANKS:
                            act.wait_ge(out_ready, 16 * g + 4 * m + (t + 2))
                            act.wait_ge(halo_done, n + (t + 1))
                            nc.scalar.copy(conv_in[t % 2][:, HALO:], po[t][:]).then_inc(evacuated[t], 1)
                        if t > 0:
                            act.wait_ge(tap_done, CONV_K * n + CONV_K * (t + 2))
                            act.wait_ge(stored[t - 1], 16 * ((g - 2) * TG + m + 1))
                            nc.scalar.activation(stage[t - 1], conv_out[(t - 1) % 2], ACT.Silu)\
                                .then_inc(staged[t - 1], 1)

            act.wait_ge(wg_loaded, 16)
            nc.scalar.copy(wg_hi[:], wg_raw[:]).then_inc(wg_hi_done, 1)
            for g, scale in enumerate((SB_SCALE, 1.0)):
                split(g)
                evacuate_hi(g, scale)
            split(2)
            evacuate_copy(2)
            split(3)
            evacuate_gate(3, ACT.Silu)
            for g in (4, 5):
                split(g)
                evacuate_conv(g)
            split(6)
            evacuate_copy(6)
            split(7)
            evacuate_gate(7, ACT.Sigmoid)
            split(8)
            evacuate_gate(8, ACT.Silu)
            for t in (1, 3):
                act.wait_ge(out_ready, 16 * GROUPS + (t + 2))
                act.wait_ge(stored[t], 16 * ((GROUPS - 2) * TG + 1))
                nc.scalar.copy(stage[t][0:GATES, :], po[t][0:GATES, :]).then_inc(evacuated[t], 1)

        @block.vector
        def _(dve):
            for s, count in ([(x_read, 1), (x_read, 1), (u_lo_done, 4), (w_used, KT - 1), (out_ready, 1),
                              (tap_done, 2 * CONV_K)] +
                             [(s, 1) for s in evacuated + staged] +
                             [(s, 16) for s in stored + stored_hi + stored_lo]):
                dve.sem_inc(s, count)
            dve.wait_ge(consts_loaded, 16)
            with dve.Fori(0, TOK // 2) as n:
                for i in range(2):
                    dve.wait_ge(rstd_done, 2 * n + (i + 1))
                    nc.vector.scalar_tensor_tensor(out=xn[i][:], in0=x_in[i][:], scalar=rstd[:, i:i + 1],
                                                   in1=pre_w[:], op0=ALU.mult, op1=ALU.mult).then_inc(x_read, 1)
                for i in range(2):
                    for h in range(2):
                        dve.wait_ge(u_hi_done, 4 * n + (2 * i + h + 1))
                        hi = uT_hi[:, 4 * h:4 * h + 4, bass.ds((2 * n + i) * P, P)].bitcast(F32)
                        nc.vector.tensor_tensor(uT_lo[:, 4 * h:4 * h + 4, bass.ds((2 * n + i) * P, P)],
                                                pt[h][:].rearrange("p (k t) -> p k t", k=4), hi,
                                                ALU.subtract).then_inc(u_lo_done, 1)

            def split(g):
                for k in range(KT):
                    dve.wait_ge(w_hi_done, KT * g + (k + 1))
                    nc.vector.tensor_tensor(w_lo[:, k, :], w_raw[:, k, :], w_hi[:, k, :].bitcast(F32),
                                            ALU.subtract).then_inc(w_lo_done, 1)

            def evacuate_lo(g, scale):
                with dve.Fori(0, TG) as m:
                    for t in range(TG):
                        n = 2 * TG * g + 2 * m + (t // 2 + 1)
                        dve.wait_ge(staged_hi[t % 2], n)
                        dve.wait_ge(stored_lo[t % 2], 16 * n)
                        nc.vector.scalar_tensor_tensor(out=stage_lo[t % 2][:], in0=po[t][:], scalar=scale,
                                                       in1=stage_hi[t % 2][:, 0:GROUP].bitcast(F32), op0=ALU.mult,
                                                       op1=ALU.subtract).then_inc(evacuated[t], 1)

            def evacuate_copy(g):
                with dve.Fori(0, TG) as m:
                    for t in (0, 2):
                        dve.wait_ge(out_ready, 16 * g + 4 * m + (t + 2))
                        dve.wait_ge(stored[t], 16 * ((g - 2) * TG + m + 1))
                        nc.vector.tensor_copy(stage[t], po[t][:]).then_inc(evacuated[t], 1)

            def weigh_gate(g, w):
                with dve.Fori(0, TG) as m:
                    for t in range(BANKS):
                        dve.wait_ge(evacuated[t], TG * g + m + 2)
                        nc.vector.tensor_tensor(stage[t], stage[t], w, ALU.mult).then_inc(staged[t], 1)

            def convolve(g):
                with dve.Fori(0, TG) as m:
                    n = TG * TG * (g - 4) + TG * m
                    c = (g - 4) * TG + m
                    w = [cw[:, bass.ds(c, 1), j] for j in range(CONV_K)]
                    for t in range(BANKS):
                        x_in_, out = conv_in[t % 2], conv_out[t % 2]
                        if t == 0:
                            dve.wait_ge(tap_done, CONV_K * n + CONV_K)
                            nc.vector.memset(x_in_[:, 0:HALO], 0.0).then_inc(halo_done, 1)
                        dve.wait_ge(evacuated[t], TG * g + m + 2)
                        dve.wait_ge(staged[(t + 2) % BANKS], TG * (g - 3) + m + (1 if t < 2 else 2))
                        nc.vector.tensor_scalar(out, x_in_[:, 0:GROUP], w[0], cb[:, bass.ds(c, 1)], ALU.mult, ALU.add)\
                            .then_inc(tap_done, 1)
                        if t < BANKS - 1:
                            dve.wait_ge(tap_done, CONV_K * n + CONV_K * (t + 2))
                            nc.vector.tensor_copy(conv_in[(t + 1) % 2][:, 0:HALO], x_in_[:, GROUP:])\
                                .then_inc(halo_done, 1)
                        for j in range(1, CONV_K):
                            dve.wait_ge(tap_done, CONV_K * n + (CONV_K * (t + 2) + j))
                            nc.vector.scalar_tensor_tensor(out=out, in0=x_in_[:, j:j + GROUP], scalar=w[j], in1=out,
                                                           op0=ALU.mult, op1=ALU.add).then_inc(tap_done, 1)

            dve.wait_ge(wg_hi_done, 1)
            nc.vector.tensor_tensor(wg_lo[:], wg_raw[:], wg_hi[:].bitcast(F32), ALU.subtract).then_inc(wg_lo_done, 1)
            for g, scale in enumerate((SB_SCALE, 1.0)):
                split(g)
                evacuate_lo(g, scale)
            split(2)
            evacuate_copy(2)
            split(3)
            dve.wait_ge(gate_w_loaded, 32)
            weigh_gate(3, gate_w[0])
            dve.wait_ge(conv_w_loaded, 16 * (CONV_K + 1))
            for i in range(2):
                dve.wait_ge(stored_hi[i], 16 * (4 * TG + 1))
                dve.wait_ge(stored_lo[i], 16 * (4 * TG + 1))
            for g in (4, 5):
                split(g)
                convolve(g)
            split(6)
            evacuate_copy(6)
            split(7)
            split(8)
            weigh_gate(8, gate_w[1])
            for t in (0, 2):
                dve.wait_ge(out_ready, 16 * GROUPS + (t + 2))
                dve.wait_ge(stored[t], 16 * ((GROUPS - 2) * TG + 1))
                nc.vector.tensor_copy(stage[t][0:GATES, :], po[t][0:GATES, :]).then_inc(evacuated[t], 1)

        @block.tensor
        def _(pe):
            pe.wait_ge(ident_ready, 1)
            with pe.Fori(0, TOK // 2) as n:
                for i in range(2):
                    pe.wait_ge(x_read, 2 * n + (i + 3))
                    for h in range(2):
                        pe.wait_ge(u_lo_done, 4 * n + (2 * i + h + 3))
                        for k in range(4):
                            mm = pe.transpose(pt[h][:, k * P:(k + 1) * P],
                                              xn[i][:, (4 * h + k) * P:(4 * h + k + 1) * P], ident[:])
                        mm.then_inc(xpose_done, 1)
            pe.wait_ge(u_lo_done, 2 * TOK + 4)

            PARTS = ((1, 0), (0, 1), (0, 0))

            def group(g, transposed):
                for m in range(TG):
                    for t in range(BANKS):
                        pe.wait_ge(evacuated[t], TG * g + (m + 1))
                        first, final = (m, t) == (0, 0), (m, t) == (TG - 1, BANKS - 1)
                        for k in range(KT):
                            if first:
                                pe.wait_ge(w_lo_done, KT * g + (k + 1))
                            for n, (w_part, u_part) in enumerate(PARTS):
                                w, u = (w_hi, w_lo)[w_part], (uT_hi, uT_lo)[u_part]
                                if transposed:
                                    lhsT, rhs = w[:, k, m * P:(m + 1) * P], u[:, k, t * GROUP:(t + 1) * GROUP]
                                else:
                                    token = m * BANKS + t
                                    lhsT, rhs = u[:, k, token * P:(token + 1) * P], w[:, k, :]
                                mm = pe.matmul(po[t][:], lhsT, rhs, start=(k == 0 and n == 0),
                                               stop=(k == KT - 1 and n == 2))
                            if final and k < KT - 1:
                                mm.then_inc(w_used, 1)
                        mm.then_inc(out_ready, 1)

            with pe.Fori(0, 2) as a:
                with pe.Fori(0, 2) as b:
                    group(4 * a + b, True)
                with pe.Fori(0, 2) as b:
                    group(4 * a + b + 2, False)
            group(GROUPS - 1, False)
            pe.wait_ge(wg_lo_done, 1)
            for t in range(TG):
                pe.wait_ge(evacuated[t], TG * GROUPS + 1)
                for k in range(KT):
                    for n, (w_part, u_part) in enumerate(PARTS):
                        w, u = (wg_hi, wg_lo)[w_part], (uT_hi, uT_lo)[u_part]
                        mm = pe.matmul(po[t][0:GATES, :], w[:, k, :], u[:, k, t * GROUP:(t + 1) * GROUP],
                                       start=(k == 0 and n == 0), stop=(k == KT - 1 and n == 2))
                mm.then_inc(out_ready, 1)


def stick_breaking_attention(nc, qk_hi, qk_lo, proj_n, y_sb):
    with ExitStack() as ctx:
        def sb(name, shape, dt=F32):
            return ctx.enter_context(nc.sbuf_tensor(name, shape, dt))

        def sem(name):
            return ctx.enter_context(nc.semaphore(name))

        def psum(name, shape):
            return ctx.enter_context(nc.psum_tensor(name, shape, F32))

        PAIRS = SB_HEADS // 2
        BUFS, ZS = 8, 4
        units = []
        for head in range(2):
            for i in range(TOK):
                for c in reversed(range(i // 4 + 1)):
                    keys = min(GROUP, (i + 1) * P - c * GROUP)
                    units.append((head, i, c * GROUP, keys, c == i // 4, c == 0))
        UNITS = len(units)
        assert UNITS % BUFS == 0
        X_LAG, T_LAG, V_LAG, O_LAG = 3, 4, 5, 6

        kst = [sb(f"kst{s}", [P, SEQ], F32R) for s in range(2)]
        qst_hi = [sb(f"qst_hi{s}", [P, SEQ], F32R) for s in range(2)]
        qst_lo = [sb(f"qst_lo{s}", [P, SEQ], F32R) for s in range(2)]
        v = sb("b_v", [P, TOK, SB_WIDTH])
        buf = [sb(f"b_buf{s}", [P, GROUP]) for s in range(BUFS)]
        run = [sb(f"b_run{s}", [P, GROUP]) for s in range(2)]
        aT = [sb(f"b_aT{s}", [P, GROUP]) for s in range(2)]
        ident = sb("b_ident", [P, P])
        ident_b = sb("b_ident_b", [P, P], BF16)
        hidden = sb("b_hidden", [P, P], BF16)
        z = [psum(f"b_z{s}", [P, GROUP]) for s in range(ZS)]
        turned = [psum(f"b_turned{s}", [P, GROUP]) for s in range(2)]
        o = [psum(f"b_o{s}", [P, P]) for s in range(2)]

        zeroed = sem("b_zeroed")
        consts_ready = sem("b_consts_ready")
        qk_loaded = [sem(f"qk_loaded{s}") for s in range(2)]
        v_loaded = sem("b_v_loaded")
        z_done = sem("z_done")
        e_done = sem("e_done")
        ln_done = sem("ln_done")
        sp_done = sem("sp_done")
        run_done = sem("run_done")
        arg_done = sem("arg_done")
        a_done = sem("a_done")
        turned_done = sem("turned_done")
        aT_done = sem("aT_done")
        av_done = sem("av_done")
        o_read = sem("o_read")
        block = ctx.enter_context(nc.Block())

        @block.gpsimd
        def _(pool):
            for tile in (ident, ident_b, hidden):
                nc.gpsimd.memset(tile[:], 0.0).then_inc(zeroed, 1)
            pool.wait_ge(zeroed, 3)
            for tile in (ident, ident_b):
                nc.gpsimd.affine_select(out=tile[:], in_=tile[:], compare_op=ALU.not_equal, fill=1.0, base=0,
                                        pattern=[[-1, P]], channel_multiplier=1).then_inc(consts_ready, 1)
            nc.gpsimd.affine_select(out=hidden[:], in_=hidden[:], compare_op=ALU.is_gt, fill=MASKED, base=0,
                                    pattern=[[-1, P]], channel_multiplier=1).then_inc(consts_ready, 1)

        @block.sync
        def _(sp):
            def load_head(s, head):
                q, k = bass.ds(head * SB_DIM, SB_DIM), bass.ds(head * SB_DIM + SB_WIDTH, SB_DIM)
                for tile, top, bottom in ((kst, qk_hi[k, :], qk_lo[k, :]), (qst_hi, qk_hi[q, :], qk_hi[q, :]),
                                          (qst_lo, qk_lo[q, :], qk_lo[q, :])):
                    sp.dma_start(tile[s][0:64, :].bitcast(F32), top).then_inc(qk_loaded[s], 16)
                    sp.dma_start(tile[s][64:128, :].bitcast(F32), bottom).then_inc(qk_loaded[s], 16)

            load_head(0, 0)
            sp.dma_start(v[:], proj_n[:, 0:SB_WIDTH].rearrange("(j p) n -> p j n", p=P)).then_inc(v_loaded, 16)
            load_head(1, 1)
            with sp.Fori(1, PAIRS) as it:
                for s in range(2):
                    sp.wait_ge(z_done, (it - 1) * UNITS + UNITS // 2 * (s + 1))
                    load_head(s, 2 * it + s)

        @block.tensor
        def _(pe):
            pe.wait_ge(consts_ready, 3)
            with pe.Fori(0, PAIRS) as it:
                for step in range(UNITS + V_LAG):
                    if 0 <= step - T_LAG < UNITS:
                        u = step - T_LAG
                        keys = units[u][3]
                        pe.wait_ge(a_done, it * UNITS + (u + 1))
                        pe.wait_ge(aT_done, it * UNITS + (u + 1))
                        for j in range(keys // P):
                            mm = pe.transpose(turned[u % 2][:, j * P:(j + 1) * P],
                                              buf[u % BUFS][:, j * P:(j + 1) * P], ident[:])
                        mm.then_inc(turned_done, 1)
                    if step < UNITS:
                        u = step
                        head, i, key0, keys, first, last = units[u]
                        if u in (0, UNITS // 2):
                            pe.wait_ge(qk_loaded[head], 96 * it + 96)
                        pe.wait_ge(arg_done, it * UNITS + (u + 1))
                        q = slice(i * P, (i + 1) * P)
                        out, k = z[u % ZS][:, 0:keys], kst[head][:, key0:key0 + keys]
                        pe.matmul(out, qst_lo[head][:, q], k, start=True, stop=False)
                        mm = pe.matmul(out, qst_hi[head][:, q], k, start=False, stop=not first)
                        if first:
                            mm = pe.matmul(z[u % ZS][:, keys - P:keys], ident_b[:], hidden[:], start=False, stop=True)
                        mm.then_inc(z_done, 1)
                    if 0 <= step - V_LAG < UNITS:
                        u = step - V_LAG
                        head, i, key0, keys, first, last = units[u]
                        if u == 0:
                            pe.wait_ge(v_loaded, 16)
                        pe.wait_ge(aT_done, it * UNITS + (u + 3))
                        if first:
                            pe.wait_ge(o_read, it * 2 * TOK + head * TOK + i + 1)
                        for j in range(keys // P):
                            mm = pe.matmul(o[i % 2][:], aT[u % 2][:, j * P:(j + 1) * P],
                                           v[:, key0 // P + j, bass.ds(it * P, P)],
                                           start=(first and j == 0), stop=(last and j == keys // P - 1))
                        mm.then_inc(av_done, 1)

        @block.scalar
        def _(act):
            act.preload_act_table_set("natural_log_exp_and_others")
            with act.Fori(0, PAIRS) as it:
                for step in range(UNITS + V_LAG):
                    if step < UNITS:
                        keys = units[step][3]
                        b = buf[step % BUFS][:, 0:keys]
                        act.wait_ge(z_done, it * UNITS + (step + 1))
                        act.wait_ge(turned_done, it * UNITS + (step + 1))
                        nc.scalar.activation(b, z[step % ZS][:, 0:keys], ACT.Exp).then_inc(e_done, 1)
                    if 0 <= step - X_LAG < UNITS:
                        u = step - X_LAG
                        x = buf[u % BUFS][:, 0:units[u][3]]
                        act.wait_ge(arg_done, it * UNITS + (u + 1 + ZS))
                        nc.scalar.activation(x, x, ACT.Exp).then_inc(a_done, 1)
                    if step < UNITS:
                        act.wait_ge(e_done, it * UNITS + (step + 1))
                        nc.scalar.activation(b, b, ACT.Ln, bias=1.0).then_inc(ln_done, 1)
                    if 0 <= step - T_LAG < UNITS:
                        u = step - T_LAG
                        keys = units[u][3]
                        act.wait_ge(turned_done, it * UNITS + (u + 1 + BUFS))
                        act.wait_ge(av_done, it * UNITS + (u + 1))
                        nc.scalar.copy(aT[u % 2][:, 0:keys], turned[u % 2][:, 0:keys]).then_inc(aT_done, 1)

        @block.vector
        def _(dve):
            for s, count in ((arg_done, ZS), (turned_done, BUFS), (aT_done, 2), (av_done, 2), (o_read, 2)):
                dve.sem_inc(s, count)
            with dve.Fori(0, PAIRS) as it:
                for step in range(UNITS + O_LAG):
                    if step < UNITS:
                        keys = units[step][3]
                        b, zb, r = buf[step % BUFS][:, 0:keys], z[step % ZS][:, 0:keys], run[step % 2]
                        dve.wait_ge(ln_done, it * UNITS + (step + 1))
                        nc.vector.scalar_tensor_tensor(out=b, in0=b, scalar=LN_MAX, in1=zb, op0=ALU.min,
                                                       op1=ALU.max).then_inc(sp_done, 1)
                    if 0 <= step - 1 < UNITS:
                        u = step - 1
                        n = units[u][3]
                        dve.wait_ge(run_done, it * UNITS + (u + 1))
                        nc.vector.tensor_tensor(buf[u % BUFS][:, 0:n], z[u % ZS][:, 0:n], run[u % 2][:, 0:n],
                                                ALU.subtract).then_inc(arg_done, 1)
                    if step < UNITS:
                        back = b[:, ::-1]
                        start = 0.0 if units[step][4] else run[(step - 1) % 2][:, 0:1]
                        dve.wait_ge(sp_done, it * UNITS + (step + 1))
                        dve.wait_ge(arg_done, it * UNITS + (step - 1 + ZS))
                        nc.vector.tensor_tensor_scan(r[:, 0:keys][:, ::-1], back, back, start, ALU.add, ALU.bypass)\
                            .then_inc(run_done, 1)
                    if 0 <= step - O_LAG < UNITS and units[step - O_LAG][5]:
                        u = step - O_LAG
                        head, i = units[u][0:2]
                        dve.wait_ge(av_done, it * UNITS + (u + 3))
                        nc.vector.tensor_copy(y_sb[:, i, bass.ds(it * P + head * SB_DIM, SB_DIM)],
                                              o[i % 2][:, head * SB_DIM:(head + 1) * SB_DIM]).then_inc(o_read, 1)


def until(engine, semaphore, count):
    if not isinstance(count, int) or count > 0:
        engine.wait_ge(semaphore, count)


def split_weights(nc, tiles, raw, hi, lo, loaded, hi_done, lo_done):
    def load(sp):
        for k, rows in enumerate(tiles):
            until(sp, lo_done, k - 1)
            sp.dma_start(raw[k % 2][:], rows).then_inc(loaded[k % 2], 16)

    def high(act):
        for k in range(len(tiles)):
            act.wait_ge(loaded[k % 2], 16 * (k // 2 + 1))
            nc.scalar.copy(hi[:, k, :], raw[k % 2][:]).then_inc(hi_done, 1)

    def low(dve):
        for k in range(len(tiles)):
            dve.wait_ge(hi_done, k + 1)
            nc.vector.tensor_tensor(lo[:, k, :], raw[k % 2][:], hi[:, k, :].bitcast(F32), ALU.subtract)\
                .then_inc(lo_done, 1)

    return load, high, low


def mlstm_and_output_projection(nc, x, ml_i_bias, ml_f_bias, w_out, post_norm_w, ml_t, proj_n, gates_t, y_sb,
                                residual):
    with ExitStack() as ctx:
        def sb(name, shape, dt=F32):
            return ctx.enter_context(nc.sbuf_tensor(name, shape, dt))

        def sem(name):
            return ctx.enter_context(nc.semaphore(name))

        def psum(name, shape):
            return ctx.enter_context(nc.psum_tensor(name, shape, F32))

        H, DV = ML_HEADS, ML_DIM + 1
        A, CARRY, FLOOR, KEY = range(4)

        w_raw = [sb(f"c_w_raw{s}", [P, D_MODEL]) for s in range(2)]
        w_hi = sb("c_w_hi", [P, KT, D_MODEL], F32R)
        w_lo = sb("c_w_lo", [P, KT, D_MODEL], F32R)
        post_w = sb("c_post_w", [P, D_MODEL])
        ident = sb("c_ident", [P, P])
        minus_half = sb("c_minus_half", [P, SB_HEADS + H])
        eps = sb("c_eps", [P, SB_HEADS + H])
        ident_b = sb("c_ident_b", [P, P], BF16)
        hidden = sb("c_hidden", [P, 2, P], BF16)
        sel = sb("c_sel", [H, H, P])
        neg_m = sb("c_neg_m", [H, SEQ])
        cols = sb("c_cols", [P, TOK, 4, H])
        decay = sb("c_decay", [P, H, TOK])
        state = sb("c_state", [P, H, DV + 3])
        vx = [sb(f"c_vx{s}", [P, H, DV + 3]) for s in range(2)]

        scores = psum("c_scores", [P, 2, 2, P])
        k_turned = psum("c_k_turned", [P, 2, P])
        inter = psum("c_inter", [P, 2, 256])
        intra = psum("c_intra", [P, 2, 256])
        update = psum("c_update", [P, 2, 256])
        turned = psum("c_turned", [P, GROUP])
        out = [psum(f"c_out{n}", [P, GROUP]) for n in range(2)]

        w_loaded = [sem(f"c_w_loaded{s}") for s in range(2)]
        w_hi_done = sem("c_w_hi_done")
        w_lo_done = sem("c_w_lo_done")
        post_w_loaded = sem("c_post_w_loaded")
        zeroed = sem("c_zeroed")
        consts_ready = sem("c_consts_ready")
        load_w, split_hi, split_lo = split_weights(nc, [w_out[k * P:(k + 1) * P, :] for k in range(KT)], w_raw,
                                                   w_hi, w_lo, w_loaded, w_hi_done, w_lo_done)

        with ExitStack() as rows_ctx:
            def row(name, shape):
                return rows_ctx.enter_context(nc.sbuf_tensor(name, shape, F32))

            bias = row("g_bias", [H, 2])
            i_row = row("g_i", [H, SEQ])
            f_row = row("g_f", [H, SEQ])
            sp_row = row("g_sp", [H, SEQ])
            neg_b = row("g_neg_b", [H, SEQ])
            reset = row("g_reset", [H, SEQ])
            shift = row("g_shift", [H, SEQ])
            m_row = row("g_m", [H, SEQ])
            m_before = row("g_m_before", [H, TOK])
            chunk_decay = row("g_chunk_decay", [H, TOK])
            stack = row("g_stack", [P, SEQ])

            g_loaded = sem("g_loaded")
            g_dve = sem("g_dve")
            g_act = sem("g_act")
            g_turned = sem("g_turned")
            g_copied = sem("g_copied")
            g_decay = sem("g_decay")

            def chunked(t):
                return t[:].rearrange("h (c t) -> h c t", t=P)

            def ends(t):
                return chunked(t)[:, :, P - 1]

            block = rows_ctx.enter_context(nc.Block())

            @block.sync
            def _(sp):
                sp.dma_start(i_row[:], gates_t[0:H, :]).then_inc(g_loaded, 16)
                sp.dma_start(f_row[:], gates_t[H:2 * H, :]).then_inc(g_loaded, 16)
                with nc.allow_non_contiguous_dma("eight biases"):
                    sp.dma_start(bias[:, 0:1], ml_i_bias.rearrange("a h -> h a")).then_inc(g_loaded, 16)
                    sp.dma_start(bias[:, 1:2], ml_f_bias.rearrange("a h -> h a")).then_inc(g_loaded, 16)
                sp.dma_start(post_w[:], post_norm_w.broadcast_to([P, D_MODEL])).then_inc(post_w_loaded, 16)
                load_w(sp)
                sp.wait_ge(post_w_loaded, 16)

            @block.gpsimd
            def _(pool):
                nc.gpsimd.memset(reset[:], 1.0).then_inc(zeroed, 1)
                for t in (shift, m_before, stack, ident, ident_b, hidden, sel, state):
                    nc.gpsimd.memset(t[:], 0.0).then_inc(zeroed, 1)
                nc.gpsimd.memset(minus_half[:], -0.5).then_inc(consts_ready, 1)
                nc.gpsimd.memset(eps[:], EPS).then_inc(consts_ready, 1)
                for s in range(2):
                    nc.gpsimd.memset(vx[s][:, :, ML_DIM:DV], 1.0).then_inc(consts_ready, 1)
                pool.wait_ge(zeroed, 9)
                nc.gpsimd.memset(chunked(reset)[:, :, 0:1], 0.0).then_inc(consts_ready, 1)
                for t in (ident, ident_b):
                    nc.gpsimd.affine_select(out=t[:], in_=t[:], compare_op=ALU.not_equal, fill=1.0, base=0,
                                            pattern=[[-1, P]], channel_multiplier=1).then_inc(consts_ready, 1)
                nc.gpsimd.affine_select(out=hidden[:], in_=hidden[:], compare_op=ALU.is_ge, fill=MASKED, base=0,
                                        pattern=[[0, 2], [1, P]], channel_multiplier=-1).then_inc(consts_ready, 1)
                nc.gpsimd.affine_select(out=sel[:], in_=sel[:], compare_op=ALU.not_equal, fill=1.0, base=0,
                                        pattern=[[-1, H], [0, P]], channel_multiplier=1).then_inc(consts_ready, 1)

            @block.scalar
            def _(act):
                act.preload_act_table_set("natural_log_exp_and_others")
                act.wait_ge(g_dve, 1)
                nc.scalar.activation(sp_row[:], f_row[:], ACT.Exp).then_inc(g_act, 1)
                act.wait_ge(g_act, 1)
                nc.scalar.activation(sp_row[:], sp_row[:], ACT.Ln, bias=1.0).then_inc(g_act, 1)
                act.wait_ge(g_dve, 9)
                nc.scalar.activation(stack[32:32 + H, :], i_row[:], ACT.Exp).then_inc(g_act, 1)
                act.wait_ge(g_dve, 10)
                nc.scalar.activation(stack[64:64 + H, :], reset[:], ACT.Exp).then_inc(g_act, 1)
                act.wait_ge(g_dve, 11)
                nc.scalar.activation(shift[:], shift[:], ACT.Exp).then_inc(g_act, 1)
                act.wait_ge(g_dve, 12)
                nc.scalar.activation(chunk_decay[:], chunk_decay[:], ACT.Exp).then_inc(g_act, 1)
                split_hi(act)

            @block.vector
            def _(dve):
                dve.wait_ge(g_loaded, 64)
                dve.wait_ge(consts_ready, 9)
                nc.vector.tensor_scalar(f_row[:], f_row[:], bias[:, 1:2], -1.0, ALU.add, ALU.mult).then_inc(g_dve, 1)
                dve.wait_ge(g_act, 2)
                nc.vector.scalar_tensor_tensor(out=sp_row[:], in0=sp_row[:], scalar=LN_MAX, in1=f_row[:],
                                               op0=ALU.min, op1=ALU.max).then_inc(g_dve, 1)
                dve.wait_ge(g_dve, 2)
                nc.vector.tensor_tensor_scan(neg_b[:], reset[:], sp_row[:], 0.0, ALU.mult, ALU.add).then_inc(g_dve, 1)
                dve.wait_ge(g_dve, 3)
                nc.vector.scalar_tensor_tensor(out=stack[0:H, :], in0=i_row[:], scalar=bias[:, 0:1], in1=neg_b[:],
                                               op0=ALU.add, op1=ALU.add).then_inc(g_dve, 1)
                nc.vector.tensor_scalar_mul(chunked(shift)[:, 1:, 0], ends(neg_b)[:, :TOK - 1], -1.0).then_inc(g_dve, 1)
                dve.wait_ge(g_dve, 5)
                nc.vector.tensor_tensor_scan(m_row[:], shift[:], stack[0:H, :], 0.0, ALU.add, ALU.max)\
                    .then_inc(g_dve, 1)
                dve.wait_ge(g_dve, 6)
                nc.vector.tensor_tensor(m_before[:, 1:], ends(m_row)[:, :TOK - 1], ends(neg_b)[:, :TOK - 1],
                                        ALU.subtract).then_inc(g_dve, 1)
                nc.vector.tensor_scalar_mul(neg_m[:], m_row[:], -1.0).then_inc(g_dve, 1)
                dve.wait_ge(g_dve, 8)
                nc.vector.tensor_tensor(chunked(i_row), m_before[:].unsqueeze(2).broadcast_to([H, TOK, P]),
                                        chunked(m_row), ALU.subtract).then_inc(g_dve, 1)
                nc.vector.tensor_tensor(reset[:], neg_b[:], m_row[:], ALU.subtract).then_inc(g_dve, 1)
                nc.vector.tensor_tensor(chunked(shift), stack[0:H, :].rearrange("h (c t) -> h c t", t=P),
                                        chunked(m_row)[:, :, P - 1:P].broadcast_to([H, TOK, P]),
                                        ALU.subtract).then_inc(g_dve, 1)
                nc.vector.tensor_tensor(chunk_decay[:], m_before[:], ends(m_row), ALU.subtract).then_inc(g_dve, 1)
                dve.wait_ge(g_act, 5)
                nc.vector.tensor_scalar_mul(stack[96:96 + H, :], shift[:], ML_SCALE).then_inc(g_dve, 1)
                split_lo(dve)
                for n in range(TOK // 4):
                    dve.wait_ge(g_turned, n + 1)
                    nc.vector.tensor_copy(cols[:, 4 * n:4 * n + 4, :, :],
                                          (turned, out[0])[n % 2][:].rearrange("p (c q x) -> p c q x", c=4, q=4)
                                          [:, :, :, 0:H]).then_inc(g_copied, 1)
                dve.wait_ge(g_decay, 1)
                nc.vector.tensor_copy(decay[:], out[1][:, 0:H * TOK].rearrange("p (h c) -> p h c", h=H))\
                    .then_inc(g_copied, 1)

            @block.tensor
            def _(pe):
                pe.wait_ge(g_act, 6)
                pe.wait_ge(g_dve, 13)
                for n in range(TOK // 4):
                    until(pe, g_copied, n - 1)
                    for c in range(4):
                        mm = pe.transpose((turned, out[0])[n % 2][:, c * P:(c + 1) * P],
                                          stack[:, (4 * n + c) * P:(4 * n + c + 1) * P], ident[:])
                    mm.then_inc(g_turned, 1)
                for h in range(H):
                    mm = pe.matmul(out[1][:, h * TOK:(h + 1) * TOK], sel[:, h, :], chunk_decay[:],
                                   start=True, stop=True)
                mm.then_inc(g_decay, 1)

        qk = [sb(f"c_qk{s}", [P, 2 * H, P]) for s in range(2)]
        gates = [sb(f"c_gates{s}", [P, 3 * GROUP]) for s in range(2)]
        x_in = [sb(f"c_x{s}", [P, D_MODEL]) for s in range(2)]
        h_out = [sb(f"c_h{s}", [P, D_MODEL]) for s in range(2)]
        wt = [sb(f"c_wt{s}", [P, 2, P]) for s in range(2)]
        kw = [sb(f"c_kw{s}", [P, 2, P]) for s in range(2)]
        carried = [sb(f"c_carried{s}", [P, 2, DV + 3]) for s in range(2)]
        num = sb("c_num", [P, H, DV + 3])
        den = sb("c_den", [P, 3, H])
        y = [sb(f"c_y{s}", [P, D_MODEL]) for s in range(2)]
        squares = sb("c_squares", [P, D_MODEL])
        ss = sb("c_ss", [P, SB_HEADS + H])
        rstd = sb("c_rstd", [P, SB_HEADS + H])
        post_ss = sb("c_post_ss", [P, 2])
        post_rstd = sb("c_post_rstd", [P, 2])
        junk = sb("c_junk", [P, 2, GROUP])
        yT_hi = sb("c_yT_hi", [P, KT, P], F32R)
        yT_lo = sb("c_yT_lo", [P, KT, P], F32R)

        def per_slot(name):
            return [sem(f"{name}{s}") for s in range(2)]

        qk_loaded, v_loaded, gates_loaded, x_loaded = map(per_slot, ("c_qk_loaded", "c_v_loaded", "c_gates_loaded",
                                                                      "c_x_loaded"))
        h_stored = per_slot("c_h_stored")
        scores_done = sem("scores_done")
        k_turned_done = sem("k_turned_done")
        weights_done = sem("weights_done")
        p_done = sem("p_done")
        kw_done = sem("kw_done")
        inter_done = sem("inter_done")
        carried_done = sem("carried_done")
        intra_done = sem("intra_done")
        num_done = sem("num_done")
        update_done = sem("update_done")
        state_done = sem("state_done")
        den_done = sem("den_done")
        ml_y_done = sem("ml_y_done")
        squares_done = sem("squares_done")
        ss_done = sem("ss_done")
        mean_done = sem("c_mean_done")
        rstd_done = sem("c_rstd_done")
        scaled_done = sem("scaled_done")
        sb_y_done = sem("sb_y_done")
        ml_gated = sem("ml_gated")
        y_turned = sem("y_turned")
        yT_hi_done = sem("yT_hi_done")
        yT_lo_done = sem("yT_lo_done")
        out_done = sem("c_out_done")
        post_ss_done = sem("post_ss_done")
        post_mean_done = sem("post_mean_done")
        post_rstd_done = sem("post_rstd_done")
        normed_done = sem("normed_done")
        h_done = sem("h_done")

        block = ctx.enter_context(nc.Block())
        LAG = 2

        FIRST = 2 * LAG

        def steps(fori, step):
            for c in range(FIRST):
                step(c, c % 2, True, c >= LAG)
            with fori(0, (TOK - FIRST) // 2) as n:
                for s in range(2):
                    step(2 * n + (FIRST + s), s, True, True)
            for c in range(TOK, TOK + LAG):
                step(c, c % 2, False, True)

        def tile(c):
            return bass.ds(c * P, P) if not isinstance(c, int) else slice(c * P, (c + 1) * P)

        def at(c):
            return bass.ds(c, 1) if not isinstance(c, int) else slice(c, c + 1)

        @block.sync
        def _(sp):
            def step(c, s, mlstm, dense):
                if mlstm:
                    until(sp, update_done, 2 * c - 2)
                    src = ml_t[:, tile(c)].rearrange("(j p) t -> p j t", p=P)
                    sp.dma_start(qk[s][:], src).then_inc(qk_loaded[s], 16)
                    sp.dma_start(vx[s][:, :, 0:ML_DIM],
                                 proj_n[tile(c), 2 * GROUP:3 * GROUP].rearrange("p (h d) -> p h d", h=H))\
                        .then_inc(v_loaded[s], 16)
                    until(sp, sb_y_done, c - 1)
                    until(sp, ml_gated, c - 1)
                    sp.dma_start(gates[s][:, 0:GROUP], proj_n[tile(c), GROUP:2 * GROUP]).then_inc(gates_loaded[s], 16)
                    sp.dma_start(gates[s][:, GROUP:], proj_n[tile(c), 3 * GROUP:5 * GROUP])\
                        .then_inc(gates_loaded[s], 16)
                if dense:
                    d = c - LAG
                    until(sp, h_done, d - 1)
                    sp.dma_start(x_in[s][:], x[tile(d), :]).then_inc(x_loaded[s], 16)
                    if not isinstance(c, int) or c > LAG:
                        store(d - 1, 1 - s)

            def store(d, s):
                until(sp, h_done, d + 1)
                sp.dma_start(residual[tile(d), :], h_out[s][:]).then_inc(h_stored[s], 16)

            steps(sp.Fori, step)
            store(TOK - 1, 1)
            for s in range(2):
                sp.wait_ge(h_stored[s], 16 * (TOK // 2))

        @block.tensor
        def _(pe):
            def score(u, c, s, p):
                q, k = qk[s][:, 2 * p:2 * p + 2, :], qk[s][:, H + 2 * p:H + 2 * p + 2, :]
                if p == 0:
                    pe.wait_ge(qk_loaded[s], 16 * (c // 2) + 16 if isinstance(c, int) else (c - s) * 8 + 16)
                until(pe, p_done, u)
                for i in range(2):
                    pe.matmul(scores[:, 0, i, :], k[:, i, :], q[:, i, :], start=True, stop=True)
                pe.matmul(scores[:, 1, :, :], ident_b[:], hidden[:], start=True, stop=False)
                for i in range(2):
                    mm = pe.matmul(scores[:, 1, i, :], sel[:, 2 * p + i, :], neg_m[:, tile(c)], start=False, stop=(i == 1))
                mm.then_inc(scores_done, 1)
                until(pe, kw_done, u)
                for i in range(2):
                    mm = pe.transpose(k_turned[:, i, :], k[:, i, :], ident[:])
                mm.then_inc(k_turned_done, 1)

            def combine(u, c, s, p):
                if p == 0:
                    pe.wait_ge(v_loaded[s], 16 * (c // 2) + 16 if isinstance(c, int) else (c - s) * 8 + 16)
                until(pe, state_done, u - 1)
                until(pe, carried_done, u)
                for i in range(2):
                    mm = pe.matmul(inter[:, i, 0:DV], qk[s][:, 2 * p + i, :], state[:, 2 * p + i, 0:DV],
                                   start=True, stop=True)
                mm.then_inc(inter_done, 1)
                until(pe, p_done, u + 1)
                until(pe, num_done, u)
                for i in range(2):
                    mm = pe.matmul(intra[:, i, 0:DV], wt[p][:, i, :], vx[s][:, 2 * p + i, 0:DV], start=True, stop=True)
                mm.then_inc(intra_done, 1)
                until(pe, kw_done, u + 1)
                until(pe, state_done, u)
                for i in range(2):
                    mm = pe.matmul(update[:, i, 0:DV], kw[p][:, i, :], vx[s][:, 2 * p + i, 0:DV],
                                   start=True, stop=True)
                mm.then_inc(update_done, 1)

            def turn(d, s):
                until(pe, sb_y_done, d + 1)
                until(pe, ml_gated, d + 1)
                for h in range(2):
                    until(pe, yT_lo_done, 2 * d + h)
                    for k in range(4):
                        mm = pe.transpose(turned[:, k * P:(k + 1) * P], y[s][:, (4 * h + k) * P:(4 * h + k + 1) * P],
                                          ident[:])
                    mm.then_inc(y_turned, 1)

            def project(d, n):
                if n == 0:
                    until(pe, yT_lo_done, 2 * d + 2)
                until(pe, normed_done, 2 * d - 1 + n)
                for k in range(KT):
                    for j, (yT, w) in enumerate(((yT_lo, w_hi), (yT_hi, w_lo), (yT_hi, w_hi))):
                        mm = pe.matmul(out[n][:], yT[:, k, :], w[:, k, n * GROUP:(n + 1) * GROUP],
                                       start=(k == 0 and j == 0), stop=(k == KT - 1 and j == 2))
                mm.then_inc(out_done, 1)

            def step(c, s, mlstm, dense):
                if mlstm:
                    score(2 * c, c, s, 0)
                if dense:
                    turn(c - LAG, s)
                    project(c - LAG, 0)
                if mlstm:
                    score(2 * c + 1, c, s, 1)
                    combine(2 * c, c, s, 0)
                if dense:
                    project(c - LAG, 1)
                if mlstm:
                    combine(2 * c + 1, c, s, 1)

            steps(pe.Fori, step)

        @block.scalar
        def _(act):
            act.preload_act_table_set("natural_log_exp_and_others")

            def weigh(u, c, p):
                until(act, scores_done, u + 1)
                until(act, intra_done, u - 1)
                for i in range(2):
                    a = nc.scalar.activation(wt[p][:, i, :], scores[:, 1, i, :], ACT.Exp,
                                             bias=cols[:, at(c), A, 2 * p + i])
                a.then_inc(weights_done, 1)
                until(act, k_turned_done, u + 1)
                until(act, update_done, u - 1)
                for i in range(2):
                    a = nc.scalar.activation(kw[p][:, i, :], k_turned[:, i, :], ACT.Copy,
                                             scale=cols[:, at(c), KEY, 2 * p + i])
                a.then_inc(kw_done, 1)

            def carry(u, c, p):
                until(act, inter_done, u + 1)
                until(act, num_done, u - 1)
                for i in range(2):
                    a = nc.scalar.activation(carried[p][:, i, 0:DV], inter[:, i, 0:DV], ACT.Copy,
                                             scale=cols[:, at(c), CARRY, 2 * p + i])
                a.then_inc(carried_done, 1)

            def high(d):
                for h in range(2):
                    until(act, y_turned, 2 * d + h + 1)
                    until(act, out_done, 2 * d)
                    nc.scalar.copy(yT_hi[:, 4 * h:4 * h + 4, :], turned[:].rearrange("p (k t) -> p k t", k=4))\
                        .then_inc(yT_hi_done, 1)

            def square(b):
                until(act, ss_done, 2 * b)
                nc.scalar.activation(squares[:, 0:SB_WIDTH], y_sb[:, at(b), :].rearrange("p a n -> p (a n)"),
                                     ACT.Square, scale=SB_DIM ** -0.5).then_inc(squares_done, 1)
                until(act, ml_y_done, b + 1)
                nc.scalar.activation(squares[:, SB_WIDTH:], num[:, :, 0:ML_DIM], ACT.Square, scale=ML_DIM ** -0.5)\
                    .then_inc(squares_done, 1)

            def square_out(d, n):
                until(act, out_done, 2 * d + n + 1)
                until(act, post_mean_done, 2 * d)
                nc.scalar.activation(junk[:, n, :], out[n][:], ACT.Square, scale=D_MODEL ** -0.5,
                                     accum_out=post_ss[:, n:n + 1])\
                    .then_inc(post_ss_done, 1)

            def step(c, s, mlstm, dense):
                if mlstm:
                    weigh(2 * c, c, 0)
                if dense:
                    high(c - LAG)
                if not (isinstance(c, int) and not 1 <= c <= TOK):
                    square(c - 1)
                if mlstm:
                    weigh(2 * c + 1, c, 1)
                    carry(2 * c, c, 0)
                if dense:
                    square_out(c - LAG, 0)
                    square_out(c - LAG, 1)
                if mlstm:
                    carry(2 * c + 1, c, 1)

            steps(act.Fori, step)

        @block.gpsimd
        def _(pool):
            def head_norms(b, s):
                until(pool, ss_done, 2 * b + 2)
                until(pool, ml_gated, b)
                nc.gpsimd.tensor_tensor(ss[:], ss[:], eps[:], ALU.add).then_inc(mean_done, 1)
                until(pool, mean_done, b + 1)
                nc.gpsimd.tensor_tensor(rstd[:], ss[:], minus_half[:], ALU.pow).then_inc(rstd_done, 1)
                until(pool, scaled_done, b + 1)
                nc.gpsimd.tensor_tensor(y[s][:, 0:SB_WIDTH], y[s][:, 0:SB_WIDTH], gates[s][:, 0:GROUP], ALU.mult)\
                    .then_inc(sb_y_done, 1)

            def post_norm(d):
                until(pool, post_ss_done, 2 * d + 2)
                until(pool, normed_done, 2 * d)
                nc.gpsimd.tensor_tensor(post_rstd[:, 0:1], post_ss[:, 0:1], post_ss[:, 1:2], ALU.add)\
                    .then_inc(post_mean_done, 1)
                until(pool, post_mean_done, 2 * d + 1)
                nc.gpsimd.tensor_tensor(post_rstd[:, 0:1], post_rstd[:, 0:1], eps[:, 0:1], ALU.add)\
                    .then_inc(post_mean_done, 1)
                until(pool, post_mean_done, 2 * d + 2)
                nc.gpsimd.tensor_tensor(post_rstd[:, 1:2], post_rstd[:, 0:1], minus_half[:, 0:1], ALU.pow)\
                    .then_inc(post_rstd_done, 1)

            def add_residual(d, s):
                until(pool, normed_done, 2 * d + 2)
                pool.wait_ge(x_loaded[s], 16 * (d // 2) + 16 if isinstance(d, int) else (d - s) * 8 + 16)
                nc.gpsimd.tensor_tensor(h_out[s][:], h_out[s][:], x_in[s][:], ALU.add).then_inc(h_done, 1)

            def step(c, s, mlstm, dense):
                if not (isinstance(c, int) and not 1 <= c <= TOK):
                    head_norms(c - 1, 1 - s)
                if dense:
                    post_norm(c - LAG)
                    add_residual(c - LAG, s)

            steps(pool.Fori, step)

        @block.vector
        def _(dve):
            def weights_times_scores(u, p):
                until(dve, weights_done, u + 1)
                nc.vector.scalar_tensor_tensor(out=wt[p][:], in0=scores[:, 0, :, :], scalar=ML_SCALE, in1=wt[p][:],
                                               op0=ALU.mult, op1=ALU.mult).then_inc(p_done, 1)

            def low(d):
                for h in range(2):
                    until(dve, yT_hi_done, 2 * d + h + 1)
                    nc.vector.tensor_tensor(yT_lo[:, 4 * h:4 * h + 4, :], turned[:].rearrange("p (k t) -> p k t", k=4),
                                            yT_hi[:, 4 * h:4 * h + 4, :].bitcast(F32), ALU.subtract)\
                        .then_inc(yT_lo_done, 1)

            def norm_heads(b, s):
                for n, (first, heads, width) in enumerate(((0, SB_HEADS, SB_DIM), (SB_WIDTH, H, ML_DIM))):
                    until(dve, squares_done, 2 * b + n + 1)
                    if n == 0:
                        until(dve, rstd_done, b)
                    nc.vector.tensor_reduce(ss[:, (0, SB_HEADS)[n]:(SB_HEADS, SB_HEADS + H)[n]],
                                            squares[:, first:first + heads * width]
                                            .rearrange("p (h d) -> p h d", h=heads), AX.X, ALU.add)\
                        .then_inc(ss_done, 1)
                until(dve, rstd_done, b + 1)
                until(dve, y_turned, 2 * b - 2)
                nc.vector.tensor_tensor(y[s][:, 0:SB_WIDTH].rearrange("p (h d) -> p h d", h=SB_HEADS),
                                        y_sb[:, at(b), :].rearrange("p a (h d) -> p (a h) d", h=SB_HEADS),
                                        rstd[:, 0:SB_HEADS].unsqueeze(2).broadcast_to([P, SB_HEADS, SB_DIM]),
                                        ALU.mult).then_inc(scaled_done, 1)
                for h in range(H):
                    i = nc.vector.scalar_tensor_tensor(
                        out=y[s][:, SB_WIDTH + h * ML_DIM:SB_WIDTH + (h + 1) * ML_DIM], in0=num[:, h, 0:ML_DIM],
                        scalar=rstd[:, SB_HEADS + h:SB_HEADS + h + 1],
                        in1=gates[s][:, 2 * GROUP + h * ML_DIM:2 * GROUP + (h + 1) * ML_DIM],
                        op0=ALU.mult, op1=ALU.mult)
                i.then_inc(ml_gated, 1)

            def numerator(u, c, p):
                until(dve, carried_done, u + 1)
                until(dve, intra_done, u + 1)
                until(dve, ml_gated, c)
                nc.vector.tensor_tensor(num[:, 2 * p:2 * p + 2, 0:DV], carried[p][:, :, 0:DV], intra[:, :, 0:DV],
                                        ALU.add).then_inc(num_done, 1)
                until(dve, update_done, u + 1)
                for i in range(2):
                    h = 2 * p + i
                    a = nc.vector.scalar_tensor_tensor(out=state[:, h, 0:DV], in0=state[:, h, 0:DV],
                                                       scalar=decay[:, h, at(c)], in1=update[:, i, 0:DV],
                                                       op0=ALU.mult, op1=ALU.add)
                a.then_inc(state_done, 1)

            def divide(c, s):
                until(dve, num_done, 2 * c + 2)
                dens = num[:, :, ML_DIM]
                nc.vector.scalar_tensor_tensor(out=den[:, 0, :], in0=dens, scalar=-1.0, in1=dens,
                                               op0=ALU.mult, op1=ALU.max).then_inc(den_done, 1)
                until(dve, den_done, 3 * c + 1)
                nc.vector.tensor_tensor(den[:, 1, :], den[:, 0, :],
                                        cols[:, at(c), FLOOR, :].rearrange("p a h -> p (a h)"), ALU.max)\
                    .then_inc(den_done, 1)
                until(dve, den_done, 3 * c + 2)
                nc.vector.reciprocal(den[:, 2, :], den[:, 1, :]).then_inc(den_done, 1)
                until(dve, den_done, 3 * c + 3)
                dve.wait_ge(gates_loaded[s], 32 * (c // 2) + 32 if isinstance(c, int) else (c - s) * 16 + 32)
                for h in range(H):
                    i = nc.vector.scalar_tensor_tensor(
                        out=num[:, h, 0:ML_DIM], in0=num[:, h, 0:ML_DIM], scalar=den[:, 2, h:h + 1],
                        in1=gates[s][:, GROUP + h * ML_DIM:GROUP + (h + 1) * ML_DIM], op0=ALU.mult, op1=ALU.mult)
                i.then_inc(ml_y_done, 1)

            def post(d, s):
                until(dve, post_rstd_done, d + 1)
                until(dve, h_stored[s], 16 * ((d - s) // 2) if isinstance(d, int) else (d - s) * 8)
                for n in range(2):
                    half = slice(n * GROUP, (n + 1) * GROUP)
                    nc.vector.scalar_tensor_tensor(out=h_out[s][:, half], in0=out[n][:], scalar=post_rstd[:, 1:2],
                                                   in1=post_w[:, half], op0=ALU.mult, op1=ALU.mult)\
                        .then_inc(normed_done, 1)

            def step(c, s, mlstm, dense):
                if mlstm:
                    weights_times_scores(2 * c, 0)
                if dense:
                    low(c - LAG)
                if not (isinstance(c, int) and not 1 <= c <= TOK):
                    norm_heads(c - 1, 1 - s)
                if mlstm:
                    weights_times_scores(2 * c + 1, 1)
                    numerator(2 * c, c, 0)
                    numerator(2 * c + 1, c, 1)
                    divide(c, s)
                if dense:
                    post(c - LAG, s)

            steps(dve.Fori, step)


def layer_embedding(nc, p, ple_w_up, ple_w_gate, ple_b_gate, residual, result):
    with ExitStack() as ctx:
        def sb(name, shape, dt=F32):
            return ctx.enter_context(nc.sbuf_tensor(name, shape, dt))

        def sem(name):
            return ctx.enter_context(nc.semaphore(name))

        def psum(name, shape):
            return ctx.enter_context(nc.psum_tensor(name, shape, F32))

        PT = PLE // P
        w_raw = [sb(f"d_w_raw{s}", [P, D_MODEL]) for s in range(2)]
        w_hi = sb("d_w_hi", [P, KT + PT, D_MODEL], F32R)
        w_lo = sb("d_w_lo", [P, KT + PT, D_MODEL], F32R)
        bias = sb("d_bias", [P, D_MODEL])
        ident = sb("d_ident", [P, P])
        h_in = [sb(f"d_h{s}", [P, D_MODEL]) for s in range(2)]
        p_in = [sb(f"d_p{s}", [P, PLE]) for s in range(2)]
        hT_hi = [sb(f"d_hT_hi{s}", [P, KT + PT, P], F32R) for s in range(2)]
        hT_lo = [sb(f"d_hT_lo{s}", [P, KT + PT, P], F32R) for s in range(2)]
        gate = [sb(f"d_gate{s}", [P, D_MODEL]) for s in range(2)]
        turned = [psum(f"d_turned{n}", [P, GROUP]) for n in range(3)]
        product = [psum(f"d_product{n}", [P, GROUP]) for n in range(4)]

        w_loaded = [sem(f"d_w_loaded{s}") for s in range(2)]
        w_hi_done = sem("d_w_hi_done")
        w_lo_done = sem("d_w_lo_done")
        bias_loaded = sem("d_bias_loaded")
        zeroed = sem("d_zeroed")
        ident_ready = sem("d_ident_ready")
        h_loaded = [sem(f"d_h_loaded{s}") for s in range(2)]
        p_loaded = [sem(f"d_p_loaded{s}") for s in range(2)]
        stored = [sem(f"d_stored{s}") for s in range(2)]
        turned_done = sem("d_turned_done")
        hi_done = sem("d_hi_done")
        lo_done = sem("d_lo_done")
        product_done = sem("product_done")
        biased = sem("biased")
        sigmoid_done = sem("sigmoid_done")
        gated = sem("gated")
        sum_done = sem("sum_done")
        tiles = [ple_w_gate[k * P:(k + 1) * P, :] for k in range(KT)] + \
                [ple_w_up[k * P:(k + 1) * P, :] for k in range(PT)]
        load_w, split_hi, split_lo = split_weights(nc, tiles, w_raw, w_hi, w_lo, w_loaded, w_hi_done, w_lo_done)
        PIECES = ((0, 4), (4, 4), (KT, PT))
        block = ctx.enter_context(nc.Block())

        @block.gpsimd
        def _(pool):
            nc.gpsimd.memset(ident[:], 0.0).then_inc(zeroed, 1)
            pool.wait_ge(zeroed, 1)
            nc.gpsimd.affine_select(out=ident[:], in_=ident[:], compare_op=ALU.not_equal, fill=1.0, base=0,
                                    pattern=[[-1, P]], channel_multiplier=1).then_inc(ident_ready, 1)
            with pool.Fori(0, TOK // 2) as n:
                for s in range(2):
                    pool.wait_ge(sum_done, 2 * n + (s + 1))
                    pool.wait_ge(turned_done, 6 * n + (3 * s + 1))
                    rows = bass.ds((2 * n + s) * P, P)
                    pool.dma_start(h_in[s][:], residual[rows, :]).then_inc(h_loaded[s], 16)
                    pool.dma_start(p_in[s][:], p[rows, :]).then_inc(p_loaded[s], 16)

        @block.sync
        def _(sp):
            sp.dma_start(bias[:], ple_b_gate.broadcast_to([P, D_MODEL])).then_inc(bias_loaded, 16)
            load_w(sp)
            with sp.Fori(0, TOK // 2) as n:
                for s in range(2):
                    sp.wait_ge(sum_done, 2 * n + (s + 3))
                    sp.dma_start(result[bass.ds((2 * n + s) * P, P), :], gate[s][:]).then_inc(stored[s], 16)
            for s in range(2):
                sp.wait_ge(stored[s], 16 * (TOK // 2 + 1))

        @block.tensor
        def _(pe):
            def turn(n, s):
                pe.wait_ge(h_loaded[s], 16 * n + 16)
                pe.wait_ge(p_loaded[s], 16 * n + 16)
                for j, (k0, count) in enumerate(PIECES):
                    src = p_in[s] if k0 == KT else h_in[s]
                    pe.wait_ge(lo_done, 6 * n + (3 * s + j + 4))
                    for k in range(count):
                        at = (k0 % KT + k) * P
                        mm = pe.transpose(turned[j][:, k * P:(k + 1) * P], src[:, at:at + P], ident[:])
                    mm.then_inc(turned_done, 1)

            def multiply(n, s, first):
                if not first:
                    pe.wait_ge(lo_done, 6 * n + (3 * s + 3 + 6))
                for j in range(4):
                    if j < 2:
                        pe.wait_ge(biased, 4 * n + (2 * s + j + 1))
                    else:
                        pe.wait_ge(gated, 4 * n + (2 * s + j - 2 + 1))
                    half = slice(j % 2 * GROUP, (j % 2 + 1) * GROUP)
                    ks = range(KT) if j < 2 else range(KT, KT + PT)
                    for k in ks:
                        if first:
                            pe.wait_ge(w_lo_done, k + 1)
                        for i, (a, w) in enumerate(((hT_lo, w_hi), (hT_hi, w_lo), (hT_hi, w_hi))):
                            mm = pe.matmul(product[j][:], a[s][:, k, :], w[:, k, half],
                                           start=(k == ks[0] and i == 0), stop=(k == ks[-1] and i == 2))
                    mm.then_inc(product_done, 1)

            pe.wait_ge(ident_ready, 1)
            turn(0, 0)
            pe.wait_ge(lo_done, 9)
            turn(0, 1)
            multiply(0, 0, True)
            with pe.Fori(0, TOK // 2 - 1) as n:
                turn(n + 1, 0)
                multiply(n, 1, False)
                turn(n + 1, 1)
                multiply(n + 1, 0, False)
            multiply(TOK // 2 - 1, 1, False)

        @block.scalar
        def _(act):
            def high(n, s):
                for j, (k0, count) in enumerate(PIECES):
                    act.wait_ge(turned_done, 6 * n + (3 * s + j + 1 + 6))
                    nc.scalar.copy(hT_hi[s][:, k0:k0 + count, :],
                                   turned[j][:, 0:count * P].rearrange("p (k t) -> p k t", t=P)).then_inc(hi_done, 1)

            def sigmoid(n, s):
                act.wait_ge(biased, 4 * n + (2 * s + 2 + 2))
                nc.scalar.activation(gate[s][:], gate[s][:], ACT.Sigmoid).then_inc(sigmoid_done, 1)

            split_hi(act)
            high(0, 0)
            high(0, 1)
            with act.Fori(0, TOK // 2 - 1) as n:
                sigmoid(n, 0)
                high(n + 1, 0)
                sigmoid(n, 1)
                high(n + 1, 1)
            sigmoid(TOK // 2 - 1, 0)
            sigmoid(TOK // 2 - 1, 1)

        @block.vector
        def _(dve):
            for s, count in [(lo_done, 6), (turned_done, 6), (biased, 2), (gated, 2), (sum_done, 2)] + \
                            [(s, 16) for s in stored]:
                dve.sem_inc(s, count)

            def low(n, s):
                for j, (k0, count) in enumerate(PIECES):
                    dve.wait_ge(hi_done, 6 * n + (3 * s + j + 1))
                    nc.vector.tensor_tensor(hT_lo[s][:, k0:k0 + count, :],
                                            turned[j][:, 0:count * P].rearrange("p (k t) -> p k t", t=P),
                                            hT_hi[s][:, k0:k0 + count, :].bitcast(F32), ALU.subtract)\
                        .then_inc(lo_done, 1)

            def finish(n, s):
                dve.wait_ge(stored[s], 16 * n + 16)
                for j in range(2):
                    half = slice(j * GROUP, (j + 1) * GROUP)
                    dve.wait_ge(product_done, 8 * n + (4 * s + j + 1))
                    nc.vector.tensor_tensor(gate[s][:, half], product[j][:], bias[:, half], ALU.add)\
                        .then_inc(biased, 1)
                dve.wait_ge(sigmoid_done, 2 * n + (s + 1))
                for j in range(2):
                    half = slice(j * GROUP, (j + 1) * GROUP)
                    dve.wait_ge(product_done, 8 * n + (4 * s + j + 3))
                    nc.vector.tensor_tensor(gate[s][:, half], gate[s][:, half], product[2 + j][:], ALU.mult)\
                        .then_inc(gated, 1)
                dve.wait_ge(gated, 4 * n + (2 * s + 2 + 2))
                nc.vector.tensor_tensor(gate[s][:], gate[s][:], h_in[s][:], ALU.add).then_inc(sum_done, 1)

            split_lo(dve)
            low(0, 0)
            dve.wait_ge(bias_loaded, 16)
            low(0, 1)
            with dve.Fori(0, TOK // 2 - 1) as n:
                finish(n, 0)
                low(n + 1, 0)
                finish(n, 1)
                low(n + 1, 1)
            finish(TOK // 2 - 1, 0)
            finish(TOK // 2 - 1, 1)


def hybrid_block(nc, x, p, pre_norm_w, w_in, ml_conv_w, ml_conv_b, ml_i_bias, ml_f_bias, sb_norm_w, ml_norm_w,
                 w_out, post_norm_w, ple_w_up, ple_w_gate, ple_b_gate, out):
    def scratch(name, shape):
        return nc.dram_tensor(name, shape, F32, kind="Internal").ap()

    qk_hi = scratch("qk_hi", [2 * SB_WIDTH, SEQ])
    qk_lo = scratch("qk_lo", [2 * SB_WIDTH, SEQ])
    ml_t = scratch("ml_t", [2 * ML_WIDTH, SEQ])
    proj_n = scratch("proj_n", [SEQ, 5 * GROUP])
    gates_t = scratch("gates_t", [GATES, SEQ])
    residual = scratch("residual", [SEQ, D_MODEL])
    input_projection(nc, x[0], pre_norm_w, w_in[0], ml_conv_w[0], ml_conv_b, sb_norm_w, ml_norm_w,
                     qk_hi, qk_lo, ml_t, proj_n, gates_t)
    with nc.sbuf_tensor("y_sb", [P, TOK, SB_WIDTH], F32) as y_sb:
        stick_breaking_attention(nc, qk_hi, qk_lo, proj_n, y_sb)
        mlstm_and_output_projection(nc, x[0], ml_i_bias, ml_f_bias, w_out[0], post_norm_w, ml_t, proj_n, gates_t,
                                    y_sb, residual)
    layer_embedding(nc, p[0, 0], ple_w_up[0], ple_w_gate[0], ple_b_gate, residual, out[0])


_INS = ['x', 'p', 'pre_norm_w', 'w_in', 'ml_conv_w', 'ml_conv_b', 'ml_i_bias', 'ml_f_bias', 'sb_norm_w', 'ml_norm_w',
        'w_out', 'post_norm_w', 'ple_w_up', 'ple_w_gate', 'ple_b_gate']


def kernel(**inputs):
    import numpy as np
    import concourse.bacc as bacc
    from concourse.bass_utils import run_bass_kernel_spmd

    nc = bacc.Bacc("TRN2", target_bir_lowering=False, num_devices=1)
    arrays, args = {}, []
    for name in _INS:
        a = np.ascontiguousarray(inputs[name])
        arrays[f"in_{name}"] = a
        args.append(nc.dram_tensor(f"in_{name}", a.shape, mybir.dt.from_np(a.dtype), kind="ExternalInput").ap())
    out = nc.dram_tensor("out", (1, SEQ, D_MODEL), F32, kind="ExternalOutput").ap()
    hybrid_block(nc, *args, out)
    return run_bass_kernel_spmd(nc, [arrays], core_ids=[0]).results[0]["out"]
```

```python
from contextlib import ExitStack

import concourse.bass as bass
import concourse.mybir as mybir

P = 128
F32 = mybir.dt.float32
F32R = mybir.dt.float32r
BF16 = mybir.dt.bfloat16
ALU = mybir.AluOpType
ACT = mybir.ActivationFunctionType
AX = mybir.AxisListType

SEQ, D_MODEL, PLE = 2048, 1024, 256
SB_WIDTH, ML_WIDTH = 512, 512
SB_HEADS, SB_DIM = 8, 64
ML_HEADS, ML_DIM = 4, 128
CONV_K = 4
EPS = 1e-6
SB_SCALE = SB_DIM ** -0.5
ML_SCALE = ML_DIM ** -0.5

TOK = SEQ // P
KT = D_MODEL // P
GROUP = 512
TG = SEQ // GROUP
BANKS = 4
GATES = 2 * ML_HEADS
GATE_COL = 4 * SB_WIDTH + 5 * ML_WIDTH
GROUPS = GATE_COL // GROUP
MASKED = -1e30
BIG = 2.0 ** 100
LN_MAX = 40.0


def until(engine, semaphore, count):
    if not isinstance(count, int) or count > 0:
        engine.wait_ge(semaphore, count)


def input_projection(nc, x, pre_norm_w, w_in, conv_w, conv_b, sb_norm_w, ml_norm_w, qk_hi, qk_lo, ml_t, proj_n,
                     gates_t):
    with ExitStack() as ctx:
        def sb(name, shape, dt=F32):
            return ctx.enter_context(nc.sbuf_tensor(name, shape, dt))

        def sem(name):
            return ctx.enter_context(nc.semaphore(name))

        ident = sb("a_ident", [P, P])
        cw = sb("conv_w", [P, 2 * TG, CONV_K])
        cb = sb("conv_b", [P, 2 * TG])
        pre_w = sb("pre_w", [P, D_MODEL])
        minus_half = sb("a_minus_half", [P, 1])
        eps = sb("a_eps", [P, 1])
        x_in = [sb(f"x_in{i}", [P, D_MODEL]) for i in range(2)]
        xn = [sb(f"xn{i}", [P, D_MODEL]) for i in range(2)]
        mean_sq = sb("a_mean_sq", [P, 2])
        mean_eps = sb("a_mean_eps", [P, 2])
        rstd = sb("a_rstd", [P, 2])
        uT_hi = sb("uT_hi", [P, KT, SEQ], F32R)
        uT_lo = sb("uT_lo", [P, KT, SEQ], F32R)
        w_raw = sb("w_raw", [P, KT, GROUP])
        w_hi = sb("w_hi", [P, KT, GROUP], F32R)
        w_lo = sb("w_lo", [P, KT, GROUP], F32R)
        wg_raw = sb("wg_raw", [P, KT, GATES])
        wg_hi = sb("wg_hi", [P, KT, GATES], F32R)
        wg_lo = sb("wg_lo", [P, KT, GATES], F32R)
        stage = [x_in[i // 2][:, i % 2 * GROUP:(i % 2 + 1) * GROUP] for i in range(BANKS)]
        HALO = CONV_K - 1
        stage_hi = [sb(f"stage_hi{i}", [P, GROUP + HALO + 1], F32R) for i in range(2)]
        stage_lo = [sb(f"stage_lo{i}", [P, GROUP], F32R) for i in range(2)]
        conv_in = [t[:, 0:GROUP + HALO].bitcast(F32) for t in stage_hi]
        conv_out = [t[:].bitcast(F32) for t in stage_lo]
        gate_w = [xn[0][:, 0:SB_WIDTH], xn[0][:, SB_WIDTH:]]
        pt = [ctx.enter_context(nc.psum_tensor(f"a_pt{i}", [P, GROUP], F32)) for i in range(2)]
        po = [ctx.enter_context(nc.psum_tensor(f"a_po{i}", [P, GROUP], F32)) for i in range(BANKS)]

        consts_loaded = sem("a_consts_loaded")
        half_ready = sem("a_half_ready")
        ident_ready = sem("a_ident_ready")
        x_loaded = [sem(f"x_loaded{i}") for i in range(2)]
        x_read = sem("x_read")
        mean_sq_done = sem("a_mean_sq_done")
        mean_eps_done = sem("a_mean_eps_done")
        rstd_done = sem("a_rstd_done")
        xpose_done = sem("a_xpose_done")
        u_hi_done = sem("u_hi_done")
        u_lo_done = sem("u_lo_done")
        w_loaded = sem("w_loaded")
        wg_loaded = sem("wg_loaded")
        w_hi_done = sem("w_hi_done")
        w_lo_done = sem("w_lo_done")
        wg_hi_done = sem("wg_hi_done")
        wg_lo_done = sem("wg_lo_done")
        w_used = sem("w_used")
        out_ready = sem("out_ready")
        evacuated = [sem(f"evacuated{i}") for i in range(BANKS)]
        stored = [sem(f"stored{i}") for i in range(BANKS)]
        staged_hi = [sem(f"staged_hi{i}") for i in range(2)]
        stored_hi = [sem(f"stored_hi{i}") for i in range(2)]
        stored_lo = [sem(f"stored_lo{i}") for i in range(2)]

        conv_w_loaded = sem("conv_w_loaded")
        gate_w_loaded = sem("gate_w_loaded")
        halo_done = sem("halo_done")
        conv_in_done = sem("conv_in_done")
        tap_done = sem("tap_done")
        staged = [sem(f"staged{i}") for i in range(BANKS)]

        w_view = w_in.rearrange("(k p) n -> p k n", p=P)
        block = ctx.enter_context(nc.Block())

        @block.gpsimd
        def _(pool):
            nc.gpsimd.memset(minus_half[:], -0.5).then_inc(half_ready, 1)
            nc.gpsimd.memset(eps[:], EPS).then_inc(half_ready, 1)
            nc.gpsimd.memset(ident[:], 0.0).then_inc(half_ready, 1)
            pool.wait_ge(half_ready, 3)
            nc.gpsimd.affine_select(out=ident[:], in_=ident[:], compare_op=ALU.not_equal, fill=1.0, base=0,
                                    pattern=[[-1, P]], channel_multiplier=1).then_inc(ident_ready, 1)
            pool.dma_start(w_raw[:], w_view[:, :, 0:GROUP]).then_inc(w_loaded, 16)
            with nc.allow_non_contiguous_dma("eight gate columns"):
                pool.dma_start(wg_raw[:], w_view[:, :, GATE_COL:GATE_COL + GATES]).then_inc(wg_loaded, 16)
            with pool.Fori(0, TOK // 2) as n:
                for i in range(2):
                    m = mean_eps[:, i:i + 1]
                    pool.wait_ge(mean_sq_done, 2 * n + (i + 1))
                    pool.wait_ge(x_read, 2 * n + (i + 1))
                    nc.gpsimd.tensor_tensor(m, mean_sq[:, i:i + 1], eps[:], ALU.add).then_inc(mean_eps_done, 1)
                    pool.wait_ge(mean_eps_done, 2 * n + (i + 1))
                    nc.gpsimd.tensor_tensor(rstd[:, i:i + 1], m, minus_half[:], ALU.pow).then_inc(rstd_done, 1)
            with pool.Fori(1, GROUPS) as g:
                pool.wait_ge(w_lo_done, g * KT)
                pool.dma_start(w_raw[:], w_view[:, :, bass.ds(g * GROUP, GROUP)]).then_inc(w_loaded, 16)

        @block.sync
        def _(sp):
            sp.dma_start(pre_w[:], pre_norm_w.broadcast_to([P, D_MODEL])).then_inc(consts_loaded, 16)
            with sp.Fori(0, TOK // 2) as n:
                for i in range(2):
                    sp.wait_ge(x_read, 2 * n + (i + 1))
                    sp.dma_start(x_in[i][:], x[bass.ds((2 * n + i) * P, P), :]).then_inc(x_loaded[i], 16)

            sp.wait_ge(u_lo_done, 2 * TOK + 4)
            sp.dma_start(gate_w[0], sb_norm_w.broadcast_to([P, SB_WIDTH])).then_inc(gate_w_loaded, 16)
            sp.dma_start(gate_w[1], ml_norm_w.broadcast_to([P, ML_WIDTH])).then_inc(gate_w_loaded, 16)
            with nc.allow_non_contiguous_dma("the convolution's few weights"):
                for j in range(CONV_K):
                    sp.dma_start(cw[:, :, j], conv_w[j, :].rearrange("(c p) -> p c", p=P)).then_inc(conv_w_loaded, 16)
                sp.dma_start(cb[:], conv_b.rearrange("a (c p) -> p (a c)", p=P)).then_inc(conv_w_loaded, 16)

            for g in range(2):
                with sp.Fori(0, TG) as m:
                    for t in range(TG):
                        i = t % 2
                        rows, cols = bass.ds((g * TG + m) * P, P), bass.ds(t * GROUP, GROUP)
                        n = 2 * TG * g + 2 * m + (t // 2 + 1)
                        sp.wait_ge(staged_hi[i], n)
                        sp.dma_start(qk_hi[rows, cols], stage_hi[i][:, 0:GROUP].bitcast(F32))\
                            .then_inc(stored_hi[i], 16)
                        sp.wait_ge(evacuated[t], TG * g + m + 2)
                        sp.dma_start(qk_lo[rows, cols], stage_lo[i][:].bitcast(F32)).then_inc(stored_lo[i], 16)

            def store(ready, g, dram, row, row_step, col):
                with sp.Fori(0, TG) as m:
                    for t in range(BANKS):
                        sp.wait_ge(ready[t], g * TG + m + 2)
                        rows = bass.ds((row + m * row_step + (0 if dram is ml_t else t)) * P, P)
                        cols = slice(t * GROUP, (t + 1) * GROUP) if dram is ml_t else slice(col, col + GROUP)
                        sp.dma_start(dram[rows, cols], stage[t]).then_inc(stored[t], 16)

            store(evacuated, 2, proj_n, 0, BANKS, 0)
            store(staged, 0, proj_n, 0, BANKS, GROUP)
            for c in range(2):
                store(staged, 1 + c, ml_t, c * TG, 1, 0)
            store(evacuated, 6, proj_n, 0, BANKS, 2 * GROUP)
            store(evacuated, 7, proj_n, 0, BANKS, 3 * GROUP)
            store(staged, 3, proj_n, 0, BANKS, 4 * GROUP)
            for t in range(TG):
                sp.wait_ge(evacuated[t], GROUPS * TG + 2)
                sp.dma_start(gates_t[:, t * GROUP:(t + 1) * GROUP], stage[t][0:GATES, :]).then_inc(stored[t], 16)
            for t in range(BANKS):
                sp.wait_ge(stored[t], 16 * ((GROUPS - 2) * TG + 2))
            for i in range(2):
                sp.wait_ge(stored_hi[i], 16 * (4 * TG + 1))
                sp.wait_ge(stored_lo[i], 16 * (4 * TG + 1))

        @block.scalar
        def _(act):
            with act.Fori(0, TOK // 2) as n:
                for i in range(2):
                    act.wait_ge(x_loaded[i], 16 * (n + 1))
                    act.wait_ge(u_lo_done, 4 * n + 2 * (i + 1))
                    nc.scalar.activation(xn[i][:], x_in[i][:], ACT.Square, scale=D_MODEL ** -0.5,
                                         accum_out=mean_sq[:, i:i + 1])\
                        .then_inc(mean_sq_done, 1)
                for i in range(2):
                    for h in range(2):
                        act.wait_ge(xpose_done, 4 * n + (2 * i + h + 1))
                        nc.scalar.copy(uT_hi[:, 4 * h:4 * h + 4, bass.ds((2 * n + i) * P, P)],
                                       pt[h][:].rearrange("p (k t) -> p k t", k=4)).then_inc(u_hi_done, 1)

            def split(g):
                act.wait_ge(w_loaded, 16 * g + 16)
                for k in range(KT):
                    if k < KT - 1:
                        act.wait_ge(w_used, (KT - 1) * g + (k + 1))
                    else:
                        act.wait_ge(out_ready, 16 * g + 1)
                    nc.scalar.copy(w_hi[:, k, :], w_raw[:, k, :]).then_inc(w_hi_done, 1)

            def evacuate_hi(g, scale):
                with act.Fori(0, TG) as m:
                    for t in range(TG):
                        act.wait_ge(out_ready, 16 * g + 4 * m + (t + 2))
                        act.wait_ge(stored_hi[t % 2], 16 * (2 * TG * g + 2 * m + (t // 2 + 1)))
                        act.wait_ge(evacuated[(t + 2) % BANKS], TG * g + m + (1 if t < 2 else 2))
                        nc.scalar.mul(stage_hi[t % 2][:, 0:GROUP], po[t][:], scale).then_inc(staged_hi[t % 2], 1)

            def evacuate_copy(g):
                with act.Fori(0, TG) as m:
                    for t in (1, 3):
                        act.wait_ge(out_ready, 16 * g + 4 * m + (t + 2))
                        act.wait_ge(stored[t], 16 * ((g - 2) * TG + m + 1))
                        nc.scalar.copy(stage[t], po[t][:]).then_inc(evacuated[t], 1)

            def evacuate_gate(g, func):
                with act.Fori(0, TG) as m:
                    for t in range(BANKS):
                        act.wait_ge(out_ready, 16 * g + 4 * m + (t + 2))
                        act.wait_ge(stored[t], 16 * ((g - 2) * TG + m + 1))
                        nc.scalar.activation(stage[t], po[t][:], func).then_inc(evacuated[t], 1)

            def evacuate_conv(g):
                with act.Fori(0, TG) as m:
                    n = TG * TG * (g - 4) + TG * m
                    for t in range(BANKS + 1):
                        if t < BANKS:
                            act.wait_ge(out_ready, 16 * g + 4 * m + (t + 2))
                            act.wait_ge(halo_done, n + (t + 1))
                            nc.scalar.copy(conv_in[t % 2][:, HALO:], po[t][:]).then_inc(evacuated[t], 1)
                        if t > 0:
                            act.wait_ge(tap_done, CONV_K * n + CONV_K * (t + 2))
                            act.wait_ge(stored[t - 1], 16 * ((g - 2) * TG + m + 1))
                            nc.scalar.activation(stage[t - 1], conv_out[(t - 1) % 2], ACT.Silu)\
                                .then_inc(staged[t - 1], 1)

            act.wait_ge(wg_loaded, 16)
            nc.scalar.copy(wg_hi[:], wg_raw[:]).then_inc(wg_hi_done, 1)
            for g, scale in enumerate((-SB_SCALE, 1.0)):
                split(g)
                evacuate_hi(g, scale)
            split(2)
            evacuate_copy(2)
            split(3)
            evacuate_gate(3, ACT.Silu)
            for g in (4, 5):
                split(g)
                evacuate_conv(g)
            split(6)
            evacuate_copy(6)
            split(7)
            evacuate_gate(7, ACT.Sigmoid)
            split(8)
            evacuate_gate(8, ACT.Silu)
            for t in (1, 3):
                act.wait_ge(out_ready, 16 * GROUPS + (t + 2))
                act.wait_ge(stored[t], 16 * ((GROUPS - 2) * TG + 1))
                nc.scalar.copy(stage[t][0:GATES, :], po[t][0:GATES, :]).then_inc(evacuated[t], 1)

        @block.vector
        def _(dve):
            for s, count in ([(x_read, 1), (x_read, 1), (u_lo_done, 4), (w_used, KT - 1), (out_ready, 1),
                              (tap_done, 2 * CONV_K)] +
                             [(s, 1) for s in evacuated + staged] +
                             [(s, 16) for s in stored + stored_hi + stored_lo]):
                dve.sem_inc(s, count)
            dve.wait_ge(consts_loaded, 16)
            with dve.Fori(0, TOK // 2) as n:
                for i in range(2):
                    dve.wait_ge(rstd_done, 2 * n + (i + 1))
                    nc.vector.scalar_tensor_tensor(out=xn[i][:], in0=x_in[i][:], scalar=rstd[:, i:i + 1],
                                                   in1=pre_w[:], op0=ALU.mult, op1=ALU.mult).then_inc(x_read, 1)
                for i in range(2):
                    for h in range(2):
                        dve.wait_ge(u_hi_done, 4 * n + (2 * i + h + 1))
                        hi = uT_hi[:, 4 * h:4 * h + 4, bass.ds((2 * n + i) * P, P)].bitcast(F32)
                        nc.vector.tensor_tensor(uT_lo[:, 4 * h:4 * h + 4, bass.ds((2 * n + i) * P, P)],
                                                pt[h][:].rearrange("p (k t) -> p k t", k=4), hi,
                                                ALU.subtract).then_inc(u_lo_done, 1)

            def split(g):
                for k in range(KT):
                    dve.wait_ge(w_hi_done, KT * g + (k + 1))
                    nc.vector.tensor_tensor(w_lo[:, k, :], w_raw[:, k, :], w_hi[:, k, :].bitcast(F32),
                                            ALU.subtract).then_inc(w_lo_done, 1)

            def evacuate_lo(g, scale):
                with dve.Fori(0, TG) as m:
                    for t in range(TG):
                        n = 2 * TG * g + 2 * m + (t // 2 + 1)
                        dve.wait_ge(staged_hi[t % 2], n)
                        dve.wait_ge(stored_lo[t % 2], 16 * n)
                        nc.vector.scalar_tensor_tensor(out=stage_lo[t % 2][:], in0=po[t][:], scalar=scale,
                                                       in1=stage_hi[t % 2][:, 0:GROUP].bitcast(F32), op0=ALU.mult,
                                                       op1=ALU.subtract).then_inc(evacuated[t], 1)

            def evacuate_copy(g):
                with dve.Fori(0, TG) as m:
                    for t in (0, 2):
                        dve.wait_ge(out_ready, 16 * g + 4 * m + (t + 2))
                        dve.wait_ge(stored[t], 16 * ((g - 2) * TG + m + 1))
                        nc.vector.tensor_copy(stage[t], po[t][:]).then_inc(evacuated[t], 1)

            def weigh_gate(g, w):
                with dve.Fori(0, TG) as m:
                    for t in range(BANKS):
                        dve.wait_ge(evacuated[t], TG * g + m + 2)
                        nc.vector.tensor_tensor(stage[t], stage[t], w, ALU.mult).then_inc(staged[t], 1)

            def convolve(g):
                with dve.Fori(0, TG) as m:
                    n = TG * TG * (g - 4) + TG * m
                    c = (g - 4) * TG + m
                    w = [cw[:, bass.ds(c, 1), j] for j in range(CONV_K)]
                    for t in range(BANKS):
                        x_in_, out = conv_in[t % 2], conv_out[t % 2]
                        if t == 0:
                            dve.wait_ge(tap_done, CONV_K * n + CONV_K)
                            nc.vector.memset(x_in_[:, 0:HALO], 0.0).then_inc(halo_done, 1)
                        dve.wait_ge(evacuated[t], TG * g + m + 2)
                        dve.wait_ge(staged[(t + 2) % BANKS], TG * (g - 3) + m + (1 if t < 2 else 2))
                        nc.vector.tensor_scalar(out, x_in_[:, 0:GROUP], w[0], cb[:, bass.ds(c, 1)], ALU.mult, ALU.add)\
                            .then_inc(tap_done, 1)
                        if t < BANKS - 1:
                            dve.wait_ge(tap_done, CONV_K * n + CONV_K * (t + 2))
                            nc.vector.tensor_copy(conv_in[(t + 1) % 2][:, 0:HALO], x_in_[:, GROUP:])\
                                .then_inc(halo_done, 1)
                        for j in range(1, CONV_K):
                            dve.wait_ge(tap_done, CONV_K * n + (CONV_K * (t + 2) + j))
                            nc.vector.scalar_tensor_tensor(out=out, in0=x_in_[:, j:j + GROUP], scalar=w[j], in1=out,
                                                           op0=ALU.mult, op1=ALU.add).then_inc(tap_done, 1)

            dve.wait_ge(wg_hi_done, 1)
            nc.vector.tensor_tensor(wg_lo[:], wg_raw[:], wg_hi[:].bitcast(F32), ALU.subtract).then_inc(wg_lo_done, 1)
            for g, scale in enumerate((-SB_SCALE, 1.0)):
                split(g)
                evacuate_lo(g, scale)
            split(2)
            evacuate_copy(2)
            split(3)
            dve.wait_ge(gate_w_loaded, 32)
            weigh_gate(3, gate_w[0])
            dve.wait_ge(conv_w_loaded, 16 * (CONV_K + 1))
            for i in range(2):
                dve.wait_ge(stored_hi[i], 16 * (4 * TG + 1))
                dve.wait_ge(stored_lo[i], 16 * (4 * TG + 1))
            for g in (4, 5):
                split(g)
                convolve(g)
            split(6)
            evacuate_copy(6)
            split(7)
            split(8)
            weigh_gate(8, gate_w[1])
            for t in (0, 2):
                dve.wait_ge(out_ready, 16 * GROUPS + (t + 2))
                dve.wait_ge(stored[t], 16 * ((GROUPS - 2) * TG + 1))
                nc.vector.tensor_copy(stage[t][0:GATES, :], po[t][0:GATES, :]).then_inc(evacuated[t], 1)

        @block.tensor
        def _(pe):
            pe.wait_ge(ident_ready, 1)
            with pe.Fori(0, TOK // 2) as n:
                for i in range(2):
                    pe.wait_ge(x_read, 2 * n + (i + 3))
                    for h in range(2):
                        pe.wait_ge(u_lo_done, 4 * n + (2 * i + h + 3))
                        for k in range(4):
                            mm = pe.transpose(pt[h][:, k * P:(k + 1) * P],
                                              xn[i][:, (4 * h + k) * P:(4 * h + k + 1) * P], ident[:])
                        mm.then_inc(xpose_done, 1)
            pe.wait_ge(u_lo_done, 2 * TOK + 4)

            PARTS = ((1, 0), (0, 1), (0, 0))

            def group(g, transposed):
                for m in range(TG):
                    for t in range(BANKS):
                        pe.wait_ge(evacuated[t], TG * g + (m + 1))
                        first, final = (m, t) == (0, 0), (m, t) == (TG - 1, BANKS - 1)
                        for k in range(KT):
                            if first:
                                pe.wait_ge(w_lo_done, KT * g + (k + 1))
                            for n, (w_part, u_part) in enumerate(PARTS):
                                w, u = (w_hi, w_lo)[w_part], (uT_hi, uT_lo)[u_part]
                                if transposed:
                                    lhsT, rhs = w[:, k, m * P:(m + 1) * P], u[:, k, t * GROUP:(t + 1) * GROUP]
                                else:
                                    token = m * BANKS + t
                                    lhsT, rhs = u[:, k, token * P:(token + 1) * P], w[:, k, :]
                                mm = pe.matmul(po[t][:], lhsT, rhs, start=(k == 0 and n == 0),
                                               stop=(k == KT - 1 and n == 2))
                            if final and k < KT - 1:
                                mm.then_inc(w_used, 1)
                        mm.then_inc(out_ready, 1)

            with pe.Fori(0, 2) as a:
                with pe.Fori(0, 2) as b:
                    group(4 * a + b, True)
                with pe.Fori(0, 2) as b:
                    group(4 * a + b + 2, False)
            group(GROUPS - 1, False)
            pe.wait_ge(wg_lo_done, 1)
            for t in range(TG):
                pe.wait_ge(evacuated[t], TG * GROUPS + 1)
                for k in range(KT):
                    for n, (w_part, u_part) in enumerate(PARTS):
                        w, u = (wg_hi, wg_lo)[w_part], (uT_hi, uT_lo)[u_part]
                        mm = pe.matmul(po[t][0:GATES, :], w[:, k, :], u[:, k, t * GROUP:(t + 1) * GROUP],
                                       start=(k == 0 and n == 0), stop=(k == KT - 1 and n == 2))
                mm.then_inc(out_ready, 1)


def stick_breaking_attention(nc, qk_hi, qk_lo, proj_n, y_sb):
    with ExitStack() as ctx:
        def sb(name, shape, dt=F32):
            return ctx.enter_context(nc.sbuf_tensor(name, shape, dt))

        def sem(name):
            return ctx.enter_context(nc.semaphore(name))

        def psum(name, shape):
            return ctx.enter_context(nc.psum_tensor(name, shape, F32))

        PAIRS = SB_HEADS // 2
        BUFS, YS = 8, 4
        units = []
        for head in range(2):
            for i in range(TOK):
                for c in reversed(range(i // 4 + 1)):
                    keys = min(GROUP, (i + 1) * P - c * GROUP)
                    units.append((head, i, c * GROUP, keys, c == i // 4, c == 0))
        UNITS = len(units)
        assert UNITS % BUFS == 0 and UNITS % YS == 0
        firsts = [u for u in range(UNITS) if units[u][4]]
        E_LAG, SP_LAG, S_LAG, X_LAG, T_LAG, C_LAG, V_LAG, O_LAG = 1, 2, 3, 5, 6, 7, 8, 9

        def rank(u):
            return len(firsts) * (u // UNITS) + sum(f <= u % UNITS for f in firsts)

        def pipeline(fori, step):
            for n in range(O_LAG):
                step(0, n)
            with fori(0, PAIRS - 1) as it:
                for n in range(O_LAG, UNITS + O_LAG):
                    step(it, n)
            for n in range(O_LAG, UNITS + O_LAG):
                step(PAIRS - 1, n)

        def has(it, u):
            return u >= 0 and not (isinstance(it, int) and it == PAIRS - 1 and u >= UNITS)

        kst = [sb(f"kst{s}", [P, SEQ], F32R) for s in range(2)]
        qst_hi = [sb(f"qst_hi{s}", [P, SEQ], F32R) for s in range(2)]
        qst_lo = [sb(f"qst_lo{s}", [P, SEQ], F32R) for s in range(2)]
        v = sb("b_v", [P, TOK, SB_WIDTH])
        buf = [sb(f"b_buf{s}", [P, GROUP]) for s in range(BUFS)]
        aT = [sb(f"b_aT{s}", [P, GROUP]) for s in range(2)]
        ident = sb("b_ident", [P, P])
        lowest = sb("b_lowest", [P, P])
        y = [psum(f"b_y{s}", [P, GROUP]) for s in range(YS)]
        turned = [psum(f"b_turned{s}", [P, GROUP]) for s in range(2)]
        o = [psum(f"b_o{s}", [P, P]) for s in range(2)]

        zeroed = sem("b_zeroed")
        consts_ready = sem("b_consts_ready")
        qk_loaded = [sem(f"qk_loaded{s}") for s in range(2)]
        v_loaded = sem("b_v_loaded")
        y_done = sem("y_done")
        e_done = sem("e_done")
        ln_done = sem("ln_done")
        ln_masked = sem("ln_masked")
        sp_done = sem("sp_done")
        scan_done = sem("scan_done")
        log_done = sem("log_done")
        log_masked = sem("log_masked")
        a_done = sem("a_done")
        turned_done = sem("turned_done")
        aT_done = [sem(f"aT_done{s}") for s in range(2)]
        av_done = sem("av_done")
        o_read = sem("o_read")
        block = ctx.enter_context(nc.Block())

        @block.gpsimd
        def _(pool):
            nc.gpsimd.memset(ident[:], 0.0).then_inc(zeroed, 1)
            nc.gpsimd.memset(lowest[:], 0.0).then_inc(zeroed, 1)
            pool.wait_ge(zeroed, 2)
            nc.gpsimd.affine_select(out=ident[:], in_=ident[:], compare_op=ALU.not_equal, fill=1.0, base=0,
                                    pattern=[[-1, P]], channel_multiplier=1).then_inc(consts_ready, 1)
            nc.gpsimd.affine_select(out=lowest[:], in_=lowest[:], compare_op=ALU.is_gt, fill=-BIG, base=0,
                                    pattern=[[-1, P]], channel_multiplier=1).then_inc(consts_ready, 1)
            pool.wait_ge(consts_ready, 2)

            def step(it, n):
                u = n - X_LAG + 1
                if has(it, u) and units[u % UNITS][4]:
                    keys = units[u % UNITS][3]
                    own = buf[u % BUFS][:, keys - P:keys]
                    pool.wait_ge(log_done, it * UNITS + (u + 1 + YS))
                    nc.gpsimd.tensor_tensor(own, own, lowest[:], ALU.add).then_inc(log_masked, 1)
                n -= E_LAG
                if has(it, n) and units[n % UNITS][4]:
                    keys = units[n % UNITS][3]
                    own = buf[n % BUFS][:, keys - P:keys]
                    pool.wait_ge(ln_done, it * UNITS + (n + 1))
                    nc.gpsimd.tensor_tensor(own, own, lowest[:], ALU.add).then_inc(ln_masked, 1)

            pipeline(pool.Fori, step)

        @block.sync
        def _(sp):
            def load_head(s, head):
                q, k = bass.ds(head * SB_DIM, SB_DIM), bass.ds(head * SB_DIM + SB_WIDTH, SB_DIM)
                for tile, top, bottom in ((kst, qk_hi[k, :], qk_lo[k, :]), (qst_hi, qk_hi[q, :], qk_hi[q, :]),
                                          (qst_lo, qk_lo[q, :], qk_lo[q, :])):
                    sp.dma_start(tile[s][0:64, :].bitcast(F32), top).then_inc(qk_loaded[s], 16)
                    sp.dma_start(tile[s][64:128, :].bitcast(F32), bottom).then_inc(qk_loaded[s], 16)

            load_head(0, 0)
            sp.dma_start(v[:], proj_n[:, 0:SB_WIDTH].rearrange("(j p) n -> p j n", p=P)).then_inc(v_loaded, 16)
            load_head(1, 1)
            with sp.Fori(1, PAIRS) as it:
                for s in range(2):
                    sp.wait_ge(y_done, (it - 1) * UNITS + UNITS // 2 * (s + 1))
                    load_head(s, 2 * it + s)

        @block.tensor
        def _(pe):
            def turn(it, u):
                keys = units[u % UNITS][3]
                pe.wait_ge(a_done, it * UNITS + (u + 1))
                pe.wait_ge(aT_done[u % 2], it * (UNITS // 2) + (u // 2 + 1))
                for j in range(keys // P):
                    mm = pe.transpose(turned[u % 2][:, j * P:(j + 1) * P], buf[u % BUFS][:, j * P:(j + 1) * P],
                                      ident[:])
                mm.then_inc(turned_done, 1)

            def score(it, u):
                head, i, key0, keys, first, last = units[u % UNITS]
                if u % UNITS in (0, UNITS // 2):
                    pe.wait_ge(qk_loaded[head], 96 * it + (96 * (u // UNITS) + 96))
                pe.wait_ge(log_done, it * UNITS + (u + 1))
                q = slice(i * P, (i + 1) * P)
                out, k = y[u % YS][:, 0:keys], kst[head][:, key0:key0 + keys]
                pe.matmul(out, qst_lo[head][:, q], k, start=True, stop=False)
                pe.matmul(out, qst_hi[head][:, q], k, start=False, stop=True).then_inc(y_done, 1)

            def times_v(it, u):
                head, i, key0, keys, first, last = units[u % UNITS]
                if u == 0:
                    pe.wait_ge(v_loaded, 16)
                pe.wait_ge(aT_done[u % 2], it * (UNITS // 2) + (u // 2 + 2))
                if first:
                    pe.wait_ge(o_read, it * (2 * TOK) + (2 * TOK * (u // UNITS) + head * TOK + i + 1))
                for j in range(keys // P):
                    mm = pe.matmul(o[i % 2][:], aT[u % 2][:, j * P:(j + 1) * P],
                                   v[:, key0 // P + j, bass.ds((it + u // UNITS) * P, P)],
                                   start=(first and j == 0), stop=(last and j == keys // P - 1))
                mm.then_inc(av_done, 1)

            def step(it, n):
                if has(it, n):
                    score(it, n)
                if has(it, n - T_LAG):
                    turn(it, n - T_LAG)
                if has(it, n - V_LAG):
                    times_v(it, n - V_LAG)

            pe.wait_ge(consts_ready, 2)
            pipeline(pe.Fori, step)

        def copy_turned(engine, copy, it, u):
            keys = units[u % UNITS][3]
            engine.wait_ge(turned_done, it * UNITS + (u + 1 + BUFS))
            engine.wait_ge(av_done, it * UNITS + (u + 1))
            copy(aT[u % 2][:, 0:keys], turned[u % 2][:, 0:keys]).then_inc(aT_done[u % 2], 1)

        @block.scalar
        def _(act):
            def step(it, n):
                e, x, c = n - E_LAG, n - X_LAG, n - C_LAG
                b = buf[e % BUFS][:, 0:units[e % UNITS][3]]
                if has(it, e):
                    act.wait_ge(y_done, it * UNITS + (e + 1))
                    act.wait_ge(turned_done, it * UNITS + (e + 1))
                    nc.scalar.activation(b, y[e % YS][:, 0:units[e % UNITS][3]], ACT.Exp).then_inc(e_done, 1)
                if has(it, x):
                    a = buf[x % BUFS][:, 0:units[x % UNITS][3]]
                    if units[x % UNITS][4]:
                        act.wait_ge(log_masked, it * len(firsts) + rank(x))
                    else:
                        act.wait_ge(log_done, it * UNITS + (x + 1 + YS))
                    nc.scalar.activation(a, a, ACT.Exp).then_inc(a_done, 1)
                if has(it, e):
                    act.wait_ge(e_done, it * UNITS + (e + 1))
                    nc.scalar.activation(b, b, ACT.Ln, bias=1.0).then_inc(ln_done, 1)
                if has(it, c) and c % 2 == 0:
                    copy_turned(act, nc.scalar.copy, it, c)

            act.preload_act_table_set("natural_log_exp_and_others")
            pipeline(act.Fori, step)

        @block.vector
        def _(dve):
            for s, count in ((log_done, YS - 1), (turned_done, BUFS), (aT_done[0], 1), (aT_done[1], 1), (av_done, 2),
                             (o_read, 2)):
                dve.sem_inc(s, count)

            def softplus(it, u):
                keys, first = units[u % UNITS][3:5]
                b = buf[u % BUFS][:, 0:keys]
                if first:
                    dve.wait_ge(ln_masked, it * len(firsts) + rank(u))
                else:
                    dve.wait_ge(ln_done, it * UNITS + (u + 1))
                nc.vector.scalar_tensor_tensor(out=b, in0=b, scalar=LN_MAX, in1=y[u % YS][:, 0:keys], op0=ALU.min,
                                               op1=ALU.max).then_inc(sp_done, 1)

            def scan(it, u):
                keys = units[u % UNITS][3]
                b = buf[u % BUFS]
                down = b[:, 0:keys - 1][:, ::-1]
                dve.wait_ge(log_done, it * UNITS + (u + YS))
                nc.vector.tensor_tensor_scan(down, y[u % YS][:, 1:keys][:, ::-1], down,
                                             b[:, keys - 1:keys], ALU.add, ALU.subtract)\
                    .then_inc(log_done if not has(it, u + 1) else scan_done, 1)

            def start(it, u):
                keys, first = units[u % UNITS][3:5]
                last_key, before = buf[u % BUFS][:, keys - 1:keys], (u - 1) % BUFS
                dve.wait_ge(sp_done, it * UNITS + (u + 1))
                until(dve, scan_done, it * UNITS + u)
                if first:
                    nc.vector.tensor_scalar_mul(last_key, last_key, -1.0).then_inc(log_done, 1)
                else:
                    nc.vector.scalar_tensor_tensor(out=last_key, in0=y[(u - 1) % YS][:, 0:1], scalar=buf[before][:, 0:1],
                                                   in1=last_key, op0=ALU.add, op1=ALU.subtract).then_inc(log_done, 1)

            def step(it, n):
                if has(it, n - SP_LAG):
                    softplus(it, n - SP_LAG)
                if has(it, n - S_LAG):
                    scan(it, n - S_LAG)
                if has(it, n - C_LAG) and (n - C_LAG) % 2 == 1:
                    copy_turned(dve, nc.vector.tensor_copy, it, n - C_LAG)
                if has(it, n - SP_LAG):
                    start(it, n - SP_LAG)
                u = n - O_LAG
                if has(it, u) and units[u % UNITS][5]:
                    head, i = units[u % UNITS][0:2]
                    dve.wait_ge(av_done, it * UNITS + (u + 3))
                    nc.vector.tensor_copy(y_sb[:, i, bass.ds((it + u // UNITS) * P + head * SB_DIM, SB_DIM)],
                                          o[i % 2][:, head * SB_DIM:(head + 1) * SB_DIM]).then_inc(o_read, 1)

            pipeline(dve.Fori, step)


def split_weights(nc, tiles, raw, hi, lo, loaded, hi_done, lo_done):
    def load(sp):
        for k, rows in enumerate(tiles):
            until(sp, lo_done, k - 1)
            sp.dma_start(raw[k % 2][:], rows).then_inc(loaded[k % 2], 16)

    def high(act):
        for k in range(len(tiles)):
            act.wait_ge(loaded[k % 2], 16 * (k // 2 + 1))
            nc.scalar.copy(hi[:, k, :], raw[k % 2][:]).then_inc(hi_done, 1)

    def low(dve):
        for k in range(len(tiles)):
            dve.wait_ge(hi_done, k + 1)
            nc.vector.tensor_tensor(lo[:, k, :], raw[k % 2][:], hi[:, k, :].bitcast(F32), ALU.subtract)\
                .then_inc(lo_done, 1)

    return load, high, low


def mlstm_and_output_projection(nc, x, ml_i_bias, ml_f_bias, w_out, post_norm_w, ml_t, proj_n, gates_t, y_sb,
                                residual):
    with ExitStack() as ctx:
        def sb(name, shape, dt=F32):
            return ctx.enter_context(nc.sbuf_tensor(name, shape, dt))

        def sem(name):
            return ctx.enter_context(nc.semaphore(name))

        def psum(name, shape):
            return ctx.enter_context(nc.psum_tensor(name, shape, F32))

        H, DV = ML_HEADS, ML_DIM + 1
        A, CARRY, FLOOR, KEY = range(4)

        w_raw = [sb(f"c_w_raw{s}", [P, D_MODEL]) for s in range(2)]
        w_hi = sb("c_w_hi", [P, KT, D_MODEL], F32R)
        w_lo = sb("c_w_lo", [P, KT, D_MODEL], F32R)
        post_w = sb("c_post_w", [P, D_MODEL])
        ident = sb("c_ident", [P, P])
        minus_half = sb("c_minus_half", [P, SB_HEADS + H])
        eps = sb("c_eps", [P, SB_HEADS + H])
        ident_b = sb("c_ident_b", [P, P], BF16)
        hidden = sb("c_hidden", [P, 2, P], BF16)
        sel = sb("c_sel", [H, H, P])
        neg_m = sb("c_neg_m", [H, SEQ])
        cols = sb("c_cols", [P, TOK, 4, H])
        decay = sb("c_decay", [P, H, TOK])
        state = sb("c_state", [P, H, DV + 3])
        vx = [sb(f"c_vx{s}", [P, H, DV + 3]) for s in range(2)]

        scores = psum("c_scores", [P, 2, 2, P])
        k_turned = psum("c_k_turned", [P, 2, P])
        inter = psum("c_inter", [P, 2, 256])
        intra = psum("c_intra", [P, 2, 256])
        update = psum("c_update", [P, 2, 256])
        turned = psum("c_turned", [P, GROUP])
        out = [psum(f"c_out{n}", [P, GROUP]) for n in range(2)]

        w_loaded = [sem(f"c_w_loaded{s}") for s in range(2)]
        w_hi_done = sem("c_w_hi_done")
        w_lo_done = sem("c_w_lo_done")
        post_w_loaded = sem("c_post_w_loaded")
        zeroed = sem("c_zeroed")
        consts_ready = sem("c_consts_ready")
        load_w, split_hi, split_lo = split_weights(nc, [w_out[k * P:(k + 1) * P, :] for k in range(KT)], w_raw,
                                                   w_hi, w_lo, w_loaded, w_hi_done, w_lo_done)

        with ExitStack() as rows_ctx:
            def row(name, shape):
                return rows_ctx.enter_context(nc.sbuf_tensor(name, shape, F32))

            bias = row("g_bias", [H, 2])
            i_row = row("g_i", [H, SEQ])
            f_row = row("g_f", [H, SEQ])
            sp_row = row("g_sp", [H, SEQ])
            neg_b = row("g_neg_b", [H, SEQ])
            reset = row("g_reset", [H, SEQ])
            shift = row("g_shift", [H, SEQ])
            m_row = row("g_m", [H, SEQ])
            m_before = row("g_m_before", [H, TOK])
            chunk_decay = row("g_chunk_decay", [H, TOK])
            stack = row("g_stack", [P, SEQ])

            g_loaded = sem("g_loaded")
            g_dve = sem("g_dve")
            g_act = sem("g_act")
            g_turned = sem("g_turned")
            g_copied = sem("g_copied")
            g_decay = sem("g_decay")

            def chunked(t):
                return t[:].rearrange("h (c t) -> h c t", t=P)

            def ends(t):
                return chunked(t)[:, :, P - 1]

            block = rows_ctx.enter_context(nc.Block())

            @block.sync
            def _(sp):
                sp.dma_start(i_row[:], gates_t[0:H, :]).then_inc(g_loaded, 16)
                sp.dma_start(f_row[:], gates_t[H:2 * H, :]).then_inc(g_loaded, 16)
                with nc.allow_non_contiguous_dma("eight biases"):
                    sp.dma_start(bias[:, 0:1], ml_i_bias.rearrange("a h -> h a")).then_inc(g_loaded, 16)
                    sp.dma_start(bias[:, 1:2], ml_f_bias.rearrange("a h -> h a")).then_inc(g_loaded, 16)
                sp.dma_start(post_w[:], post_norm_w.broadcast_to([P, D_MODEL])).then_inc(post_w_loaded, 16)
                load_w(sp)
                sp.wait_ge(post_w_loaded, 16)

            @block.gpsimd
            def _(pool):
                nc.gpsimd.memset(reset[:], 1.0).then_inc(zeroed, 1)
                for t in (shift, m_before, stack, ident, ident_b, hidden, sel, state):
                    nc.gpsimd.memset(t[:], 0.0).then_inc(zeroed, 1)
                nc.gpsimd.memset(minus_half[:], -0.5).then_inc(consts_ready, 1)
                nc.gpsimd.memset(eps[:], EPS).then_inc(consts_ready, 1)
                for s in range(2):
                    nc.gpsimd.memset(vx[s][:, :, ML_DIM:DV], 1.0).then_inc(consts_ready, 1)
                pool.wait_ge(zeroed, 9)
                nc.gpsimd.memset(chunked(reset)[:, :, 0:1], 0.0).then_inc(consts_ready, 1)
                for t in (ident, ident_b):
                    nc.gpsimd.affine_select(out=t[:], in_=t[:], compare_op=ALU.not_equal, fill=1.0, base=0,
                                            pattern=[[-1, P]], channel_multiplier=1).then_inc(consts_ready, 1)
                nc.gpsimd.affine_select(out=hidden[:], in_=hidden[:], compare_op=ALU.is_ge, fill=MASKED, base=0,
                                        pattern=[[0, 2], [1, P]], channel_multiplier=-1).then_inc(consts_ready, 1)
                nc.gpsimd.affine_select(out=sel[:], in_=sel[:], compare_op=ALU.not_equal, fill=1.0, base=0,
                                        pattern=[[-1, H], [0, P]], channel_multiplier=1).then_inc(consts_ready, 1)

            @block.scalar
            def _(act):
                act.preload_act_table_set("natural_log_exp_and_others")
                act.wait_ge(g_dve, 1)
                nc.scalar.activation(sp_row[:], f_row[:], ACT.Exp).then_inc(g_act, 1)
                act.wait_ge(g_act, 1)
                nc.scalar.activation(sp_row[:], sp_row[:], ACT.Ln, bias=1.0).then_inc(g_act, 1)
                act.wait_ge(g_dve, 9)
                nc.scalar.activation(stack[32:32 + H, :], i_row[:], ACT.Exp).then_inc(g_act, 1)
                act.wait_ge(g_dve, 10)
                nc.scalar.activation(stack[64:64 + H, :], reset[:], ACT.Exp).then_inc(g_act, 1)
                act.wait_ge(g_dve, 11)
                nc.scalar.activation(shift[:], shift[:], ACT.Exp).then_inc(g_act, 1)
                act.wait_ge(g_dve, 12)
                nc.scalar.activation(chunk_decay[:], chunk_decay[:], ACT.Exp).then_inc(g_act, 1)
                split_hi(act)

            @block.vector
            def _(dve):
                dve.wait_ge(g_loaded, 64)
                dve.wait_ge(consts_ready, 9)
                nc.vector.tensor_scalar(f_row[:], f_row[:], bias[:, 1:2], -1.0, ALU.add, ALU.mult).then_inc(g_dve, 1)
                dve.wait_ge(g_act, 2)
                nc.vector.scalar_tensor_tensor(out=sp_row[:], in0=sp_row[:], scalar=LN_MAX, in1=f_row[:],
                                               op0=ALU.min, op1=ALU.max).then_inc(g_dve, 1)
                dve.wait_ge(g_dve, 2)
                nc.vector.tensor_tensor_scan(neg_b[:], reset[:], sp_row[:], 0.0, ALU.mult, ALU.add).then_inc(g_dve, 1)
                dve.wait_ge(g_dve, 3)
                nc.vector.scalar_tensor_tensor(out=stack[0:H, :], in0=i_row[:], scalar=bias[:, 0:1], in1=neg_b[:],
                                               op0=ALU.add, op1=ALU.add).then_inc(g_dve, 1)
                nc.vector.tensor_scalar_mul(chunked(shift)[:, 1:, 0], ends(neg_b)[:, :TOK - 1], -1.0).then_inc(g_dve, 1)
                dve.wait_ge(g_dve, 5)
                nc.vector.tensor_tensor_scan(m_row[:], shift[:], stack[0:H, :], 0.0, ALU.add, ALU.max)\
                    .then_inc(g_dve, 1)
                dve.wait_ge(g_dve, 6)
                nc.vector.tensor_tensor(m_before[:, 1:], ends(m_row)[:, :TOK - 1], ends(neg_b)[:, :TOK - 1],
                                        ALU.subtract).then_inc(g_dve, 1)
                nc.vector.tensor_scalar_mul(neg_m[:], m_row[:], -1.0).then_inc(g_dve, 1)
                dve.wait_ge(g_dve, 8)
                nc.vector.tensor_tensor(chunked(i_row), m_before[:].unsqueeze(2).broadcast_to([H, TOK, P]),
                                        chunked(m_row), ALU.subtract).then_inc(g_dve, 1)
                nc.vector.tensor_tensor(reset[:], neg_b[:], m_row[:], ALU.subtract).then_inc(g_dve, 1)
                nc.vector.tensor_tensor(chunked(shift), stack[0:H, :].rearrange("h (c t) -> h c t", t=P),
                                        chunked(m_row)[:, :, P - 1:P].broadcast_to([H, TOK, P]),
                                        ALU.subtract).then_inc(g_dve, 1)
                nc.vector.tensor_tensor(chunk_decay[:], m_before[:], ends(m_row), ALU.subtract).then_inc(g_dve, 1)
                dve.wait_ge(g_act, 5)
                nc.vector.tensor_scalar_mul(stack[96:96 + H, :], shift[:], ML_SCALE).then_inc(g_dve, 1)
                split_lo(dve)
                for n in range(TOK // 4):
                    dve.wait_ge(g_turned, n + 1)
                    nc.vector.tensor_copy(cols[:, 4 * n:4 * n + 4, :, :],
                                          (turned, out[0])[n % 2][:].rearrange("p (c q x) -> p c q x", c=4, q=4)
                                          [:, :, :, 0:H]).then_inc(g_copied, 1)
                dve.wait_ge(g_decay, 1)
                nc.vector.tensor_copy(decay[:], out[1][:, 0:H * TOK].rearrange("p (h c) -> p h c", h=H))\
                    .then_inc(g_copied, 1)

            @block.tensor
            def _(pe):
                pe.wait_ge(g_act, 6)
                pe.wait_ge(g_dve, 13)
                for n in range(TOK // 4):
                    until(pe, g_copied, n - 1)
                    for c in range(4):
                        mm = pe.transpose((turned, out[0])[n % 2][:, c * P:(c + 1) * P],
                                          stack[:, (4 * n + c) * P:(4 * n + c + 1) * P], ident[:])
                    mm.then_inc(g_turned, 1)
                for h in range(H):
                    mm = pe.matmul(out[1][:, h * TOK:(h + 1) * TOK], sel[:, h, :], chunk_decay[:],
                                   start=True, stop=True)
                mm.then_inc(g_decay, 1)

        qk = [sb(f"c_qk{s}", [P, 2 * H, P]) for s in range(2)]
        gates = [sb(f"c_gates{s}", [P, 3 * GROUP]) for s in range(2)]
        x_in = [sb(f"c_x{s}", [P, D_MODEL]) for s in range(2)]
        h_out = [sb(f"c_h{s}", [P, D_MODEL]) for s in range(2)]
        wt = [sb(f"c_wt{s}", [P, 2, P]) for s in range(2)]
        kw = [sb(f"c_kw{s}", [P, 2, P]) for s in range(2)]
        carried = [sb(f"c_carried{s}", [P, 2, DV + 3]) for s in range(2)]
        num = sb("c_num", [P, H, DV + 3])
        den = sb("c_den", [P, 3, H])
        y = [sb(f"c_y{s}", [P, D_MODEL]) for s in range(2)]
        squares = sb("c_squares", [P, D_MODEL])
        ss = sb("c_ss", [P, SB_HEADS + H])
        rstd = sb("c_rstd", [P, SB_HEADS + H])
        post_ss = sb("c_post_ss", [P, 2])
        post_rstd = sb("c_post_rstd", [P, 2])
        junk = sb("c_junk", [P, 2, GROUP])
        yT_hi = sb("c_yT_hi", [P, KT, P], F32R)
        yT_lo = sb("c_yT_lo", [P, KT, P], F32R)

        def per_slot(name):
            return [sem(f"{name}{s}") for s in range(2)]

        qk_loaded, v_loaded, gates_loaded, x_loaded = map(per_slot, ("c_qk_loaded", "c_v_loaded", "c_gates_loaded",
                                                                      "c_x_loaded"))
        h_stored = per_slot("c_h_stored")
        scores_done = sem("scores_done")
        k_turned_done = sem("k_turned_done")
        weights_done = sem("weights_done")
        p_done = sem("p_done")
        kw_done = sem("kw_done")
        inter_done = sem("inter_done")
        carried_done = sem("carried_done")
        intra_done = sem("intra_done")
        num_done = sem("num_done")
        update_done = sem("update_done")
        state_done = sem("state_done")
        den_done = sem("den_done")
        ml_y_done = sem("ml_y_done")
        squares_done = sem("squares_done")
        ss_done = sem("ss_done")
        mean_done = sem("c_mean_done")
        rstd_done = sem("c_rstd_done")
        scaled_done = sem("scaled_done")
        sb_y_done = sem("sb_y_done")
        ml_gated = sem("ml_gated")
        y_turned = sem("y_turned")
        yT_hi_done = sem("yT_hi_done")
        yT_lo_done = sem("yT_lo_done")
        out_done = sem("c_out_done")
        post_ss_done = sem("post_ss_done")
        post_mean_done = sem("post_mean_done")
        post_rstd_done = sem("post_rstd_done")
        normed_done = sem("normed_done")
        h_done = sem("h_done")

        block = ctx.enter_context(nc.Block())
        LAG = 2

        FIRST = 2 * LAG

        def steps(fori, step):
            for c in range(FIRST):
                step(c, c % 2, True, c >= LAG)
            with fori(0, (TOK - FIRST) // 2) as n:
                for s in range(2):
                    step(2 * n + (FIRST + s), s, True, True)
            for c in range(TOK, TOK + LAG):
                step(c, c % 2, False, True)

        def tile(c):
            return bass.ds(c * P, P) if not isinstance(c, int) else slice(c * P, (c + 1) * P)

        def at(c):
            return bass.ds(c, 1) if not isinstance(c, int) else slice(c, c + 1)

        @block.sync
        def _(sp):
            def step(c, s, mlstm, dense):
                if mlstm:
                    until(sp, update_done, 2 * c - 2)
                    src = ml_t[:, tile(c)].rearrange("(j p) t -> p j t", p=P)
                    sp.dma_start(qk[s][:], src).then_inc(qk_loaded[s], 16)
                    sp.dma_start(vx[s][:, :, 0:ML_DIM],
                                 proj_n[tile(c), 2 * GROUP:3 * GROUP].rearrange("p (h d) -> p h d", h=H))\
                        .then_inc(v_loaded[s], 16)
                    until(sp, sb_y_done, c - 1)
                    until(sp, ml_gated, c - 1)
                    sp.dma_start(gates[s][:, 0:GROUP], proj_n[tile(c), GROUP:2 * GROUP]).then_inc(gates_loaded[s], 16)
                    sp.dma_start(gates[s][:, GROUP:], proj_n[tile(c), 3 * GROUP:5 * GROUP])\
                        .then_inc(gates_loaded[s], 16)
                if dense:
                    d = c - LAG
                    until(sp, h_done, d - 1)
                    sp.dma_start(x_in[s][:], x[tile(d), :]).then_inc(x_loaded[s], 16)
                    if not isinstance(c, int) or c > LAG:
                        store(d - 1, 1 - s)

            def store(d, s):
                until(sp, h_done, d + 1)
                sp.dma_start(residual[tile(d), :], h_out[s][:]).then_inc(h_stored[s], 16)

            steps(sp.Fori, step)
            store(TOK - 1, 1)
            for s in range(2):
                sp.wait_ge(h_stored[s], 16 * (TOK // 2))

        @block.tensor
        def _(pe):
            def score(u, c, s, p):
                q, k = qk[s][:, 2 * p:2 * p + 2, :], qk[s][:, H + 2 * p:H + 2 * p + 2, :]
                if p == 0:
                    pe.wait_ge(qk_loaded[s], 16 * (c // 2) + 16 if isinstance(c, int) else (c - s) * 8 + 16)
                until(pe, p_done, u)
                for i in range(2):
                    pe.matmul(scores[:, 0, i, :], k[:, i, :], q[:, i, :], start=True, stop=True)
                pe.matmul(scores[:, 1, :, :], ident_b[:], hidden[:], start=True, stop=False)
                for i in range(2):
                    mm = pe.matmul(scores[:, 1, i, :], sel[:, 2 * p + i, :], neg_m[:, tile(c)], start=False, stop=(i == 1))
                mm.then_inc(scores_done, 1)
                until(pe, kw_done, u)
                for i in range(2):
                    mm = pe.transpose(k_turned[:, i, :], k[:, i, :], ident[:])
                mm.then_inc(k_turned_done, 1)

            def combine(u, c, s, p):
                if p == 0:
                    pe.wait_ge(v_loaded[s], 16 * (c // 2) + 16 if isinstance(c, int) else (c - s) * 8 + 16)
                until(pe, state_done, u - 1)
                until(pe, carried_done, u)
                for i in range(2):
                    mm = pe.matmul(inter[:, i, 0:DV], qk[s][:, 2 * p + i, :], state[:, 2 * p + i, 0:DV],
                                   start=True, stop=True)
                mm.then_inc(inter_done, 1)
                until(pe, p_done, u + 1)
                until(pe, num_done, u)
                for i in range(2):
                    mm = pe.matmul(intra[:, i, 0:DV], wt[p][:, i, :], vx[s][:, 2 * p + i, 0:DV], start=True, stop=True)
                mm.then_inc(intra_done, 1)
                until(pe, kw_done, u + 1)
                until(pe, state_done, u)
                for i in range(2):
                    mm = pe.matmul(update[:, i, 0:DV], kw[p][:, i, :], vx[s][:, 2 * p + i, 0:DV],
                                   start=True, stop=True)
                mm.then_inc(update_done, 1)

            def turn(d, s):
                until(pe, sb_y_done, d + 1)
                until(pe, ml_gated, d + 1)
                for h in range(2):
                    until(pe, yT_lo_done, 2 * d + h)
                    for k in range(4):
                        mm = pe.transpose(turned[:, k * P:(k + 1) * P], y[s][:, (4 * h + k) * P:(4 * h + k + 1) * P],
                                          ident[:])
                    mm.then_inc(y_turned, 1)

            def project(d, n):
                if n == 0:
                    until(pe, yT_lo_done, 2 * d + 2)
                until(pe, normed_done, 2 * d - 1 + n)
                for k in range(KT):
                    for j, (yT, w) in enumerate(((yT_lo, w_hi), (yT_hi, w_lo), (yT_hi, w_hi))):
                        mm = pe.matmul(out[n][:], yT[:, k, :], w[:, k, n * GROUP:(n + 1) * GROUP],
                                       start=(k == 0 and j == 0), stop=(k == KT - 1 and j == 2))
                mm.then_inc(out_done, 1)

            def step(c, s, mlstm, dense):
                if mlstm:
                    score(2 * c, c, s, 0)
                if dense:
                    turn(c - LAG, s)
                    project(c - LAG, 0)
                if mlstm:
                    score(2 * c + 1, c, s, 1)
                    combine(2 * c, c, s, 0)
                if dense:
                    project(c - LAG, 1)
                if mlstm:
                    combine(2 * c + 1, c, s, 1)

            steps(pe.Fori, step)

        @block.scalar
        def _(act):
            act.preload_act_table_set("natural_log_exp_and_others")

            def weigh(u, c, p):
                until(act, scores_done, u + 1)
                until(act, intra_done, u - 1)
                for i in range(2):
                    a = nc.scalar.activation(wt[p][:, i, :], scores[:, 1, i, :], ACT.Exp,
                                             bias=cols[:, at(c), A, 2 * p + i])
                a.then_inc(weights_done, 1)
                until(act, k_turned_done, u + 1)
                until(act, update_done, u - 1)
                for i in range(2):
                    a = nc.scalar.activation(kw[p][:, i, :], k_turned[:, i, :], ACT.Copy,
                                             scale=cols[:, at(c), KEY, 2 * p + i])
                a.then_inc(kw_done, 1)

            def carry(u, c, p):
                until(act, inter_done, u + 1)
                until(act, num_done, u - 1)
                for i in range(2):
                    a = nc.scalar.activation(carried[p][:, i, 0:DV], inter[:, i, 0:DV], ACT.Copy,
                                             scale=cols[:, at(c), CARRY, 2 * p + i])
                a.then_inc(carried_done, 1)

            def high(d):
                for h in range(2):
                    until(act, y_turned, 2 * d + h + 1)
                    until(act, out_done, 2 * d)
                    nc.scalar.copy(yT_hi[:, 4 * h:4 * h + 4, :], turned[:].rearrange("p (k t) -> p k t", k=4))\
                        .then_inc(yT_hi_done, 1)

            def square(b):
                until(act, ss_done, 2 * b)
                nc.scalar.activation(squares[:, 0:SB_WIDTH], y_sb[:, at(b), :].rearrange("p a n -> p (a n)"),
                                     ACT.Square, scale=SB_DIM ** -0.5).then_inc(squares_done, 1)
                until(act, ml_y_done, b + 1)
                nc.scalar.activation(squares[:, SB_WIDTH:], num[:, :, 0:ML_DIM], ACT.Square, scale=ML_DIM ** -0.5)\
                    .then_inc(squares_done, 1)

            def square_out(d, n):
                until(act, out_done, 2 * d + n + 1)
                until(act, post_mean_done, 2 * d)
                nc.scalar.activation(junk[:, n, :], out[n][:], ACT.Square, scale=D_MODEL ** -0.5,
                                     accum_out=post_ss[:, n:n + 1])\
                    .then_inc(post_ss_done, 1)

            def step(c, s, mlstm, dense):
                if mlstm:
                    weigh(2 * c, c, 0)
                if dense:
                    high(c - LAG)
                if not (isinstance(c, int) and not 1 <= c <= TOK):
                    square(c - 1)
                if mlstm:
                    weigh(2 * c + 1, c, 1)
                    carry(2 * c, c, 0)
                if dense:
                    square_out(c - LAG, 0)
                    square_out(c - LAG, 1)
                if mlstm:
                    carry(2 * c + 1, c, 1)

            steps(act.Fori, step)

        @block.gpsimd
        def _(pool):
            def head_norms(b, s):
                until(pool, ss_done, 2 * b + 2)
                until(pool, ml_gated, b)
                nc.gpsimd.tensor_tensor(ss[:], ss[:], eps[:], ALU.add).then_inc(mean_done, 1)
                until(pool, mean_done, b + 1)
                nc.gpsimd.tensor_tensor(rstd[:], ss[:], minus_half[:], ALU.pow).then_inc(rstd_done, 1)
                until(pool, scaled_done, b + 1)
                nc.gpsimd.tensor_tensor(y[s][:, 0:SB_WIDTH], y[s][:, 0:SB_WIDTH], gates[s][:, 0:GROUP], ALU.mult)\
                    .then_inc(sb_y_done, 1)

            def post_norm(d):
                until(pool, post_ss_done, 2 * d + 2)
                until(pool, normed_done, 2 * d)
                nc.gpsimd.tensor_tensor(post_rstd[:, 0:1], post_ss[:, 0:1], post_ss[:, 1:2], ALU.add)\
                    .then_inc(post_mean_done, 1)
                until(pool, post_mean_done, 2 * d + 1)
                nc.gpsimd.tensor_tensor(post_rstd[:, 0:1], post_rstd[:, 0:1], eps[:, 0:1], ALU.add)\
                    .then_inc(post_mean_done, 1)
                until(pool, post_mean_done, 2 * d + 2)
                nc.gpsimd.tensor_tensor(post_rstd[:, 1:2], post_rstd[:, 0:1], minus_half[:, 0:1], ALU.pow)\
                    .then_inc(post_rstd_done, 1)

            def add_residual(d, s):
                until(pool, normed_done, 2 * d + 2)
                pool.wait_ge(x_loaded[s], 16 * (d // 2) + 16 if isinstance(d, int) else (d - s) * 8 + 16)
                nc.gpsimd.tensor_tensor(h_out[s][:], h_out[s][:], x_in[s][:], ALU.add).then_inc(h_done, 1)

            def step(c, s, mlstm, dense):
                if not (isinstance(c, int) and not 1 <= c <= TOK):
                    head_norms(c - 1, 1 - s)
                if dense:
                    post_norm(c - LAG)
                    add_residual(c - LAG, s)

            steps(pool.Fori, step)

        @block.vector
        def _(dve):
            def weights_times_scores(u, p):
                until(dve, weights_done, u + 1)
                nc.vector.scalar_tensor_tensor(out=wt[p][:], in0=scores[:, 0, :, :], scalar=ML_SCALE, in1=wt[p][:],
                                               op0=ALU.mult, op1=ALU.mult).then_inc(p_done, 1)

            def low(d):
                for h in range(2):
                    until(dve, yT_hi_done, 2 * d + h + 1)
                    nc.vector.tensor_tensor(yT_lo[:, 4 * h:4 * h + 4, :], turned[:].rearrange("p (k t) -> p k t", k=4),
                                            yT_hi[:, 4 * h:4 * h + 4, :].bitcast(F32), ALU.subtract)\
                        .then_inc(yT_lo_done, 1)

            def norm_heads(b, s):
                for n, (first, heads, width) in enumerate(((0, SB_HEADS, SB_DIM), (SB_WIDTH, H, ML_DIM))):
                    until(dve, squares_done, 2 * b + n + 1)
                    if n == 0:
                        until(dve, rstd_done, b)
                    nc.vector.tensor_reduce(ss[:, (0, SB_HEADS)[n]:(SB_HEADS, SB_HEADS + H)[n]],
                                            squares[:, first:first + heads * width]
                                            .rearrange("p (h d) -> p h d", h=heads), AX.X, ALU.add)\
                        .then_inc(ss_done, 1)
                until(dve, rstd_done, b + 1)
                until(dve, y_turned, 2 * b - 2)
                nc.vector.tensor_tensor(y[s][:, 0:SB_WIDTH].rearrange("p (h d) -> p h d", h=SB_HEADS),
                                        y_sb[:, at(b), :].rearrange("p a (h d) -> p (a h) d", h=SB_HEADS),
                                        rstd[:, 0:SB_HEADS].unsqueeze(2).broadcast_to([P, SB_HEADS, SB_DIM]),
                                        ALU.mult).then_inc(scaled_done, 1)
                for h in range(H):
                    i = nc.vector.scalar_tensor_tensor(
                        out=y[s][:, SB_WIDTH + h * ML_DIM:SB_WIDTH + (h + 1) * ML_DIM], in0=num[:, h, 0:ML_DIM],
                        scalar=rstd[:, SB_HEADS + h:SB_HEADS + h + 1],
                        in1=gates[s][:, 2 * GROUP + h * ML_DIM:2 * GROUP + (h + 1) * ML_DIM],
                        op0=ALU.mult, op1=ALU.mult)
                i.then_inc(ml_gated, 1)

            def numerator(u, c, p):
                until(dve, carried_done, u + 1)
                until(dve, intra_done, u + 1)
                until(dve, ml_gated, c)
                nc.vector.tensor_tensor(num[:, 2 * p:2 * p + 2, 0:DV], carried[p][:, :, 0:DV], intra[:, :, 0:DV],
                                        ALU.add).then_inc(num_done, 1)
                until(dve, update_done, u + 1)
                for i in range(2):
                    h = 2 * p + i
                    a = nc.vector.scalar_tensor_tensor(out=state[:, h, 0:DV], in0=state[:, h, 0:DV],
                                                       scalar=decay[:, h, at(c)], in1=update[:, i, 0:DV],
                                                       op0=ALU.mult, op1=ALU.add)
                a.then_inc(state_done, 1)

            def divide(c, s):
                until(dve, num_done, 2 * c + 2)
                dens = num[:, :, ML_DIM]
                nc.vector.scalar_tensor_tensor(out=den[:, 0, :], in0=dens, scalar=-1.0, in1=dens,
                                               op0=ALU.mult, op1=ALU.max).then_inc(den_done, 1)
                until(dve, den_done, 3 * c + 1)
                nc.vector.tensor_tensor(den[:, 1, :], den[:, 0, :],
                                        cols[:, at(c), FLOOR, :].rearrange("p a h -> p (a h)"), ALU.max)\
                    .then_inc(den_done, 1)
                until(dve, den_done, 3 * c + 2)
                nc.vector.reciprocal(den[:, 2, :], den[:, 1, :]).then_inc(den_done, 1)
                until(dve, den_done, 3 * c + 3)
                dve.wait_ge(gates_loaded[s], 32 * (c // 2) + 32 if isinstance(c, int) else (c - s) * 16 + 32)
                for h in range(H):
                    i = nc.vector.scalar_tensor_tensor(
                        out=num[:, h, 0:ML_DIM], in0=num[:, h, 0:ML_DIM], scalar=den[:, 2, h:h + 1],
                        in1=gates[s][:, GROUP + h * ML_DIM:GROUP + (h + 1) * ML_DIM], op0=ALU.mult, op1=ALU.mult)
                i.then_inc(ml_y_done, 1)

            def post(d, s):
                until(dve, post_rstd_done, d + 1)
                until(dve, h_stored[s], 16 * ((d - s) // 2) if isinstance(d, int) else (d - s) * 8)
                for n in range(2):
                    half = slice(n * GROUP, (n + 1) * GROUP)
                    nc.vector.scalar_tensor_tensor(out=h_out[s][:, half], in0=out[n][:], scalar=post_rstd[:, 1:2],
                                                   in1=post_w[:, half], op0=ALU.mult, op1=ALU.mult)\
                        .then_inc(normed_done, 1)

            def step(c, s, mlstm, dense):
                if mlstm:
                    weights_times_scores(2 * c, 0)
                if dense:
                    low(c - LAG)
                if not (isinstance(c, int) and not 1 <= c <= TOK):
                    norm_heads(c - 1, 1 - s)
                if mlstm:
                    weights_times_scores(2 * c + 1, 1)
                    numerator(2 * c, c, 0)
                    numerator(2 * c + 1, c, 1)
                    divide(c, s)
                if dense:
                    post(c - LAG, s)

            steps(dve.Fori, step)


def layer_embedding(nc, p, ple_w_up, ple_w_gate, ple_b_gate, residual, result):
    with ExitStack() as ctx:
        def sb(name, shape, dt=F32):
            return ctx.enter_context(nc.sbuf_tensor(name, shape, dt))

        def sem(name):
            return ctx.enter_context(nc.semaphore(name))

        def psum(name, shape):
            return ctx.enter_context(nc.psum_tensor(name, shape, F32))

        PT = PLE // P
        LOADS = 4
        w_raw = [sb(f"d_w_raw{s}", [P, D_MODEL]) for s in range(2)]
        w_hi = sb("d_w_hi", [P, KT + PT, D_MODEL], F32R)
        w_lo = sb("d_w_lo", [P, KT + PT, D_MODEL], F32R)
        bias = sb("d_bias", [P, D_MODEL])
        ident = sb("d_ident", [P, P])
        h_in = [sb(f"d_h{q}", [P, D_MODEL]) for q in range(LOADS)]
        p_in = [sb(f"d_p{q}", [P, PLE]) for q in range(LOADS)]
        hT_hi = [sb(f"d_hT_hi{s}", [P, KT + PT, P], F32R) for s in range(2)]
        hT_lo = [sb(f"d_hT_lo{s}", [P, KT + PT, P], F32R) for s in range(2)]
        gate = [sb(f"d_gate{s}", [P, D_MODEL]) for s in range(2)]
        turned = [psum(f"d_turned{n}", [P, GROUP]) for n in range(3)]
        product = [psum(f"d_product{n}", [P, GROUP]) for n in range(4)]

        w_loaded = [sem(f"d_w_loaded{s}") for s in range(2)]
        w_hi_done = sem("d_w_hi_done")
        w_lo_done = sem("d_w_lo_done")
        bias_loaded = sem("d_bias_loaded")
        zeroed = sem("d_zeroed")
        ident_ready = sem("d_ident_ready")
        h_loaded = [sem(f"d_h_loaded{q}") for q in range(LOADS)]
        p_loaded = [sem(f"d_p_loaded{q}") for q in range(LOADS)]
        stored = [sem(f"d_stored{s}") for s in range(2)]
        turned_done = sem("d_turned_done")
        hi_done = sem("d_hi_done")
        lo_done = sem("d_lo_done")
        product_done = sem("product_done")
        biased = sem("biased")
        sigmoid_done = sem("sigmoid_done")
        gated = sem("gated")
        sum_done = sem("sum_done")
        tiles = [ple_w_gate[k * P:(k + 1) * P, :] for k in range(KT)] + \
                [ple_w_up[k * P:(k + 1) * P, :] for k in range(PT)]
        load_w, split_hi, split_lo = split_weights(nc, tiles, w_raw, w_hi, w_lo, w_loaded, w_hi_done, w_lo_done)
        PIECES = ((0, 4), (4, 4), (KT, PT))

        def tile_steps(fori, step):
            step(0, 0)
            with fori(0, TOK // LOADS - 1) as n:
                for j in range(1, LOADS + 1):
                    step(n, j)
            for j in range(1, LOADS):
                step(TOK // LOADS - 1, j)

        def is_last(n, j):
            return isinstance(n, int) and LOADS * n + j == TOK - 1

        block = ctx.enter_context(nc.Block())

        @block.gpsimd
        def _(pool):
            nc.gpsimd.memset(ident[:], 0.0).then_inc(zeroed, 1)
            pool.wait_ge(zeroed, 1)
            nc.gpsimd.affine_select(out=ident[:], in_=ident[:], compare_op=ALU.not_equal, fill=1.0, base=0,
                                    pattern=[[-1, P]], channel_multiplier=1).then_inc(ident_ready, 1)

            def load(n, q):
                rows = bass.ds((LOADS * n + q) * P, P)
                pool.dma_start(h_in[q][:], residual[rows, :]).then_inc(h_loaded[q], 16)
                pool.dma_start(p_in[q][:], p[rows, :]).then_inc(p_loaded[q], 16)

            for q in range(LOADS):
                load(0, q)
            with pool.Fori(1, TOK // LOADS) as n:
                for q in range(LOADS):
                    pool.wait_ge(sum_done, LOADS * n + (q + 1 - LOADS))
                    load(n, q)

        @block.sync
        def _(sp):
            sp.dma_start(bias[:], ple_b_gate.broadcast_to([P, D_MODEL])).then_inc(bias_loaded, 16)
            load_w(sp)
            with sp.Fori(0, TOK // 2) as n:
                for s in range(2):
                    sp.wait_ge(sum_done, 2 * n + (s + 1))
                    sp.dma_start(result[bass.ds((2 * n + s) * P, P), :], gate[s][:]).then_inc(stored[s], 16)
            for s in range(2):
                sp.wait_ge(stored[s], 16 * (TOK // 2))

        @block.tensor
        def _(pe):
            def turn(n, j):
                t, q = LOADS * n + j, j % LOADS
                pe.wait_ge(h_loaded[q], 16 * (n + (j // LOADS + 1)))
                pe.wait_ge(p_loaded[q], 16 * (n + (j // LOADS + 1)))
                for i, (k0, count) in enumerate(PIECES):
                    src = p_in[q] if k0 == KT else h_in[q]
                    until(pe, lo_done, 3 * t + (i - 2))
                    for k in range(count):
                        at = (k0 % KT + k) * P
                        mm = pe.transpose(turned[i][:, k * P:(k + 1) * P], src[:, at:at + P], ident[:])
                    mm.then_inc(turned_done, 1)

            def multiply(n, j, first):
                t, s = LOADS * n + j, j % 2
                until(pe, lo_done, 3 * t + 3)
                for b in range(4):
                    if b < 2:
                        until(pe, biased, 2 * t + (b - 1))
                    else:
                        until(pe, gated, 2 * t + (b - 3))
                    half = slice(b % 2 * GROUP, (b % 2 + 1) * GROUP)
                    ks = range(KT) if b < 2 else range(KT, KT + PT)
                    for k in ks:
                        if first:
                            pe.wait_ge(w_lo_done, k + 1)
                        for i, (a, w) in enumerate(((hT_lo, w_hi), (hT_hi, w_lo), (hT_hi, w_hi))):
                            mm = pe.matmul(product[b][:], a[s][:, k, :], w[:, k, half],
                                           start=(k == ks[0] and i == 0), stop=(k == ks[-1] and i == 2))
                    mm.then_inc(product_done, 1)
                    if b == 0 and not is_last(n, j):
                        turn(n, j + 1)

            pe.wait_ge(ident_ready, 1)
            turn(0, 0)
            tile_steps(pe.Fori, lambda n, j: multiply(n, j, isinstance(n, int) and n == 0 and j == 0))

        @block.scalar
        def _(act):
            act.preload_act_table_set("sigmoid_and_others")

            def high(n, j):
                t, s = LOADS * n + j, j % 2
                for i, (k0, count) in enumerate(PIECES):
                    act.wait_ge(turned_done, 3 * t + (i + 1))
                    nc.scalar.copy(hT_hi[s][:, k0:k0 + count, :],
                                   turned[i][:, 0:count * P].rearrange("p (k t) -> p k t", t=P)).then_inc(hi_done, 1)

            def step(n, j):
                t, s = LOADS * n + j, j % 2
                if not is_last(n, j):
                    high(n, j + 1)
                for b in range(2):
                    half = slice(b * GROUP, (b + 1) * GROUP)
                    act.wait_ge(biased, 2 * t + (b + 1))
                    nc.scalar.activation(gate[s][:, half], gate[s][:, half], ACT.Sigmoid).then_inc(sigmoid_done, 1)

            high(0, 0)
            split_hi(act)
            tile_steps(act.Fori, step)

        @block.vector
        def _(dve):
            def low(n, j):
                t, s = LOADS * n + j, j % 2
                for i, (k0, count) in enumerate(PIECES):
                    dve.wait_ge(hi_done, 3 * t + (i + 1))
                    nc.vector.tensor_tensor(hT_lo[s][:, k0:k0 + count, :],
                                            turned[i][:, 0:count * P].rearrange("p (k t) -> p k t", t=P),
                                            hT_hi[s][:, k0:k0 + count, :].bitcast(F32), ALU.subtract)\
                        .then_inc(lo_done, 1)

            def step(n, j):
                t, s = LOADS * n + j, j % 2
                until(dve, stored[s], 16 * (LOADS // 2 * n + j // 2))
                for b in range(2):
                    half = slice(b * GROUP, (b + 1) * GROUP)
                    dve.wait_ge(product_done, 4 * t + (b + 1))
                    nc.vector.tensor_tensor(gate[s][:, half], product[b][:], bias[:, half], ALU.add)\
                        .then_inc(biased, 1)
                    if b == 0 and not is_last(n, j):
                        low(n, j + 1)
                for b in range(2):
                    half = slice(b * GROUP, (b + 1) * GROUP)
                    dve.wait_ge(sigmoid_done, 2 * t + (b + 1))
                    dve.wait_ge(product_done, 4 * t + (b + 3))
                    nc.vector.tensor_tensor(gate[s][:, half], gate[s][:, half], product[2 + b][:], ALU.mult)\
                        .then_inc(gated, 1)
                dve.wait_ge(gated, 2 * t + 2)
                nc.vector.tensor_tensor(gate[s][:], gate[s][:], h_in[j % LOADS][:], ALU.add).then_inc(sum_done, 1)

            low(0, 0)
            split_lo(dve)
            dve.wait_ge(bias_loaded, 16)
            tile_steps(dve.Fori, step)


def hybrid_block(nc, x, p, pre_norm_w, w_in, ml_conv_w, ml_conv_b, ml_i_bias, ml_f_bias, sb_norm_w, ml_norm_w,
                 w_out, post_norm_w, ple_w_up, ple_w_gate, ple_b_gate, out):
    def scratch(name, shape):
        return nc.dram_tensor(name, shape, F32, kind="Internal").ap()

    qk_hi = scratch("qk_hi", [2 * SB_WIDTH, SEQ])
    qk_lo = scratch("qk_lo", [2 * SB_WIDTH, SEQ])
    ml_t = scratch("ml_t", [2 * ML_WIDTH, SEQ])
    proj_n = scratch("proj_n", [SEQ, 5 * GROUP])
    gates_t = scratch("gates_t", [GATES, SEQ])
    residual = scratch("residual", [SEQ, D_MODEL])
    input_projection(nc, x[0], pre_norm_w, w_in[0], ml_conv_w[0], ml_conv_b, sb_norm_w, ml_norm_w,
                     qk_hi, qk_lo, ml_t, proj_n, gates_t)
    with nc.sbuf_tensor("y_sb", [P, TOK, SB_WIDTH], F32) as y_sb:
        stick_breaking_attention(nc, qk_hi, qk_lo, proj_n, y_sb)
        mlstm_and_output_projection(nc, x[0], ml_i_bias, ml_f_bias, w_out[0], post_norm_w, ml_t, proj_n, gates_t,
                                    y_sb, residual)
    layer_embedding(nc, p[0, 0], ple_w_up[0], ple_w_gate[0], ple_b_gate, residual, out[0])


_INS = ['x', 'p', 'pre_norm_w', 'w_in', 'ml_conv_w', 'ml_conv_b', 'ml_i_bias', 'ml_f_bias', 'sb_norm_w', 'ml_norm_w',
        'w_out', 'post_norm_w', 'ple_w_up', 'ple_w_gate', 'ple_b_gate']


def kernel(**inputs):
    import numpy as np
    import concourse.bacc as bacc
    from concourse.bass_utils import run_bass_kernel_spmd

    nc = bacc.Bacc("TRN2", target_bir_lowering=False, num_devices=1)
    arrays, args = {}, []
    for name in _INS:
        a = np.ascontiguousarray(inputs[name])
        arrays[f"in_{name}"] = a
        args.append(nc.dram_tensor(f"in_{name}", a.shape, mybir.dt.from_np(a.dtype), kind="ExternalInput").ap())
    out = nc.dram_tensor("out", (1, SEQ, D_MODEL), F32, kind="ExternalOutput").ap()
    hybrid_block(nc, *args, out)
    return run_bass_kernel_spmd(nc, [arrays], core_ids=[0]).results[0]["out"]
```

```python
from contextlib import ExitStack

import concourse.bass as bass
import concourse.mybir as mybir

P = 128
F32 = mybir.dt.float32
F32R = mybir.dt.float32r
BF16 = mybir.dt.bfloat16
ALU = mybir.AluOpType
ACT = mybir.ActivationFunctionType
AX = mybir.AxisListType

SEQ, D_MODEL, PLE = 2048, 1024, 256
SB_WIDTH, ML_WIDTH = 512, 512
SB_HEADS, SB_DIM = 8, 64
ML_HEADS, ML_DIM = 4, 128
CONV_K = 4
EPS = 1e-6
SB_SCALE = SB_DIM ** -0.5
ML_SCALE = ML_DIM ** -0.5

TOK = SEQ // P
KT = D_MODEL // P
GROUP = 512
TG = SEQ // GROUP
BANKS = 4
GATES = 2 * ML_HEADS
GATE_COL = 4 * SB_WIDTH + 5 * ML_WIDTH
GROUPS = GATE_COL // GROUP
MASKED = -1e30
BIG = 2.0 ** 100
LN_MAX = 40.0


def until(engine, semaphore, count):
    if not isinstance(count, int) or count > 0:
        engine.wait_ge(semaphore, count)


def input_projection(nc, x, pre_norm_w, w_in, conv_w, conv_b, sb_norm_w, ml_norm_w, qk_hi, qk_lo, ml_t, proj_n,
                     gates_t):
    with ExitStack() as ctx:
        def sb(name, shape, dt=F32):
            return ctx.enter_context(nc.sbuf_tensor(name, shape, dt))

        def sem(name):
            return ctx.enter_context(nc.semaphore(name))

        ident = sb("a_ident", [P, P])
        cw = sb("conv_w", [P, 2 * TG, CONV_K])
        cb = sb("conv_b", [P, 2 * TG])
        pre_w = sb("pre_w", [P, D_MODEL])
        minus_half = sb("a_minus_half", [P, 1])
        eps = sb("a_eps", [P, 1])
        x_in = [sb(f"x_in{i}", [P, D_MODEL]) for i in range(2)]
        xn = [sb(f"xn{i}", [P, D_MODEL]) for i in range(2)]
        mean_sq = sb("a_mean_sq", [P, 2])
        mean_eps = sb("a_mean_eps", [P, 2])
        rstd = sb("a_rstd", [P, 2])
        uT_hi = sb("uT_hi", [P, KT, SEQ], F32R)
        uT_lo = sb("uT_lo", [P, KT, SEQ], F32R)
        w_raw = sb("w_raw", [P, KT, GROUP])
        w_hi = sb("w_hi", [P, KT, GROUP], F32R)
        w_lo = sb("w_lo", [P, KT, GROUP], F32R)
        wg_raw = sb("wg_raw", [P, KT, GATES])
        wg_hi = sb("wg_hi", [P, KT, GATES], F32R)
        wg_lo = sb("wg_lo", [P, KT, GATES], F32R)
        stage = [x_in[i // 2][:, i % 2 * GROUP:(i % 2 + 1) * GROUP] for i in range(BANKS)]
        HALO = CONV_K - 1
        stage_hi = [sb(f"stage_hi{i}", [P, GROUP + HALO + 1], F32R) for i in range(2)]
        stage_lo = [sb(f"stage_lo{i}", [P, GROUP], F32R) for i in range(2)]
        conv_in = [t[:, 0:GROUP + HALO].bitcast(F32) for t in stage_hi]
        conv_out = [t[:].bitcast(F32) for t in stage_lo]
        gate_w = [xn[0][:, 0:SB_WIDTH], xn[0][:, SB_WIDTH:]]
        pt = [ctx.enter_context(nc.psum_tensor(f"a_pt{i}", [P, GROUP], F32)) for i in range(2)]
        po = [ctx.enter_context(nc.psum_tensor(f"a_po{i}", [P, GROUP], F32)) for i in range(BANKS)]

        consts_loaded = sem("a_consts_loaded")
        half_ready = sem("a_half_ready")
        ident_ready = sem("a_ident_ready")
        x_loaded = [sem(f"x_loaded{i}") for i in range(2)]
        x_read = sem("x_read")
        mean_sq_done = sem("a_mean_sq_done")
        mean_eps_done = sem("a_mean_eps_done")
        rstd_done = sem("a_rstd_done")
        xpose_done = sem("a_xpose_done")
        u_hi_done = sem("u_hi_done")
        u_lo_done = sem("u_lo_done")
        w_loaded = sem("w_loaded")
        wg_loaded = sem("wg_loaded")
        w_hi_done = sem("w_hi_done")
        w_lo_done = sem("w_lo_done")
        wg_hi_done = sem("wg_hi_done")
        wg_lo_done = sem("wg_lo_done")
        w_used = sem("w_used")
        out_ready = sem("out_ready")
        evacuated = [sem(f"evacuated{i}") for i in range(BANKS)]
        stored = [sem(f"stored{i}") for i in range(BANKS)]
        staged_hi = [sem(f"staged_hi{i}") for i in range(2)]
        stored_hi = [sem(f"stored_hi{i}") for i in range(2)]
        stored_lo = [sem(f"stored_lo{i}") for i in range(2)]

        conv_w_loaded = sem("conv_w_loaded")
        gate_w_loaded = sem("gate_w_loaded")
        halo_done = sem("halo_done")
        conv_in_done = sem("conv_in_done")
        tap_done = sem("tap_done")
        staged = [sem(f"staged{i}") for i in range(BANKS)]

        w_view = w_in.rearrange("(k p) n -> p k n", p=P)

        def first_group(fori, step):
            for j in range(4):
                step(0, j)
            with fori(1, TG - 1) as q:
                for j in range(4):
                    step(q, j)
            for j in range(4):
                step(TG - 1, j)

        def behind(q):
            return not isinstance(q, int) or q > 0

        def has_next(q, j):
            return not (isinstance(q, int) and 4 * q + j == TOK - 1)

        def whole_group(fori, evacuate, split_next):
            with fori(0, TG - 1) as m:
                for t in range(BANKS):
                    evacuate(m, t)
            last_tiles(evacuate, split_next)

        def last_tiles(evacuate, split_next):
            for t in range(BANKS - 1):
                evacuate(TG - 1, t)
            split_next(range(KT - 1))
            evacuate(TG - 1, BANKS - 1)
            split_next(range(KT - 1, KT))

        def nothing(ks):
            pass

        block = ctx.enter_context(nc.Block())

        @block.gpsimd
        def _(pool):
            nc.gpsimd.memset(minus_half[:], -0.5).then_inc(half_ready, 1)
            nc.gpsimd.memset(eps[:], EPS).then_inc(half_ready, 1)
            nc.gpsimd.memset(ident[:], 0.0).then_inc(half_ready, 1)
            pool.wait_ge(half_ready, 3)
            nc.gpsimd.affine_select(out=ident[:], in_=ident[:], compare_op=ALU.not_equal, fill=1.0, base=0,
                                    pattern=[[-1, P]], channel_multiplier=1).then_inc(ident_ready, 1)
            pool.dma_start(w_raw[:], w_view[:, :, 0:GROUP]).then_inc(w_loaded, 16)
            with nc.allow_non_contiguous_dma("eight gate columns"):
                pool.dma_start(wg_raw[:], w_view[:, :, GATE_COL:GATE_COL + GATES]).then_inc(wg_loaded, 16)
            with pool.Fori(0, TOK // 2) as n:
                for i in range(2):
                    m = mean_eps[:, i:i + 1]
                    pool.wait_ge(mean_sq_done, 2 * n + (i + 1))
                    pool.wait_ge(x_read, 2 * n + (i + 1))
                    nc.gpsimd.tensor_tensor(m, mean_sq[:, i:i + 1], eps[:], ALU.add).then_inc(mean_eps_done, 1)
                    pool.wait_ge(mean_eps_done, 2 * n + (i + 1))
                    nc.gpsimd.tensor_tensor(rstd[:, i:i + 1], m, minus_half[:], ALU.pow).then_inc(rstd_done, 1)
            with pool.Fori(1, GROUPS) as g:
                pool.wait_ge(w_lo_done, g * KT)
                pool.dma_start(w_raw[:], w_view[:, :, bass.ds(g * GROUP, GROUP)]).then_inc(w_loaded, 16)

        @block.sync
        def _(sp):
            sp.dma_start(pre_w[:], pre_norm_w.broadcast_to([P, D_MODEL])).then_inc(consts_loaded, 16)
            def load_x(q, j):
                i = j % 2
                sp.wait_ge(x_read, 4 * q + (j + 1))
                sp.dma_start(x_in[i][:], x[bass.ds((4 * q + j) * P, P), :]).then_inc(x_loaded[i], 16)

            def store_qk(n, t, rows, cols):
                i = t % 2
                sp.wait_ge(staged_hi[i], 2 * n + (t // 2 + 1))
                sp.dma_start(qk_hi[rows, cols], stage_hi[i][:, 0:GROUP].bitcast(F32)).then_inc(stored_hi[i], 16)
                sp.wait_ge(evacuated[t], n + 2)
                sp.dma_start(qk_lo[rows, cols], stage_lo[i][:].bitcast(F32)).then_inc(stored_lo[i], 16)

            def store_first(q, j):
                store_qk(q - 1, j, slice(j * P, (j + 1) * P), bass.ds((q - 1) * GROUP, GROUP))

            def step(q, j):
                if isinstance(q, int) and q == TG - 1:
                    if j < 2:
                        load_x(q, j + 2)
                else:
                    load_x(q, j + 2)
                if behind(q):
                    store_first(q, j)

            load_x(0, 0)
            load_x(0, 1)
            first_group(sp.Fori, step)
            for j in range(4):
                store_first(TG, j)

            sp.wait_ge(u_lo_done, 2 * TOK + 4)
            sp.dma_start(gate_w[0], sb_norm_w.broadcast_to([P, SB_WIDTH])).then_inc(gate_w_loaded, 16)
            sp.dma_start(gate_w[1], ml_norm_w.broadcast_to([P, ML_WIDTH])).then_inc(gate_w_loaded, 16)
            with nc.allow_non_contiguous_dma("the convolution's few weights"):
                for j in range(CONV_K):
                    sp.dma_start(cw[:, :, j], conv_w[j, :].rearrange("(c p) -> p c", p=P)).then_inc(conv_w_loaded, 16)
                sp.dma_start(cb[:], conv_b.rearrange("a (c p) -> p (a c)", p=P)).then_inc(conv_w_loaded, 16)

            with sp.Fori(0, TG) as m:
                for t in range(TG):
                    store_qk(m + TG, t, bass.ds((m + TG) * P, P), slice(t * GROUP, (t + 1) * GROUP))

            def store(ready, g, dram, row, row_step, col):
                with sp.Fori(0, TG) as m:
                    for t in range(BANKS):
                        sp.wait_ge(ready[t], g * TG + m + 2)
                        rows = bass.ds((row + m * row_step + (0 if dram is ml_t else t)) * P, P)
                        cols = slice(t * GROUP, (t + 1) * GROUP) if dram is ml_t else slice(col, col + GROUP)
                        sp.dma_start(dram[rows, cols], stage[t]).then_inc(stored[t], 16)

            store(evacuated, 2, proj_n, 0, BANKS, 0)
            store(staged, 0, proj_n, 0, BANKS, GROUP)
            for c in range(2):
                store(staged, 1 + c, ml_t, c * TG, 1, 0)
            store(evacuated, 6, proj_n, 0, BANKS, 2 * GROUP)
            store(evacuated, 7, proj_n, 0, BANKS, 3 * GROUP)
            store(staged, 3, proj_n, 0, BANKS, 4 * GROUP)
            for t in range(TG):
                sp.wait_ge(evacuated[t], GROUPS * TG + 2)
                sp.dma_start(gates_t[:, t * GROUP:(t + 1) * GROUP], stage[t][0:GATES, :]).then_inc(stored[t], 16)
            for t in range(BANKS):
                sp.wait_ge(stored[t], 16 * ((GROUPS - 2) * TG + 2))
            for i in range(2):
                sp.wait_ge(stored_hi[i], 16 * (4 * TG + 1))
                sp.wait_ge(stored_lo[i], 16 * (4 * TG + 1))

        @block.scalar
        def _(act):
            def square(q, j):
                i = j % 2
                act.wait_ge(x_loaded[i], 32 * q + (16 * (j // 2) + 16))
                act.wait_ge(u_lo_done, 8 * q + (2 * j + 2))
                nc.scalar.activation(xn[i][:], x_in[i][:], ACT.Square, scale=D_MODEL ** -0.5,
                                     accum_out=mean_sq[:, i:i + 1]).then_inc(mean_sq_done, 1)

            def high(q, j):
                for h in range(2):
                    act.wait_ge(xpose_done, 8 * q + (2 * j + h + 1))
                    nc.scalar.copy(uT_hi[:, 4 * h:4 * h + 4, bass.ds((4 * q + j) * P, P)],
                                   pt[h][:].rearrange("p (k t) -> p k t", k=4)).then_inc(u_hi_done, 1)

            def split(g, ks=range(KT)):
                act.wait_ge(w_loaded, 16 * g + 16)
                for k in ks:
                    if k < KT - 1:
                        act.wait_ge(w_used, (KT - 1) * g + (k + 1))
                    else:
                        act.wait_ge(out_ready, 16 * g + 1)
                    nc.scalar.copy(w_hi[:, k, :], w_raw[:, k, :]).then_inc(w_hi_done, 1)

            def evacuate_hi(g, scale):
                def tile(m, t):
                    act.wait_ge(out_ready, 4 * m + (16 * g + t + 2))
                    act.wait_ge(stored_hi[t % 2], 32 * m + 16 * (2 * TG * g + t // 2 + 1))
                    act.wait_ge(evacuated[(t + 2) % BANKS], m + (TG * g + (1 if t < 2 else 2)))
                    nc.scalar.mul(stage_hi[t % 2][:, 0:GROUP], po[t][:], scale).then_inc(staged_hi[t % 2], 1)
                return tile

            def evacuate_copy(g):
                def tile(m, t):
                    if t % 2 == 1:
                        act.wait_ge(out_ready, 4 * m + (16 * g + t + 2))
                        act.wait_ge(stored[t], 16 * m + (16 * ((g - 2) * TG + 1)))
                        nc.scalar.copy(stage[t], po[t][:]).then_inc(evacuated[t], 1)
                return tile

            def evacuate_gate(g, func):
                def tile(m, t):
                    act.wait_ge(out_ready, 4 * m + (16 * g + t + 2))
                    act.wait_ge(stored[t], 16 * m + (16 * ((g - 2) * TG + 1)))
                    nc.scalar.activation(stage[t], po[t][:], func).then_inc(evacuated[t], 1)
                return tile

            def evacuate_conv(g):
                def silu(m, t):
                    act.wait_ge(tap_done, TG * CONV_K * m + CONV_K * (TG * TG * (g - 4) + t + 3))
                    act.wait_ge(stored[t], 16 * m + (16 * ((g - 2) * TG + 1)))
                    nc.scalar.activation(stage[t], conv_out[t % 2], ACT.Silu).then_inc(staged[t], 1)

                def tile(m, t):
                    act.wait_ge(out_ready, 4 * m + (16 * g + t + 2))
                    act.wait_ge(halo_done, TG * m + (TG * TG * (g - 4) + t + 1))
                    nc.scalar.copy(conv_in[t % 2][:, HALO:], po[t][:]).then_inc(evacuated[t], 1)
                    if t > 0:
                        silu(m, t - 1)
                    if t == BANKS - 1:
                        silu(m, t)
                return tile

            first_tile = evacuate_hi(0, -SB_SCALE)

            def step(q, j):
                if has_next(q, j):
                    square(q, j + 1)
                high(q, j)
                if behind(q):
                    first_tile(q - 1, j)

            square(0, 0)
            for j in range(4):
                step(0, j)
            split(0)
            with act.Fori(1, TG - 1) as q:
                for j in range(4):
                    step(q, j)
            for j in range(4):
                step(TG - 1, j)
            last_tiles(first_tile, lambda ks: split(1, ks))
            for g, evacuate in ((1, evacuate_hi(1, 1.0)),
                                (2, evacuate_copy(2)), (3, evacuate_gate(3, ACT.Silu)),
                                (4, evacuate_conv(4)), (5, evacuate_conv(5)),
                                (6, evacuate_copy(6)), (7, evacuate_gate(7, ACT.Sigmoid)),
                                (8, evacuate_gate(8, ACT.Silu))):
                if g == 2:
                    act.wait_ge(wg_loaded, 16)
                    nc.scalar.copy(wg_hi[:], wg_raw[:]).then_inc(wg_hi_done, 1)
                whole_group(act.Fori, evacuate, (lambda ks: split(g + 1, ks)) if g < GROUPS - 1 else nothing)
            for t in (1, 3):
                act.wait_ge(out_ready, 16 * GROUPS + (t + 2))
                act.wait_ge(stored[t], 16 * ((GROUPS - 2) * TG + 1))
                nc.scalar.copy(stage[t][0:GATES, :], po[t][0:GATES, :]).then_inc(evacuated[t], 1)

        @block.vector
        def _(dve):
            for s, count in ([(x_read, 1), (x_read, 1), (u_lo_done, 4), (w_used, KT - 1), (out_ready, 1),
                              (tap_done, 2 * CONV_K)] +
                             [(s, 1) for s in evacuated + staged] +
                             [(s, 16) for s in stored + stored_hi + stored_lo]):
                dve.sem_inc(s, count)
            dve.wait_ge(consts_loaded, 16)

            def scale(q, j):
                i = j % 2
                dve.wait_ge(rstd_done, 4 * q + (j + 1))
                nc.vector.scalar_tensor_tensor(out=xn[i][:], in0=x_in[i][:], scalar=rstd[:, i:i + 1],
                                               in1=pre_w[:], op0=ALU.mult, op1=ALU.mult).then_inc(x_read, 1)

            def low(q, j):
                for h in range(2):
                    dve.wait_ge(u_hi_done, 8 * q + (2 * j + h + 1))
                    hi = uT_hi[:, 4 * h:4 * h + 4, bass.ds((4 * q + j) * P, P)].bitcast(F32)
                    nc.vector.tensor_tensor(uT_lo[:, 4 * h:4 * h + 4, bass.ds((4 * q + j) * P, P)],
                                            pt[h][:].rearrange("p (k t) -> p k t", k=4), hi,
                                            ALU.subtract).then_inc(u_lo_done, 1)

            def split(g, ks=range(KT)):
                for k in ks:
                    dve.wait_ge(w_hi_done, KT * g + (k + 1))
                    nc.vector.tensor_tensor(w_lo[:, k, :], w_raw[:, k, :], w_hi[:, k, :].bitcast(F32),
                                            ALU.subtract).then_inc(w_lo_done, 1)

            def evacuate_lo(g, factor):
                def tile(m, t):
                    dve.wait_ge(staged_hi[t % 2], 2 * m + (2 * TG * g + t // 2 + 1))
                    dve.wait_ge(stored_lo[t % 2], 32 * m + 16 * (2 * TG * g + t // 2 + 1))
                    nc.vector.scalar_tensor_tensor(out=stage_lo[t % 2][:], in0=po[t][:], scalar=factor,
                                                   in1=stage_hi[t % 2][:, 0:GROUP].bitcast(F32), op0=ALU.mult,
                                                   op1=ALU.subtract).then_inc(evacuated[t], 1)
                return tile

            def evacuate_copy(g):
                def tile(m, t):
                    if t % 2 == 0:
                        dve.wait_ge(out_ready, 4 * m + (16 * g + t + 2))
                        dve.wait_ge(stored[t], 16 * m + (16 * ((g - 2) * TG + 1)))
                        nc.vector.tensor_copy(stage[t], po[t][:]).then_inc(evacuated[t], 1)
                return tile

            def weigh_gate(g, w):
                def tile(m, t):
                    dve.wait_ge(evacuated[t], m + (TG * g + 2))
                    nc.vector.tensor_tensor(stage[t], stage[t], w, ALU.mult).then_inc(staged[t], 1)
                return tile

            def convolve(g):
                def tile(m, t):
                    n = TG * TG * (g - 4) + t
                    c = m + (g - 4) * TG
                    w = [cw[:, bass.ds(c, 1), j] for j in range(CONV_K)]
                    x_in_, out = conv_in[t % 2], conv_out[t % 2]
                    if t == 0:
                        dve.wait_ge(tap_done, TG * CONV_K * m + (CONV_K * n + CONV_K))
                        nc.vector.memset(x_in_[:, 0:HALO], 0.0).then_inc(halo_done, 1)
                    dve.wait_ge(evacuated[t], m + (TG * g + 2))
                    dve.wait_ge(staged[(t + 2) % BANKS], m + (TG * (g - 3) + (1 if t < 2 else 2)))
                    nc.vector.tensor_scalar(out, x_in_[:, 0:GROUP], w[0], cb[:, bass.ds(c, 1)], ALU.mult, ALU.add)\
                        .then_inc(tap_done, 1)
                    if t < BANKS - 1:
                        dve.wait_ge(tap_done, TG * CONV_K * m + CONV_K * (n + 2))
                        nc.vector.tensor_copy(conv_in[(t + 1) % 2][:, 0:HALO], x_in_[:, GROUP:])\
                            .then_inc(halo_done, 1)
                    for j in range(1, CONV_K):
                        dve.wait_ge(tap_done, TG * CONV_K * m + (CONV_K * (n + 2) + j))
                        nc.vector.scalar_tensor_tensor(out=out, in0=x_in_[:, j:j + GROUP], scalar=w[j], in1=out,
                                                       op0=ALU.mult, op1=ALU.add).then_inc(tap_done, 1)
                return tile

            def no_tiles(m, t):
                pass

            first_tile = evacuate_lo(0, -SB_SCALE)

            def step(q, j):
                if has_next(q, j):
                    scale(q, j + 1)
                low(q, j)
                if behind(q):
                    first_tile(q - 1, j)

            scale(0, 0)
            for j in range(4):
                step(0, j)
            split(0)
            with dve.Fori(1, TG - 1) as q:
                for j in range(4):
                    step(q, j)
            for j in range(4):
                step(TG - 1, j)
            last_tiles(first_tile, lambda ks: split(1, ks))
            for g, evacuate in ((1, evacuate_lo(1, 1.0)),
                                (2, evacuate_copy(2)), (3, weigh_gate(3, gate_w[0])),
                                (4, convolve(4)), (5, convolve(5)),
                                (6, evacuate_copy(6)), (7, no_tiles),
                                (8, weigh_gate(8, gate_w[1]))):
                if g == 2:
                    dve.wait_ge(wg_hi_done, 1)
                    nc.vector.tensor_tensor(wg_lo[:], wg_raw[:], wg_hi[:].bitcast(F32), ALU.subtract)\
                        .then_inc(wg_lo_done, 1)
                if g == 3:
                    dve.wait_ge(gate_w_loaded, 32)
                if g == 4:
                    dve.wait_ge(conv_w_loaded, 16 * (CONV_K + 1))
                    for i in range(2):
                        dve.wait_ge(stored_hi[i], 16 * (4 * TG + 1))
                        dve.wait_ge(stored_lo[i], 16 * (4 * TG + 1))
                whole_group(dve.Fori, evacuate, (lambda ks: split(g + 1, ks)) if g < GROUPS - 1 else nothing)
            for t in (0, 2):
                dve.wait_ge(out_ready, 16 * GROUPS + (t + 2))
                dve.wait_ge(stored[t], 16 * ((GROUPS - 2) * TG + 1))
                nc.vector.tensor_copy(stage[t][0:GATES, :], po[t][0:GATES, :]).then_inc(evacuated[t], 1)

        @block.tensor
        def _(pe):
            PARTS = ((1, 0), (0, 1), (0, 0))

            def turn(q, j):
                i = j % 2
                pe.wait_ge(x_read, 4 * q + (j + 3))
                for h in range(2):
                    pe.wait_ge(u_lo_done, 8 * q + (2 * j + h + 3))
                    for k in range(4):
                        mm = pe.transpose(pt[h][:, k * P:(k + 1) * P],
                                          xn[i][:, (4 * h + k) * P:(4 * h + k + 1) * P], ident[:])
                    mm.then_inc(xpose_done, 1)

            def first_tile(q, j):
                pe.wait_ge(evacuated[j], q + 1)
                pe.wait_ge(u_lo_done, 8 * q + (8 + 4))
                final = isinstance(q, int) and 4 * q + j == 4 * TG - 1
                for k in range(KT):
                    pe.wait_ge(w_lo_done, k + 1)
                    for n, (w_part, u_part) in enumerate(PARTS):
                        w, u = (w_hi, w_lo)[w_part], (uT_hi, uT_lo)[u_part]
                        mm = pe.matmul(po[j][:], w[:, k, j * P:(j + 1) * P], u[:, k, bass.ds(q * GROUP, GROUP)],
                                       start=(k == 0 and n == 0), stop=(k == KT - 1 and n == 2))
                    if final and k < KT - 1:
                        mm.then_inc(w_used, 1)
                mm.then_inc(out_ready, 1)

            def step(q, j):
                turn(q, j)
                if behind(q):
                    first_tile(q - 1, j)

            pe.wait_ge(ident_ready, 1)
            first_group(pe.Fori, step)
            for j in range(4):
                first_tile(TG - 1, j)

            def group(g, transposed):
                for m in range(TG):
                    for t in range(BANKS):
                        pe.wait_ge(evacuated[t], TG * g + (m + 1))
                        first, final = (m, t) == (0, 0), (m, t) == (TG - 1, BANKS - 1)
                        for k in range(KT):
                            if first:
                                pe.wait_ge(w_lo_done, KT * g + (k + 1))
                            for n, (w_part, u_part) in enumerate(PARTS):
                                w, u = (w_hi, w_lo)[w_part], (uT_hi, uT_lo)[u_part]
                                if transposed:
                                    lhsT, rhs = w[:, k, m * P:(m + 1) * P], u[:, k, t * GROUP:(t + 1) * GROUP]
                                else:
                                    token = m * BANKS + t
                                    lhsT, rhs = u[:, k, token * P:(token + 1) * P], w[:, k, :]
                                mm = pe.matmul(po[t][:], lhsT, rhs, start=(k == 0 and n == 0),
                                               stop=(k == KT - 1 and n == 2))
                            if final and k < KT - 1:
                                mm.then_inc(w_used, 1)
                        mm.then_inc(out_ready, 1)

            group(1, True)
            with pe.Fori(2, 4) as g:
                group(g, False)
            with pe.Fori(4, 6) as g:
                group(g, True)
            with pe.Fori(6, GROUPS) as g:
                group(g, False)
            pe.wait_ge(wg_lo_done, 1)
            for t in range(TG):
                pe.wait_ge(evacuated[t], TG * GROUPS + 1)
                for k in range(KT):
                    for n, (w_part, u_part) in enumerate(PARTS):
                        w, u = (wg_hi, wg_lo)[w_part], (uT_hi, uT_lo)[u_part]
                        mm = pe.matmul(po[t][0:GATES, :], w[:, k, :], u[:, k, t * GROUP:(t + 1) * GROUP],
                                       start=(k == 0 and n == 0), stop=(k == KT - 1 and n == 2))
                mm.then_inc(out_ready, 1)


def stick_breaking_attention(nc, qk_hi, qk_lo, proj_n, y_sb):
    with ExitStack() as ctx:
        def sb(name, shape, dt=F32):
            return ctx.enter_context(nc.sbuf_tensor(name, shape, dt))

        def sem(name):
            return ctx.enter_context(nc.semaphore(name))

        def psum(name, shape):
            return ctx.enter_context(nc.psum_tensor(name, shape, F32))

        PAIRS = SB_HEADS // 2
        BUFS, YS = 8, 4
        units = []
        for head in range(2):
            for i in range(TOK):
                parts = i // 4 + 1
                bounds = [(i + 1) * c // parts * P for c in range(parts + 1)]
                for c in reversed(range(parts)):
                    units.append((head, i, bounds[c], bounds[c + 1] - bounds[c], c == parts - 1, c == 0))
        UNITS = len(units)
        assert UNITS % BUFS == 0 and UNITS % YS == 0
        BEYOND_START = 4
        assert units[BEYOND_START][1] == 4
        firsts = [u for u in range(UNITS) if units[u][4]]
        E_LAG, SP_LAG, S_LAG, M_LAG, T_LAG, X_LAG, V_LAG, O_LAG = 1, 2, 3, 4, 5, 6, 7, 8

        def rank(u):
            return len(firsts) * (u // UNITS) + sum(f <= u % UNITS for f in firsts)

        def pipeline(fori, step):
            for n in range(O_LAG):
                step(0, n)
            with fori(0, PAIRS - 1) as it:
                for n in range(O_LAG, UNITS + O_LAG):
                    step(it, n)
            for n in range(O_LAG, UNITS + O_LAG):
                step(PAIRS - 1, n)

        def has(it, u):
            return u >= 0 and not (isinstance(it, int) and it == PAIRS - 1 and u >= UNITS)

        kst = [sb(f"kst{s}", [P, SEQ], F32R) for s in range(2)]
        qst_hi = [sb(f"qst_hi{s}", [P, SEQ], F32R) for s in range(2)]
        qst_lo = [sb(f"qst_lo{s}", [P, SEQ], F32R) for s in range(2)]
        v = sb("b_v", [P, TOK, SB_WIDTH])
        buf = [sb(f"b_buf{s}", [P, GROUP]) for s in range(BUFS)]
        aT = [sb(f"b_aT{s}", [P, GROUP]) for s in range(2)]
        ident = sb("b_ident", [P, P])
        lowest = sb("b_lowest", [P, P])
        y = [psum(f"b_y{s}", [P, GROUP]) for s in range(YS)]
        turned = [psum(f"b_turned{s}", [P, GROUP]) for s in range(2)]
        o = [psum(f"b_o{s}", [P, P]) for s in range(2)]

        zeroed = sem("b_zeroed")
        consts_ready = sem("b_consts_ready")
        qk_loaded = [sem(f"qk_loaded{s}") for s in range(2)]
        start_loaded = sem("b_start_loaded")
        v_start_loaded = sem("b_v_start_loaded")
        v_loaded = sem("b_v_loaded")
        y_done = sem("y_done")
        e_done = sem("e_done")
        ln_done = sem("ln_done")
        ln_masked = sem("ln_masked")
        sp_done = sem("sp_done")
        scan_done = sem("scan_done")
        log_done = sem("log_done")
        log_masked = sem("log_masked")
        turned_done = sem("turned_done")
        aT_done = sem("aT_done")
        av_done = sem("av_done")
        o_read = sem("o_read")
        block = ctx.enter_context(nc.Block())

        @block.gpsimd
        def _(pool):
            nc.gpsimd.memset(ident[:], 0.0).then_inc(zeroed, 1)
            nc.gpsimd.memset(lowest[:], 0.0).then_inc(zeroed, 1)
            pool.wait_ge(zeroed, 2)
            nc.gpsimd.affine_select(out=ident[:], in_=ident[:], compare_op=ALU.not_equal, fill=1.0, base=0,
                                    pattern=[[-1, P]], channel_multiplier=1).then_inc(consts_ready, 1)
            nc.gpsimd.affine_select(out=lowest[:], in_=lowest[:], compare_op=ALU.is_gt, fill=-BIG, base=0,
                                    pattern=[[-1, P]], channel_multiplier=1).then_inc(consts_ready, 1)
            pool.wait_ge(consts_ready, 2)

            def step(it, n):
                u = n - M_LAG
                if has(it, u) and units[u % UNITS][4]:
                    keys = units[u % UNITS][3]
                    own = buf[u % BUFS][:, keys - P:keys]
                    pool.wait_ge(log_done, it * UNITS + (u + 1 + YS))
                    nc.gpsimd.tensor_tensor(own, own, lowest[:], ALU.add).then_inc(log_masked, 1)
                n -= E_LAG
                if has(it, n) and units[n % UNITS][4]:
                    keys = units[n % UNITS][3]
                    own = buf[n % BUFS][:, keys - P:keys]
                    pool.wait_ge(ln_done, it * UNITS + (n + 1))
                    nc.gpsimd.tensor_tensor(own, own, lowest[:], ALU.add).then_inc(ln_masked, 1)

            pipeline(pool.Fori, step)

        @block.sync
        def _(sp):
            def load_head(s, head, cols, loaded):
                q, k = bass.ds(head * SB_DIM, SB_DIM), bass.ds(head * SB_DIM + SB_WIDTH, SB_DIM)
                for tile, top, bottom in ((kst, qk_hi[k, cols], qk_lo[k, cols]),
                                          (qst_hi, qk_hi[q, cols], qk_hi[q, cols]),
                                          (qst_lo, qk_lo[q, cols], qk_lo[q, cols])):
                    sp.dma_start(tile[s][0:SB_DIM, cols].bitcast(F32), top).then_inc(loaded, 16)
                    sp.dma_start(tile[s][SB_DIM:, cols].bitcast(F32), bottom).then_inc(loaded, 16)

            def load_v(tiles, loaded):
                rows = proj_n[tiles.start * P:tiles.stop * P, 0:SB_WIDTH]
                sp.dma_start(v[:, tiles, :], rows.rearrange("(j p) n -> p j n", p=P)).then_inc(loaded, 16)

            load_head(0, 0, slice(0, GROUP), start_loaded)
            load_v(slice(0, 4), v_start_loaded)
            load_head(0, 0, slice(GROUP, SEQ), qk_loaded[0])
            load_v(slice(4, TOK), v_loaded)
            load_head(1, 1, slice(0, SEQ), qk_loaded[1])
            with sp.Fori(1, PAIRS) as it:
                for s in range(2):
                    sp.wait_ge(y_done, (it - 1) * UNITS + UNITS // 2 * (s + 1))
                    load_head(s, 2 * it + s, slice(0, SEQ), qk_loaded[s])

        @block.tensor
        def _(pe):
            def turn(it, u):
                keys, first = units[u % UNITS][3:5]
                if first:
                    pe.wait_ge(log_masked, it * len(firsts) + rank(u))
                else:
                    pe.wait_ge(log_done, it * UNITS + (u + 1 + YS))
                pe.wait_ge(aT_done, it * UNITS + (u + 1))
                for j in range(keys // P):
                    mm = pe.transpose(turned[u % 2][:, j * P:(j + 1) * P], buf[u % BUFS][:, j * P:(j + 1) * P],
                                      ident[:])
                mm.then_inc(turned_done, 1)

            def score(it, u):
                head, i, key0, keys, first, last = units[u % UNITS]
                very_first = isinstance(it, int) and it == 0
                if very_first and u == 0:
                    pe.wait_ge(start_loaded, 96)
                if u % UNITS in (0, UNITS // 2) and not (very_first and u == 0) or very_first and u == BEYOND_START:
                    pe.wait_ge(qk_loaded[head], 96 * it + (96 * (u // UNITS) + 96))
                pe.wait_ge(log_done, it * UNITS + (u + 1))
                q = slice(i * P, (i + 1) * P)
                out, k = y[u % YS][:, 0:keys], kst[head][:, key0:key0 + keys]
                pe.matmul(out, qst_lo[head][:, q], k, start=True, stop=False)
                pe.matmul(out, qst_hi[head][:, q], k, start=False, stop=True).then_inc(y_done, 1)

            def times_v(it, u):
                head, i, key0, keys, first, last = units[u % UNITS]
                if isinstance(it, int) and it == 0 and u == 0:
                    pe.wait_ge(v_start_loaded, 16)
                if u == BEYOND_START:
                    pe.wait_ge(v_loaded, 16)
                pe.wait_ge(aT_done, it * UNITS + (u + 3))
                if first:
                    pe.wait_ge(o_read, it * (2 * TOK) + (2 * TOK * (u // UNITS) + head * TOK + i + 1))
                for j in range(keys // P):
                    mm = pe.matmul(o[i % 2][:], aT[u % 2][:, j * P:(j + 1) * P],
                                   v[:, key0 // P + j, bass.ds((it + u // UNITS) * P, P)],
                                   start=(first and j == 0), stop=(last and j == keys // P - 1))
                mm.then_inc(av_done, 1)

            def step(it, n):
                if has(it, n - T_LAG):
                    turn(it, n - T_LAG)
                if has(it, n - V_LAG):
                    times_v(it, n - V_LAG)
                if has(it, n):
                    score(it, n)

            pe.wait_ge(consts_ready, 2)
            pipeline(pe.Fori, step)

        @block.scalar
        def _(act):
            def step(it, n):
                e, x = n - E_LAG, n - X_LAG
                b = buf[e % BUFS][:, 0:units[e % UNITS][3]]
                if has(it, x):
                    keys = units[x % UNITS][3]
                    act.wait_ge(turned_done, it * UNITS + (x + 1 + BUFS))
                    act.wait_ge(av_done, it * UNITS + (x + 1))
                    nc.scalar.activation(aT[x % 2][:, 0:keys], turned[x % 2][:, 0:keys], ACT.Exp).then_inc(aT_done, 1)
                if has(it, e):
                    act.wait_ge(y_done, it * UNITS + (e + 1))
                    act.wait_ge(turned_done, it * UNITS + (e + 1))
                    nc.scalar.activation(b, y[e % YS][:, 0:units[e % UNITS][3]], ACT.Exp).then_inc(e_done, 1)
                if has(it, e):
                    act.wait_ge(e_done, it * UNITS + (e + 1))
                    nc.scalar.activation(b, b, ACT.Ln, bias=1.0).then_inc(ln_done, 1)

            act.preload_act_table_set("natural_log_exp_and_others")
            pipeline(act.Fori, step)

        @block.vector
        def _(dve):
            for s, count in ((log_done, YS - 1), (turned_done, BUFS), (aT_done, 2), (av_done, 2),
                             (o_read, 2)):
                dve.sem_inc(s, count)

            def softplus(it, u):
                keys, first = units[u % UNITS][3:5]
                b = buf[u % BUFS][:, 0:keys]
                if first:
                    dve.wait_ge(ln_masked, it * len(firsts) + rank(u))
                else:
                    dve.wait_ge(ln_done, it * UNITS + (u + 1))
                nc.vector.scalar_tensor_tensor(out=b, in0=b, scalar=LN_MAX, in1=y[u % YS][:, 0:keys], op0=ALU.min,
                                               op1=ALU.max).then_inc(sp_done, 1)

            def scan(it, u):
                keys = units[u % UNITS][3]
                b = buf[u % BUFS]
                down = b[:, 0:keys - 1][:, ::-1]
                dve.wait_ge(log_done, it * UNITS + (u + YS))
                nc.vector.tensor_tensor_scan(down, y[u % YS][:, 1:keys][:, ::-1], down,
                                             b[:, keys - 1:keys], ALU.add, ALU.subtract)\
                    .then_inc(log_done if not has(it, u + 1) else scan_done, 1)

            def start(it, u):
                keys, first = units[u % UNITS][3:5]
                last_key, before = buf[u % BUFS][:, keys - 1:keys], (u - 1) % BUFS
                dve.wait_ge(sp_done, it * UNITS + (u + 1))
                until(dve, scan_done, it * UNITS + u)
                if first:
                    nc.vector.tensor_scalar_mul(last_key, last_key, -1.0).then_inc(log_done, 1)
                else:
                    nc.vector.scalar_tensor_tensor(out=last_key, in0=y[(u - 1) % YS][:, 0:1], scalar=buf[before][:, 0:1],
                                                   in1=last_key, op0=ALU.add, op1=ALU.subtract).then_inc(log_done, 1)

            def step(it, n):
                if has(it, n - S_LAG):
                    scan(it, n - S_LAG)
                if has(it, n - SP_LAG):
                    softplus(it, n - SP_LAG)
                if has(it, n - SP_LAG):
                    start(it, n - SP_LAG)
                u = n - O_LAG
                if has(it, u) and units[u % UNITS][5]:
                    head, i = units[u % UNITS][0:2]
                    dve.wait_ge(av_done, it * UNITS + (u + 3))
                    nc.vector.tensor_copy(y_sb[:, i, bass.ds((it + u // UNITS) * P + head * SB_DIM, SB_DIM)],
                                          o[i % 2][:, head * SB_DIM:(head + 1) * SB_DIM]).then_inc(o_read, 1)

            pipeline(dve.Fori, step)


def split_weights(nc, tiles, raw, hi, lo, loaded, hi_done, lo_done):
    N = len(raw)
    every = range(len(tiles))

    def load(sp, ks=every):
        for k in ks:
            until(sp, lo_done, k - N + 1)
            sp.dma_start(raw[k % N][:, 0:D_MODEL], tiles[k]).then_inc(loaded[k % N], 16)

    def high(act, ks=every):
        for k in ks:
            act.wait_ge(loaded[k % N], 16 * (k // N + 1))
            nc.scalar.copy(hi[:, k, :], raw[k % N][:, 0:D_MODEL]).then_inc(hi_done, 1)

    def low(dve, ks=every):
        for k in ks:
            dve.wait_ge(hi_done, k + 1)
            nc.vector.tensor_tensor(lo[:, k, :], raw[k % N][:, 0:D_MODEL], hi[:, k, :].bitcast(F32), ALU.subtract)\
                .then_inc(lo_done, 1)

    return load, high, low


def mlstm_and_output_projection(nc, x, ml_i_bias, ml_f_bias, w_out, post_norm_w, ml_t, proj_n, gates_t, y_sb,
                                neg_m_rows, residual, ring, ring_loaded, ring_tiles):
    with ExitStack() as ctx:
        def sb(name, shape, dt=F32):
            return ctx.enter_context(nc.sbuf_tensor(name, shape, dt))

        def sem(name):
            return ctx.enter_context(nc.semaphore(name))

        def psum(name, shape):
            return ctx.enter_context(nc.psum_tensor(name, shape, F32))

        H, DV = ML_HEADS, ML_DIM + 1
        A, CARRY, FLOOR, KEY = range(4)

        w_raw, qk_slots, gates = ring[0:2], ring[2:4], ring[4:6]
        w_hi = sb("c_w_hi", [P, KT, D_MODEL], F32R)
        w_lo = sb("c_w_lo", [P, KT, D_MODEL], F32R)
        post_w = sb("c_post_w", [P, D_MODEL])
        ident = sb("c_ident", [P, P])
        minus_half = sb("c_minus_half", [P, SB_HEADS + H])
        eps = sb("c_eps", [P, SB_HEADS + H])
        ident_b = sb("c_ident_b", [P, P], BF16)
        hidden = sb("c_hidden", [P, 2, P], BF16)
        sel = sb("c_sel", [H, H, P])
        neg_m = sb("c_neg_m", [H, SEQ])
        cols = sb("c_cols", [P, 4, H, TOK])
        decay = sb("c_decay", [P, H, TOK])
        state = sb("c_state", [P, H, DV + 3])
        vx = [sb(f"c_vx{s}", [P, H, DV + 3]) for s in range(2)]

        scores = psum("c_scores", [P, 2, 2, P])
        k_turned = psum("c_k_turned", [P, 2, P])
        inter = psum("c_inter", [P, 2, 256])
        intra = psum("c_intra", [P, 2, 256])
        update = psum("c_update", [P, 2, 256])
        turned = psum("c_turned", [P, GROUP])
        out = [psum(f"c_out{n}", [P, GROUP]) for n in range(2)]

        w_loaded = [sem(f"c_w_loaded{s}") for s in range(2)]
        w_hi_done = sem("c_w_hi_done")
        w_lo_done = sem("c_w_lo_done")
        post_w_loaded = sem("c_post_w_loaded")
        zeroed = sem("c_zeroed")
        consts_ready = sem("c_consts_ready")
        load_w, split_hi, split_lo = split_weights(nc, [w_out[k * P:(k + 1) * P, :] for k in range(KT)], w_raw,
                                                   w_hi, w_lo, w_loaded, w_hi_done, w_lo_done)

        with ExitStack() as rows_ctx:
            def row(name, shape):
                return rows_ctx.enter_context(nc.sbuf_tensor(name, shape, F32))

            R = H * TOK
            bias = row("g_bias", [R, 2])
            i_row = row("g_i", [R, P])
            f_row = row("g_f", [R, P])
            sp_row = row("g_sp", [R, P])
            neg_b = row("g_neg_b", [R, P])
            a_row = row("g_a", [R, P])
            a_max = row("g_a_max", [R, P])
            m_row = row("g_m", [R, P])
            neg_m_row = row("g_neg_m", [R, P])
            carry_row = row("g_carry", [R, P])
            floor_row = row("g_floor", [R, P])
            key_row = row("g_key", [R, P])
            m_col = row("g_m_col", [R, 2])
            ends = row("g_ends", [1, 2, H, TOK])
            m_before = row("g_m_before", [1, H, TOK])
            neg_m_end = row("g_neg_m_end", [1, H, TOK])
            chunk_decay = row("g_chunk_decay", [1, H, TOK])
            one = row("g_one", [1, P])

            g_i_loaded = sem("g_i_loaded")
            g_f_loaded = sem("g_f_loaded")
            g_dve = sem("g_dve")
            g_act = sem("g_act")
            g_pe = sem("g_pe")
            neg_m_stored = sem("g_neg_m_stored")
            neg_m_loaded = sem("g_neg_m_loaded")

            def flat(t):
                return t[:].rearrange("a h c -> a (h c)")

            block = rows_ctx.enter_context(nc.Block())

            @block.sync
            def _(sp):
                rows = gates_t.rearrange("(g h) (c t) -> g (h c) t", g=2, t=P)
                sp.dma_start(f_row[:], rows[1]).then_inc(g_f_loaded, 16)
                with nc.allow_non_contiguous_dma("eight biases"):
                    for h in range(H):
                        sp.dma_start(bias[h * TOK:(h + 1) * TOK, 1:2], ml_f_bias[0:1, h:h + 1].broadcast_to([TOK, 1]))\
                            .then_inc(g_f_loaded, 16)
                    sp.dma_start(i_row[:], rows[0]).then_inc(g_i_loaded, 16)
                    for h in range(H):
                        sp.dma_start(bias[h * TOK:(h + 1) * TOK, 0:1], ml_i_bias[0:1, h:h + 1].broadcast_to([TOK, 1]))\
                            .then_inc(g_i_loaded, 16)
                sp.dma_start(post_w[:], post_norm_w.broadcast_to([P, D_MODEL])).then_inc(post_w_loaded, 16)
                load_w(sp, range(2))
                sp.wait_ge(g_dve, 13)
                sp.dma_start(neg_m_rows, neg_m_row[:]).then_inc(neg_m_stored, 16)
                sp.wait_ge(neg_m_stored, 16)
                sp.dma_start(neg_m[:], neg_m_rows.rearrange("(h c) t -> h (c t)", h=H)).then_inc(neg_m_loaded, 16)
                sp.wait_ge(neg_m_loaded, 16)
                sp.wait_ge(post_w_loaded, 16)

            @block.gpsimd
            def _(pool):
                for t in (ident, m_before, ident_b, hidden, sel, state):
                    nc.gpsimd.memset(t[:], 0.0).then_inc(zeroed, 1)
                nc.gpsimd.memset(one[:], 1.0).then_inc(consts_ready, 1)
                pool.wait_ge(zeroed, 1)
                nc.gpsimd.affine_select(out=ident[:], in_=ident[:], compare_op=ALU.not_equal, fill=1.0, base=0,
                                        pattern=[[-1, P]], channel_multiplier=1).then_inc(consts_ready, 1)
                pool.wait_ge(zeroed, 6)
                nc.gpsimd.affine_select(out=ident_b[:], in_=ident_b[:], compare_op=ALU.not_equal, fill=1.0, base=0,
                                        pattern=[[-1, P]], channel_multiplier=1).then_inc(consts_ready, 1)
                nc.gpsimd.affine_select(out=hidden[:], in_=hidden[:], compare_op=ALU.is_ge, fill=MASKED, base=0,
                                        pattern=[[0, 2], [1, P]], channel_multiplier=-1).then_inc(consts_ready, 1)
                nc.gpsimd.affine_select(out=sel[:], in_=sel[:], compare_op=ALU.not_equal, fill=1.0, base=0,
                                        pattern=[[-1, H], [0, P]], channel_multiplier=1).then_inc(consts_ready, 1)
                nc.gpsimd.memset(minus_half[:], -0.5).then_inc(consts_ready, 1)
                nc.gpsimd.memset(eps[:], EPS).then_inc(consts_ready, 1)
                for s in range(2):
                    nc.gpsimd.memset(vx[s][:, :, ML_DIM:DV], 1.0).then_inc(consts_ready, 1)

            @block.scalar
            def _(act):
                act.preload_act_table_set("natural_log_exp_and_others")
                act.wait_ge(g_dve, 1)
                nc.scalar.activation(sp_row[:], f_row[:], ACT.Exp).then_inc(g_act, 1)
                act.wait_ge(g_act, 1)
                nc.scalar.activation(sp_row[:], sp_row[:], ACT.Ln, bias=1.0).then_inc(g_act, 1)
                act.wait_ge(g_dve, 11)
                nc.scalar.activation(chunk_decay[:], chunk_decay[:], ACT.Exp).then_inc(g_act, 1)
                act.wait_ge(g_dve, 12)
                nc.scalar.activation(key_row[:], a_row[:], ACT.Exp, bias=m_col[:, 1:2]).then_inc(g_act, 1)
                act.wait_ge(g_dve, 14)
                nc.scalar.activation(carry_row[:], m_row[:], ACT.Exp, bias=m_col[:, 0:1], scale=-1.0).then_inc(g_act, 1)
                act.wait_ge(g_dve, 15)
                nc.scalar.activation(floor_row[:], floor_row[:], ACT.Exp).then_inc(g_act, 1)

            @block.vector
            def _(dve):
                dve.wait_ge(g_f_loaded, 16 * (H + 1))
                nc.vector.tensor_scalar(f_row[:], f_row[:], bias[:, 1:2], -1.0, ALU.add, ALU.mult).then_inc(g_dve, 1)
                dve.wait_ge(g_act, 2)
                nc.vector.scalar_tensor_tensor(out=sp_row[:], in0=sp_row[:], scalar=LN_MAX, in1=f_row[:],
                                               op0=ALU.min, op1=ALU.max).then_inc(g_dve, 1)
                dve.wait_ge(g_dve, 2)
                nc.vector.tensor_tensor_scan(neg_b[:], sp_row[:], sp_row[:], 0.0, ALU.add, ALU.bypass)\
                    .then_inc(g_dve, 1)
                dve.wait_ge(g_i_loaded, 16 * (H + 1))
                dve.wait_ge(g_dve, 3)
                nc.vector.scalar_tensor_tensor(out=a_row[:], in0=i_row[:], scalar=bias[:, 0:1], in1=neg_b[:],
                                               op0=ALU.add, op1=ALU.add).then_inc(g_dve, 1)
                dve.wait_ge(g_dve, 4)
                nc.vector.tensor_tensor_scan(a_max[:], a_row[:], a_row[:], -BIG, ALU.max, ALU.bypass).then_inc(g_dve, 1)
                dve.wait_ge(g_pe, 1)
                nc.vector.tensor_copy(ends[:].rearrange("a q h c -> a (q h c)"), turned[0:1, 0:2 * R]).then_inc(g_dve, 1)
                dve.wait_ge(g_dve, 6)
                dve.wait_ge(zeroed, 2)
                for h in range(H):
                    a = nc.vector.tensor_tensor_scan(m_before[:, h, 1:], ends[:, 1, h, :TOK - 1],
                                                     ends[:, 0, h, :TOK - 1], 0.0, ALU.max, ALU.subtract)
                a.then_inc(g_dve, 1)
                dve.wait_ge(g_dve, 7)
                nc.vector.tensor_tensor(neg_m_end[:], m_before[:], ends[:, 1, :, :], ALU.max).then_inc(g_dve, 1)
                dve.wait_ge(g_dve, 8)
                nc.vector.tensor_scalar_mul(neg_m_end[:], neg_m_end[:], -1.0).then_inc(g_dve, 1)
                dve.wait_ge(g_dve, 9)
                nc.vector.tensor_tensor(chunk_decay[:], m_before[:], neg_m_end[:], ALU.add).then_inc(g_dve, 2)
                dve.wait_ge(g_pe, 2)
                nc.vector.tensor_copy(m_col[:], out[0][0:R, 0:2]).then_inc(g_dve, 1)
                dve.wait_ge(g_dve, 12)
                nc.vector.tensor_scalar(neg_m_row[:], a_max[:], m_col[:, 0:1], -1.0, ALU.max, ALU.mult)\
                    .then_inc(g_dve, 1)
                nc.vector.tensor_scalar(m_row[:], a_max[:], m_col[:, 0:1], None, ALU.max).then_inc(g_dve, 1)
                dve.wait_ge(g_dve, 14)
                nc.vector.tensor_tensor(floor_row[:], neg_b[:], m_row[:], ALU.subtract).then_inc(g_dve, 1)
                dve.wait_ge(g_pe, 3)
                nc.vector.tensor_copy(cols[:, 0:KEY, :, :].rearrange("p q h c -> p (q h c)"), turned[:, 0:KEY * R])\
                    .then_inc(g_dve, 1)
                nc.vector.tensor_scalar_mul(cols[:, KEY, :, :].rearrange("p h c -> p (h c)"),
                                            turned[:, KEY * R:(KEY + 1) * R], ML_SCALE).then_inc(g_dve, 1)
                dve.wait_ge(g_pe, 4)
                nc.vector.tensor_copy(decay[:].rearrange("p h c -> p (h c)"), out[1][:, 0:R]).then_inc(g_dve, 1)

            @block.tensor
            def _(pe):
                pe.wait_ge(consts_ready, 2)
                pe.wait_ge(g_dve, 5)
                pe.transpose(turned[0:1, 0:R], neg_b[:, P - 1:P], ident[0:R, 0:R])
                pe.transpose(turned[0:1, R:2 * R], a_max[:, P - 1:P], ident[0:R, 0:R]).then_inc(g_pe, 1)
                pe.wait_ge(g_dve, 9)
                pe.matmul(out[0][0:R, 0:1], flat(m_before), one[:, 0:1], start=True, stop=True)
                pe.matmul(out[0][0:R, 1:2], flat(neg_m_end), one[:, 0:1], start=True, stop=True).then_inc(g_pe, 1)
                pe.wait_ge(g_act, 6)
                for n, t in enumerate((a_row, carry_row, floor_row, key_row)):
                    mm = pe.transpose(turned[:, n * R:(n + 1) * R], t[:], ident[0:R, 0:R])
                mm.then_inc(g_pe, 1)
                pe.matmul(out[1][:, 0:R], one[:], flat(chunk_decay), start=True, stop=True).then_inc(g_pe, 1)

        qk = [t[:].rearrange("p (j t) -> p j t", t=P) for t in qk_slots]
        x_in = [sb(f"c_x{s}", [P, D_MODEL]) for s in range(2)]
        h_out = [sb(f"c_h{s}", [P, D_MODEL]) for s in range(2)]
        wt = [sb(f"c_wt{s}", [P, 2, P]) for s in range(2)]
        kw = [sb(f"c_kw{s}", [P, 2, P]) for s in range(2)]
        carried = [sb(f"c_carried{s}", [P, 2, DV + 3]) for s in range(2)]
        num = sb("c_num", [P, H, DV + 3])
        den = sb("c_den", [P, 3, H])
        y = [sb(f"c_y{s}", [P, D_MODEL]) for s in range(2)]
        squares = sb("c_squares", [P, D_MODEL])
        ss = sb("c_ss", [P, SB_HEADS + H])
        rstd = sb("c_rstd", [P, SB_HEADS + H])
        post_ss = sb("c_post_ss", [P, 2])
        post_rstd = sb("c_post_rstd", [P, 2])
        junk = sb("c_junk", [P, 2, GROUP])
        yT_hi = [sb(f"c_yT_hi{s}", [P, KT, P], F32R) for s in range(2)]
        yT_lo = [sb(f"c_yT_lo{s}", [P, KT, P], F32R) for s in range(2)]

        def per_slot(name):
            return [sem(f"{name}{s}") for s in range(2)]

        qk_loaded, v_loaded, gates_loaded, x_loaded = map(per_slot, ("c_qk_loaded", "c_v_loaded", "c_gates_loaded",
                                                                      "c_x_loaded"))
        h_stored = per_slot("c_h_stored")
        scores_done = sem("scores_done")
        k_turned_done = sem("k_turned_done")
        weights_done = sem("weights_done")
        p_done = sem("p_done")
        kw_done = sem("kw_done")
        inter_done = sem("inter_done")
        carried_done = sem("carried_done")
        intra_done = sem("intra_done")
        num_done = sem("num_done")
        update_done = sem("update_done")
        state_done = sem("state_done")
        den_done = sem("den_done")
        ml_y_done = sem("ml_y_done")
        squares_done = sem("squares_done")
        ss_done = sem("ss_done")
        mean_done = sem("c_mean_done")
        rstd_done = sem("c_rstd_done")
        scaled_done = sem("scaled_done")
        sb_y_done = sem("sb_y_done")
        ml_gated = sem("ml_gated")
        y_turned = sem("y_turned")
        yT_hi_done = sem("yT_hi_done")
        yT_lo_done = sem("yT_lo_done")
        out_done = sem("c_out_done")
        out_read = sem("c_out_read")
        post_ss_done = sem("post_ss_done")
        post_mean_done = sem("post_mean_done")
        post_rstd_done = sem("post_rstd_done")
        normed_done = sem("normed_done")
        h_done = sem("h_done")

        block = ctx.enter_context(nc.Block())
        NORM_LAG, TURN_LAG, LAG = 1, 2, 3
        FIRST = 2 * LAG

        def steps(fori, step):
            for c in range(FIRST):
                step(c, c % 2)
            with fori(0, (TOK - FIRST) // 2) as n:
                for s in range(2):
                    step(2 * n + (FIRST + s), s)
            for c in range(TOK, TOK + LAG):
                step(c, c % 2)

        def has(c, lag):
            return not isinstance(c, int) or 0 <= c - lag < TOK

        def w_tiles(c, n):
            return range(3 * c + n, min(3 * c + n + 1, KT)) if isinstance(c, int) and c < LAG else ()

        def tile(c):
            return bass.ds(c * P, P) if not isinstance(c, int) else slice(c * P, (c + 1) * P)

        def at(c):
            return bass.ds(c, 1) if not isinstance(c, int) else slice(c, c + 1)

        def loads(d, s, of):
            return of * (d // 2) + of if isinstance(d, int) else (d - s) * (of // 2) + of

        @block.sync
        def _(sp):
            def step(c, s):
                if has(c, 0):
                    until(sp, update_done, 2 * c - 2)
                    src = ml_t[:, tile(c)].rearrange("(j p) t -> p j t", p=P)
                    sp.dma_start(qk[s], src).then_inc(qk_loaded[s], 16)
                    sp.dma_start(vx[s][:, :, 0:ML_DIM],
                                 proj_n[tile(c), 2 * GROUP:3 * GROUP].rearrange("p (h d) -> p h d", h=H))\
                        .then_inc(v_loaded[s], 16)
                    until(sp, sb_y_done, c - 1)
                    until(sp, ml_gated, c - 1)
                    sp.dma_start(gates[s][:, 0:GROUP], proj_n[tile(c), GROUP:2 * GROUP]).then_inc(gates_loaded[s], 16)
                    sp.dma_start(gates[s][:, GROUP:], proj_n[tile(c), 3 * GROUP:5 * GROUP])\
                        .then_inc(gates_loaded[s], 16)
                if isinstance(c, int) and c in (1, 2):
                    load_w(sp, (range(2, 6), range(6, KT))[c - 1])
                if has(c, LAG):
                    d, sd = c - LAG, (s - LAG) % 2
                    until(sp, h_done, d - 1)
                    sp.dma_start(x_in[sd][:], x[tile(d), :]).then_inc(x_loaded[sd], 16)
                    if has(c, LAG + 1):
                        store(d - 1, 1 - sd)

                if isinstance(c, int) and c == TOK:
                    sp.wait_ge(update_done, 2 * TOK)
                    prefetch(range(4))
                if isinstance(c, int) and c == TOK + 1:
                    sp.wait_ge(sb_y_done, TOK)
                    sp.wait_ge(ml_gated, TOK)
                    prefetch(range(4, len(ring)))

            def prefetch(slots):
                for n in slots:
                    sp.dma_start(ring[n][:, 0:D_MODEL], ring_tiles[n]).then_inc(ring_loaded[n], 16)

            def store(d, s):
                until(sp, h_done, d + 1)
                sp.dma_start(residual[tile(d), :], h_out[s][:]).then_inc(h_stored[s], 16)

            steps(sp.Fori, step)
            store(TOK - 1, 1)
            for s in range(2):
                sp.wait_ge(h_stored[s], 16 * (TOK // 2))

        @block.tensor
        def _(pe):
            def score(c, s, p):
                u = 2 * c + p
                q, k = qk[s][:, 2 * p:2 * p + 2, :], qk[s][:, H + 2 * p:H + 2 * p + 2, :]
                if p == 0:
                    pe.wait_ge(qk_loaded[s], loads(c, s, 16))
                until(pe, p_done, u)
                for i in range(2):
                    pe.matmul(scores[:, 0, i, :], k[:, i, :], q[:, i, :], start=True, stop=True)
                pe.matmul(scores[:, 1, :, :], ident_b[:], hidden[:], start=True, stop=False)
                for i in range(2):
                    mm = pe.matmul(scores[:, 1, i, :], sel[:, 2 * p + i, :], neg_m[:, tile(c)],
                                   start=False, stop=(i == 1))
                mm.then_inc(scores_done, 1)
                until(pe, kw_done, u)
                for i in range(2):
                    mm = pe.transpose(k_turned[:, i, :], k[:, i, :], ident[:])
                mm.then_inc(k_turned_done, 1)

            def combine(c, s, p):
                u = 2 * c + p
                if p == 0:
                    pe.wait_ge(v_loaded[s], loads(c, s, 16))
                until(pe, state_done, u - 1)
                until(pe, carried_done, u)
                for i in range(2):
                    mm = pe.matmul(inter[:, i, 0:DV], qk[s][:, 2 * p + i, :], state[:, 2 * p + i, 0:DV],
                                   start=True, stop=True)
                mm.then_inc(inter_done, 1)
                until(pe, p_done, u + 1)
                until(pe, num_done, u)
                for i in range(2):
                    mm = pe.matmul(intra[:, i, 0:DV], wt[p][:, i, :], vx[s][:, 2 * p + i, 0:DV], start=True, stop=True)
                mm.then_inc(intra_done, 1)
                until(pe, kw_done, u + 1)
                until(pe, state_done, u)
                for i in range(2):
                    mm = pe.matmul(update[:, i, 0:DV], kw[p][:, i, :], vx[s][:, 2 * p + i, 0:DV],
                                   start=True, stop=True)
                mm.then_inc(update_done, 1)

            def turn(t, s, half):
                until(pe, sb_y_done, t + 1)
                until(pe, ml_gated, t + 1)
                until(pe, yT_lo_done, 2 * t + half)
                for k in range(4):
                    mm = pe.transpose(turned[:, k * P:(k + 1) * P],
                                      y[s][:, (4 * half + k) * P:(4 * half + k + 1) * P], ident[:])
                mm.then_inc(y_turned, 1)

            def project(d, s, n):
                if isinstance(d, int) and (d, n) == (0, 0):
                    pe.wait_ge(w_lo_done, KT)
                until(pe, yT_lo_done, 2 * d + 2)
                until(pe, out_read, 2 * d - 1 + n)
                for k in range(KT):
                    for j, (yT, w) in enumerate(((yT_lo, w_hi), (yT_hi, w_lo), (yT_hi, w_hi))):
                        mm = pe.matmul(out[n][:], yT[s][:, k, :], w[:, k, n * GROUP:(n + 1) * GROUP],
                                       start=(k == 0 and j == 0), stop=(k == KT - 1 and j == 2))
                mm.then_inc(out_done, 1)

            def step(c, s):
                sd, st = (s - LAG) % 2, (s - TURN_LAG) % 2
                if has(c, 0):
                    score(c, s, 0)
                if has(c, TURN_LAG):
                    turn(c - TURN_LAG, st, 0)
                if has(c, LAG):
                    project(c - LAG, sd, 0)
                if has(c, 0):
                    score(c, s, 1)
                    combine(c, s, 0)
                if has(c, TURN_LAG):
                    turn(c - TURN_LAG, st, 1)
                if has(c, LAG):
                    project(c - LAG, sd, 1)
                if has(c, 0):
                    combine(c, s, 1)

            steps(pe.Fori, step)

        @block.scalar
        def _(act):
            act.preload_act_table_set("natural_log_exp_and_others")

            def weigh(c, p):
                u = 2 * c + p
                until(act, scores_done, u + 1)
                until(act, intra_done, u - 1)
                for i in range(2):
                    a = nc.scalar.activation(wt[p][:, i, :], scores[:, 1, i, :], ACT.Exp,
                                             bias=cols[:, A, 2 * p + i, at(c)])
                a.then_inc(weights_done, 1)
                until(act, k_turned_done, u + 1)
                until(act, update_done, u - 1)
                for i in range(2):
                    a = nc.scalar.activation(kw[p][:, i, :], k_turned[:, i, :], ACT.Copy,
                                             scale=cols[:, KEY, 2 * p + i, at(c)])
                a.then_inc(kw_done, 1)

            def carry(c, p):
                u = 2 * c + p
                until(act, inter_done, u + 1)
                until(act, num_done, u - 1)
                for i in range(2):
                    a = nc.scalar.activation(carried[p][:, i, 0:DV], inter[:, i, 0:DV], ACT.Copy,
                                             scale=cols[:, CARRY, 2 * p + i, at(c)])
                a.then_inc(carried_done, 1)

            def high(t, s, half):
                until(act, y_turned, 2 * t + half + 1)
                until(act, out_done, 2 * t - 2)
                nc.scalar.copy(yT_hi[s][:, 4 * half:4 * half + 4, :], turned[:].rearrange("p (k t) -> p k t", k=4))\
                    .then_inc(yT_hi_done, 1)

            def square(b):
                until(act, ss_done, 2 * b)
                nc.scalar.activation(squares[:, 0:SB_WIDTH], y_sb[:, at(b), :].rearrange("p a n -> p (a n)"),
                                     ACT.Square, scale=SB_DIM ** -0.5).then_inc(squares_done, 1)
                until(act, ml_y_done, b + 1)
                nc.scalar.activation(squares[:, SB_WIDTH:], num[:, :, 0:ML_DIM], ACT.Square, scale=ML_DIM ** -0.5)\
                    .then_inc(squares_done, 1)

            def evacuate(d, s, n):
                until(act, out_done, 2 * d + n + 1)
                until(act, post_mean_done, 2 * d)
                nc.scalar.activation(junk[:, n, :], out[n][:], ACT.Square, scale=D_MODEL ** -0.5,
                                     accum_out=post_ss[:, n:n + 1]).then_inc(post_ss_done, 1)
                until(act, h_stored[s], 16 * (d // 2) if isinstance(d, int) else (d - s) * 8)
                nc.scalar.copy(h_out[s][:, n * GROUP:(n + 1) * GROUP], out[n][:]).then_inc(out_read, 1)

            def step(c, s):
                sd, st = (s - LAG) % 2, (s - TURN_LAG) % 2
                if has(c, 0):
                    weigh(c, 0)
                split_hi(act, w_tiles(c, 0))
                if has(c, TURN_LAG):
                    high(c - TURN_LAG, st, 0)
                if has(c, NORM_LAG):
                    square(c - NORM_LAG)
                if has(c, LAG):
                    evacuate(c - LAG, sd, 0)
                if has(c, 0):
                    weigh(c, 1)
                    split_hi(act, w_tiles(c, 1))
                    carry(c, 0)
                split_hi(act, w_tiles(c, 2))
                if has(c, TURN_LAG):
                    high(c - TURN_LAG, st, 1)
                if has(c, LAG):
                    evacuate(c - LAG, sd, 1)
                if has(c, 0):
                    carry(c, 1)

            steps(act.Fori, step)

        @block.gpsimd
        def _(pool):
            def head_norms(b, s):
                until(pool, ss_done, 2 * b + 2)
                until(pool, ml_gated, b)
                nc.gpsimd.tensor_tensor(ss[:], ss[:], eps[:], ALU.add).then_inc(mean_done, 1)
                until(pool, mean_done, b + 1)
                nc.gpsimd.tensor_tensor(rstd[:], ss[:], minus_half[:], ALU.pow).then_inc(rstd_done, 1)
                until(pool, scaled_done, b + 1)
                nc.gpsimd.tensor_tensor(y[s][:, 0:SB_WIDTH], y[s][:, 0:SB_WIDTH], gates[s][:, 0:GROUP], ALU.mult)\
                    .then_inc(sb_y_done, 1)

            def post_norm(d):
                until(pool, post_ss_done, 2 * d + 2)
                until(pool, normed_done, d)
                nc.gpsimd.tensor_tensor(post_rstd[:, 0:1], post_ss[:, 0:1], post_ss[:, 1:2], ALU.add)\
                    .then_inc(post_mean_done, 1)
                until(pool, post_mean_done, 2 * d + 1)
                nc.gpsimd.tensor_tensor(post_rstd[:, 0:1], post_rstd[:, 0:1], eps[:, 0:1], ALU.add)\
                    .then_inc(post_mean_done, 1)
                until(pool, post_mean_done, 2 * d + 2)
                nc.gpsimd.tensor_tensor(post_rstd[:, 1:2], post_rstd[:, 0:1], minus_half[:, 0:1], ALU.pow)\
                    .then_inc(post_rstd_done, 1)

            def add_residual(d, s):
                until(pool, normed_done, d + 1)
                pool.wait_ge(x_loaded[s], loads(d, s, 16))
                nc.gpsimd.tensor_tensor(h_out[s][:], h_out[s][:], x_in[s][:], ALU.add).then_inc(h_done, 1)

            def step(c, s):
                if has(c, NORM_LAG):
                    head_norms(c - NORM_LAG, (s - NORM_LAG) % 2)
                if has(c, LAG):
                    post_norm(c - LAG)
                    add_residual(c - LAG, (s - LAG) % 2)

            steps(pool.Fori, step)

        @block.vector
        def _(dve):
            def weights_times_scores(c, p):
                until(dve, weights_done, 2 * c + p + 1)
                nc.vector.scalar_tensor_tensor(out=wt[p][:], in0=scores[:, 0, :, :], scalar=ML_SCALE, in1=wt[p][:],
                                               op0=ALU.mult, op1=ALU.mult).then_inc(p_done, 1)

            def low(t, s, half):
                until(dve, yT_hi_done, 2 * t + half + 1)
                nc.vector.tensor_tensor(yT_lo[s][:, 4 * half:4 * half + 4, :],
                                        turned[:].rearrange("p (k t) -> p k t", k=4),
                                        yT_hi[s][:, 4 * half:4 * half + 4, :].bitcast(F32), ALU.subtract)\
                    .then_inc(yT_lo_done, 1)

            def mean_squares(b):
                for n, (first, heads, width) in enumerate(((0, SB_HEADS, SB_DIM), (SB_WIDTH, H, ML_DIM))):
                    until(dve, squares_done, 2 * b + n + 1)
                    if n == 0:
                        until(dve, rstd_done, b)
                    nc.vector.tensor_reduce(ss[:, (0, SB_HEADS)[n]:(SB_HEADS, SB_HEADS + H)[n]],
                                            squares[:, first:first + heads * width]
                                            .rearrange("p (h d) -> p h d", h=heads), AX.X, ALU.add)\
                        .then_inc(ss_done, 1)

            def norm_heads(b, s):
                until(dve, rstd_done, b + 1)
                until(dve, y_turned, 2 * b - 2)
                nc.vector.tensor_tensor(y[s][:, 0:SB_WIDTH].rearrange("p (h d) -> p h d", h=SB_HEADS),
                                        y_sb[:, at(b), :].rearrange("p a (h d) -> p (a h) d", h=SB_HEADS),
                                        rstd[:, 0:SB_HEADS].unsqueeze(2).broadcast_to([P, SB_HEADS, SB_DIM]),
                                        ALU.mult).then_inc(scaled_done, 1)
                for h in range(H):
                    i = nc.vector.scalar_tensor_tensor(
                        out=y[s][:, SB_WIDTH + h * ML_DIM:SB_WIDTH + (h + 1) * ML_DIM], in0=num[:, h, 0:ML_DIM],
                        scalar=rstd[:, SB_HEADS + h:SB_HEADS + h + 1],
                        in1=gates[s][:, 2 * GROUP + h * ML_DIM:2 * GROUP + (h + 1) * ML_DIM],
                        op0=ALU.mult, op1=ALU.mult)
                i.then_inc(ml_gated, 1)

            def numerator(c, p):
                u = 2 * c + p
                until(dve, carried_done, u + 1)
                until(dve, intra_done, u + 1)
                until(dve, ml_gated, c)
                nc.vector.tensor_tensor(num[:, 2 * p:2 * p + 2, 0:DV], carried[p][:, :, 0:DV], intra[:, :, 0:DV],
                                        ALU.add).then_inc(num_done, 1)
                until(dve, update_done, u + 1)
                for i in range(2):
                    h = 2 * p + i
                    a = nc.vector.scalar_tensor_tensor(out=state[:, h, 0:DV], in0=state[:, h, 0:DV],
                                                       scalar=decay[:, h, at(c)], in1=update[:, i, 0:DV],
                                                       op0=ALU.mult, op1=ALU.add)
                a.then_inc(state_done, 1)

            def divide(c, s):
                until(dve, num_done, 2 * c + 2)
                dens = num[:, :, ML_DIM]
                nc.vector.scalar_tensor_tensor(out=den[:, 0, :], in0=dens, scalar=-1.0, in1=dens,
                                               op0=ALU.mult, op1=ALU.max).then_inc(den_done, 1)
                until(dve, den_done, 3 * c + 1)
                nc.vector.tensor_tensor(den[:, 1, :], den[:, 0, :],
                                        cols[:, FLOOR, :, at(c)].rearrange("p h a -> p (h a)"), ALU.max)\
                    .then_inc(den_done, 1)
                until(dve, den_done, 3 * c + 2)
                nc.vector.reciprocal(den[:, 2, :], den[:, 1, :]).then_inc(den_done, 1)
                until(dve, den_done, 3 * c + 3)
                dve.wait_ge(gates_loaded[s], loads(c, s, 32))
                for h in range(H):
                    i = nc.vector.scalar_tensor_tensor(
                        out=num[:, h, 0:ML_DIM], in0=num[:, h, 0:ML_DIM], scalar=den[:, 2, h:h + 1],
                        in1=gates[s][:, GROUP + h * ML_DIM:GROUP + (h + 1) * ML_DIM], op0=ALU.mult, op1=ALU.mult)
                i.then_inc(ml_y_done, 1)

            def post(d, s):
                until(dve, post_rstd_done, d + 1)
                until(dve, out_read, 2 * d + 2)
                nc.vector.scalar_tensor_tensor(out=h_out[s][:], in0=h_out[s][:], scalar=post_rstd[:, 1:2],
                                               in1=post_w[:], op0=ALU.mult, op1=ALU.mult).then_inc(normed_done, 1)

            def step(c, s):
                st = (s - TURN_LAG) % 2
                if has(c, 0):
                    weights_times_scores(c, 0)
                split_lo(dve, w_tiles(c, 0))
                if has(c, TURN_LAG):
                    low(c - TURN_LAG, st, 0)
                if has(c, NORM_LAG):
                    mean_squares(c - NORM_LAG)
                if has(c, 0):
                    weights_times_scores(c, 1)
                split_lo(dve, w_tiles(c, 1))
                if has(c, NORM_LAG):
                    norm_heads(c - NORM_LAG, (s - NORM_LAG) % 2)
                if has(c, 0):
                    numerator(c, 0)
                split_lo(dve, w_tiles(c, 2))
                if has(c, TURN_LAG):
                    low(c - TURN_LAG, st, 1)
                if has(c, 0):
                    numerator(c, 1)
                    divide(c, s)
                if has(c, LAG):
                    post(c - LAG, (s - LAG) % 2)

            steps(dve.Fori, step)


def layer_embedding(nc, p, ple_b_gate, residual, result, ring, ring_loaded, tiles):
    with ExitStack() as ctx:
        def sb(name, shape, dt=F32):
            return ctx.enter_context(nc.sbuf_tensor(name, shape, dt))

        def sem(name):
            return ctx.enter_context(nc.semaphore(name))

        def psum(name, shape):
            return ctx.enter_context(nc.psum_tensor(name, shape, F32))

        PT = PLE // P
        LOADS = 4
        w_hi = sb("d_w_hi", [P, KT + PT, D_MODEL], F32R)
        w_lo = sb("d_w_lo", [P, KT + PT, D_MODEL], F32R)
        bias = sb("d_bias", [P, D_MODEL])
        ident = sb("d_ident", [P, P])
        h_in = [sb(f"d_h{q}", [P, D_MODEL]) for q in range(LOADS)]
        p_in = [sb(f"d_p{q}", [P, PLE]) for q in range(LOADS)]
        hT_hi = [sb(f"d_hT_hi{s}", [P, KT + PT, P], F32R) for s in range(2)]
        hT_lo = [sb(f"d_hT_lo{s}", [P, KT + PT, P], F32R) for s in range(2)]
        gate = [sb(f"d_gate{s}", [P, D_MODEL]) for s in range(2)]
        turned = [psum(f"d_turned{n}", [P, GROUP]) for n in range(3)]
        product = [psum(f"d_product{n}", [P, GROUP]) for n in range(4)]

        w_hi_done = sem("d_w_hi_done")
        w_lo_done = sem("d_w_lo_done")
        bias_loaded = sem("d_bias_loaded")
        zeroed = sem("d_zeroed")
        ident_ready = sem("d_ident_ready")
        h_loaded = [sem(f"d_h_loaded{q}") for q in range(LOADS)]
        p_loaded = [sem(f"d_p_loaded{q}") for q in range(LOADS)]
        stored = [sem(f"d_stored{s}") for s in range(2)]
        turned_done = sem("d_turned_done")
        hi_done = sem("d_hi_done")
        lo_done = sem("d_lo_done")
        product_done = sem("product_done")
        biased = sem("biased")
        sigmoid_done = sem("sigmoid_done")
        gated = sem("gated")
        sum_done = sem("sum_done")
        load_w, split_hi, split_lo = split_weights(nc, tiles, ring, w_hi, w_lo, ring_loaded, w_hi_done, w_lo_done)
        PIECES = ((0, 4), (4, 4), (KT, PT))

        def tile_steps(fori, step):
            step(0, 0)
            with fori(0, TOK // LOADS - 1) as n:
                for j in range(1, LOADS + 1):
                    step(n, j)
            for j in range(1, LOADS):
                step(TOK // LOADS - 1, j)

        def is_last(n, j):
            return isinstance(n, int) and LOADS * n + j == TOK - 1

        block = ctx.enter_context(nc.Block())

        @block.gpsimd
        def _(pool):
            nc.gpsimd.memset(ident[:], 0.0).then_inc(zeroed, 1)
            pool.wait_ge(zeroed, 1)
            nc.gpsimd.affine_select(out=ident[:], in_=ident[:], compare_op=ALU.not_equal, fill=1.0, base=0,
                                    pattern=[[-1, P]], channel_multiplier=1).then_inc(ident_ready, 1)

            def load(n, q):
                rows = bass.ds((LOADS * n + q) * P, P)
                pool.dma_start(h_in[q][:], residual[rows, :]).then_inc(h_loaded[q], 16)
                pool.dma_start(p_in[q][:], p[rows, :]).then_inc(p_loaded[q], 16)

            for q in range(LOADS):
                load(0, q)
            with pool.Fori(1, TOK // LOADS) as n:
                for q in range(LOADS):
                    pool.wait_ge(sum_done, LOADS * n + (q + 1 - LOADS))
                    load(n, q)

        @block.sync
        def _(sp):
            sp.dma_start(bias[:], ple_b_gate.broadcast_to([P, D_MODEL])).then_inc(bias_loaded, 16)
            load_w(sp, range(len(ring), len(tiles)))
            with sp.Fori(0, TOK // 2) as n:
                for s in range(2):
                    sp.wait_ge(sum_done, 2 * n + (s + 1))
                    sp.dma_start(result[bass.ds((2 * n + s) * P, P), :], gate[s][:]).then_inc(stored[s], 16)
            for s in range(2):
                sp.wait_ge(stored[s], 16 * (TOK // 2))

        @block.tensor
        def _(pe):
            def turn(n, j):
                t, q = LOADS * n + j, j % LOADS
                pe.wait_ge(h_loaded[q], 16 * (n + (j // LOADS + 1)))
                pe.wait_ge(p_loaded[q], 16 * (n + (j // LOADS + 1)))
                for i, (k0, count) in enumerate(PIECES):
                    src = p_in[q] if k0 == KT else h_in[q]
                    until(pe, lo_done, 3 * t + (i - 2))
                    for k in range(count):
                        at = (k0 % KT + k) * P
                        mm = pe.transpose(turned[i][:, k * P:(k + 1) * P], src[:, at:at + P], ident[:])
                    mm.then_inc(turned_done, 1)

            def multiply(n, j, first):
                t, s = LOADS * n + j, j % 2
                until(pe, lo_done, 3 * t + 3)
                for b in range(4):
                    if b < 2:
                        until(pe, biased, 2 * t + (b - 1))
                    else:
                        until(pe, gated, 2 * t + (b - 3))
                    half = slice(b % 2 * GROUP, (b % 2 + 1) * GROUP)
                    ks = range(KT) if b < 2 else range(KT, KT + PT)
                    for k in ks:
                        if first:
                            pe.wait_ge(w_lo_done, k + 1)
                        for i, (a, w) in enumerate(((hT_lo, w_hi), (hT_hi, w_lo), (hT_hi, w_hi))):
                            mm = pe.matmul(product[b][:], a[s][:, k, :], w[:, k, half],
                                           start=(k == ks[0] and i == 0), stop=(k == ks[-1] and i == 2))
                    mm.then_inc(product_done, 1)
                    if b == 0 and not is_last(n, j):
                        turn(n, j + 1)

            pe.wait_ge(ident_ready, 1)
            turn(0, 0)
            tile_steps(pe.Fori, lambda n, j: multiply(n, j, isinstance(n, int) and n == 0 and j == 0))

        @block.scalar
        def _(act):
            act.preload_act_table_set("sigmoid_and_others")

            def high(n, j):
                t, s = LOADS * n + j, j % 2
                for i, (k0, count) in enumerate(PIECES):
                    act.wait_ge(turned_done, 3 * t + (i + 1))
                    nc.scalar.copy(hT_hi[s][:, k0:k0 + count, :],
                                   turned[i][:, 0:count * P].rearrange("p (k t) -> p k t", t=P)).then_inc(hi_done, 1)

            def step(n, j):
                t, s = LOADS * n + j, j % 2
                if not is_last(n, j):
                    high(n, j + 1)
                for b in range(2):
                    half = slice(b * GROUP, (b + 1) * GROUP)
                    act.wait_ge(biased, 2 * t + (b + 1))
                    nc.scalar.activation(gate[s][:, half], gate[s][:, half], ACT.Sigmoid).then_inc(sigmoid_done, 1)

            high(0, 0)
            split_hi(act)
            tile_steps(act.Fori, step)

        @block.vector
        def _(dve):
            def low(n, j):
                t, s = LOADS * n + j, j % 2
                for i, (k0, count) in enumerate(PIECES):
                    dve.wait_ge(hi_done, 3 * t + (i + 1))
                    nc.vector.tensor_tensor(hT_lo[s][:, k0:k0 + count, :],
                                            turned[i][:, 0:count * P].rearrange("p (k t) -> p k t", t=P),
                                            hT_hi[s][:, k0:k0 + count, :].bitcast(F32), ALU.subtract)\
                        .then_inc(lo_done, 1)

            def step(n, j):
                t, s = LOADS * n + j, j % 2
                until(dve, stored[s], 16 * (LOADS // 2 * n + j // 2))
                for b in range(2):
                    half = slice(b * GROUP, (b + 1) * GROUP)
                    dve.wait_ge(product_done, 4 * t + (b + 1))
                    nc.vector.tensor_tensor(gate[s][:, half], product[b][:], bias[:, half], ALU.add)\
                        .then_inc(biased, 1)
                    if b == 0 and not is_last(n, j):
                        low(n, j + 1)
                for b in range(2):
                    half = slice(b * GROUP, (b + 1) * GROUP)
                    dve.wait_ge(sigmoid_done, 2 * t + (b + 1))
                    dve.wait_ge(product_done, 4 * t + (b + 3))
                    nc.vector.tensor_tensor(gate[s][:, half], gate[s][:, half], product[2 + b][:], ALU.mult)\
                        .then_inc(gated, 1)
                dve.wait_ge(gated, 2 * t + 2)
                nc.vector.tensor_tensor(gate[s][:], gate[s][:], h_in[j % LOADS][:], ALU.add).then_inc(sum_done, 1)

            low(0, 0)
            split_lo(dve)
            dve.wait_ge(bias_loaded, 16)
            tile_steps(dve.Fori, step)


def hybrid_block(nc, x, p, pre_norm_w, w_in, ml_conv_w, ml_conv_b, ml_i_bias, ml_f_bias, sb_norm_w, ml_norm_w,
                 w_out, post_norm_w, ple_w_up, ple_w_gate, ple_b_gate, out):
    def scratch(name, shape):
        return nc.dram_tensor(name, shape, F32, kind="Internal").ap()

    qk_hi = scratch("qk_hi", [2 * SB_WIDTH, SEQ])
    qk_lo = scratch("qk_lo", [2 * SB_WIDTH, SEQ])
    ml_t = scratch("ml_t", [2 * ML_WIDTH, SEQ])
    proj_n = scratch("proj_n", [SEQ, 5 * GROUP])
    gates_t = scratch("gates_t", [GATES, SEQ])
    neg_m_rows = scratch("neg_m_rows", [ML_HEADS * TOK, P])
    residual = scratch("residual", [SEQ, D_MODEL])
    input_projection(nc, x[0], pre_norm_w, w_in[0], ml_conv_w[0], ml_conv_b, sb_norm_w, ml_norm_w,
                     qk_hi, qk_lo, ml_t, proj_n, gates_t)
    with ExitStack() as ctx:
        ring = [ctx.enter_context(nc.sbuf_tensor(f"ring{n}", [P, D_MODEL if n < 4 else 3 * GROUP], F32))
                for n in range(6)]
        ring_loaded = [ctx.enter_context(nc.semaphore(f"ring_loaded{n}")) for n in range(6)]
        ple_tiles = [w[k * P:(k + 1) * P, :] for w in (ple_w_gate[0], ple_w_up[0]) for k in range(w.shape[0] // P)]
        with nc.sbuf_tensor("y_sb", [P, TOK, SB_WIDTH], F32) as y_sb:
            stick_breaking_attention(nc, qk_hi, qk_lo, proj_n, y_sb)
            mlstm_and_output_projection(nc, x[0], ml_i_bias, ml_f_bias, w_out[0], post_norm_w, ml_t, proj_n, gates_t,
                                        y_sb, neg_m_rows, residual, ring, ring_loaded, ple_tiles)
        layer_embedding(nc, p[0, 0], ple_b_gate, residual, out[0], ring, ring_loaded, ple_tiles)


_INS = ['x', 'p', 'pre_norm_w', 'w_in', 'ml_conv_w', 'ml_conv_b', 'ml_i_bias', 'ml_f_bias', 'sb_norm_w', 'ml_norm_w',
        'w_out', 'post_norm_w', 'ple_w_up', 'ple_w_gate', 'ple_b_gate']


def kernel(**inputs):
    import numpy as np
    import concourse.bacc as bacc
    from concourse.bass_utils import run_bass_kernel_spmd

    nc = bacc.Bacc("TRN2", target_bir_lowering=False, num_devices=1)
    arrays, args = {}, []
    for name in _INS:
        a = np.ascontiguousarray(inputs[name])
        arrays[f"in_{name}"] = a
        args.append(nc.dram_tensor(f"in_{name}", a.shape, mybir.dt.from_np(a.dtype), kind="ExternalInput").ap())
    out = nc.dram_tensor("out", (1, SEQ, D_MODEL), F32, kind="ExternalOutput").ap()
    hybrid_block(nc, *args, out)
    return run_bass_kernel_spmd(nc, [arrays], core_ids=[0]).results[0]["out"]
```
